# Optimizing a Trainium2 kernel written in Bass

```python
import math
import jax, jax.numpy as jnp
from jax import lax
import numpy as np

D_MODEL = 1024
BATCH = 1
SEQ = 128
DEPTH = 2
DEC_BATCH = 1
DEC_SEQ = 256
PAST_LEN = 128

GRID_W = 64
N_EVEN = (DEPTH + 1) // 2
N_ODD = DEPTH // 2
LRU_WIDTH = D_MODEL // 2
LRU_HEADS = 8
LRU_BLOCK = LRU_WIDTH // LRU_HEADS
LRU_C = 8.0
LRU_CONV = 4
SC_WIDTH = D_MODEL // 2
SC_CONV = 3
IN_WIDTH = 2 * LRU_WIDTH + 3 * SC_WIDTH
N_HEADS = 16
HEAD_DIM = D_MODEL // N_HEADS
WIN_R = 8
WIN_C = 16
Q_BLOCK = 128
D_FF = 2816
N_EXPERTS = 8
TOP_K = 2
EPS = 1e-6
NEG_INF = -1e30

kernel_name = "hybrid_diffusion_rglru_shortconv_natten_moe_step"

def rmsnorm(x, g):
    xf = x.astype(jnp.float32)
    y = xf * lax.rsqrt(jnp.mean(xf * xf, axis=-1, keepdims=True) + EPS)
    return (y * g.astype(jnp.float32)).astype(x.dtype)

def adaln(cond, w_mod_l, b_mod_l):
    mod = jax.nn.silu(cond) @ w_mod_l + b_mod_l
    return jnp.split(mod[:, None, :], 6, axis=-1)

def modulate(x, shift, scale):
    return x * (1 + scale) + shift

def depthwise_conv(x, w, b, pad_left):
    k_w = w.shape[0]
    seq = x.shape[1]
    xp = jnp.pad(x, ((0, 0), (pad_left, k_w - 1 - pad_left), (0, 0)))
    y = b + xp[:, 0:seq] * w[0]
    for k in range(1, k_w):
        y = y + xp[:, k:k + seq] * w[k]
    return y

def block_diag(x, w, b):
    bsz, seq = x.shape[0], x.shape[1]
    xh = x.reshape(bsz, seq, LRU_HEADS, LRU_BLOCK)
    return jnp.einsum('blhi,hij->blhj', xh, w).reshape(bsz, seq, LRU_WIDTH) + b

def linear_scan(a, b, h0, reverse):
    edge = -1 if reverse else 0
    b = b.at[:, edge].add(a[:, edge] * h0)

    def combine(left, right):
        a_l, b_l = left
        a_r, b_r = right
        return a_l * a_r, a_r * b_l + b_r

    _, h = lax.associative_scan(combine, (a, b), axis=1, reverse=reverse)
    return h

def rg_lru(xc, wa, ba, wx, bx, lam, h0, reverse):
    xf = xc.astype(jnp.float32)
    r = jax.nn.sigmoid(block_diag(xc, wa, ba)).astype(jnp.float32)
    i = jax.nn.sigmoid(block_diag(xc, wx, bx)).astype(jnp.float32)
    log_a = -LRU_C * r * jax.nn.softplus(-lam.astype(jnp.float32))
    a = jnp.exp(log_a)
    b = jnp.sqrt(-jnp.expm1(2.0 * log_a)) * (i * xf)
    return linear_scan(a, b, h0.astype(jnp.float32), reverse)

def recurrent_conv_mixer(hn, p, i, h0):
    r_w, s_w = LRU_WIDTH, SC_WIDTH
    proj = hn @ p['w_in'][i]
    x_lru, g_lru, b_sc, c_sc, v_sc = jnp.split(proj, [r_w, 2 * r_w, 2 * r_w + s_w, 2 * r_w + 2 * s_w], axis=-1)
    xc = depthwise_conv(x_lru, p['lru_conv_w'][i], p['lru_conv_b'][i], LRU_CONV // 2)
    h_f = rg_lru(xc, p['lru_wa'][i, 0], p['lru_ba'][i, 0], p['lru_wx'][i, 0], p['lru_bx'][i, 0],
                 p['lru_lam'][i, 0], h0[:, 0], False)
    h_b = rg_lru(xc, p['lru_wa'][i, 1], p['lru_ba'][i, 1], p['lru_wx'][i, 1], p['lru_bx'][i, 1],
                 p['lru_lam'][i, 1], h0[:, 1], True)
    y_lru = (h_f + h_b).astype(hn.dtype) * jax.nn.gelu(g_lru)
    y_sc = b_sc * depthwise_conv(c_sc * v_sc, p['sc_conv_w'][i], p['sc_conv_b'][i], SC_CONV // 2)
    out = jnp.concatenate([y_lru, y_sc], axis=-1) @ p['w_out'][i]
    return out, h_f, h_b

def qkv_heads(hn, w_qkv_l):
    bsz, seq = hn.shape[0], hn.shape[1]
    qkv = (hn @ w_qkv_l).reshape(bsz, seq, 3, N_HEADS, HEAD_DIM).transpose(2, 0, 3, 1, 4)
    return qkv[0], qkv[1], qkv[2]

def merge_heads(o):
    bsz, _, seq, _ = o.shape
    return o.transpose(0, 2, 1, 3).reshape(bsz, seq, D_MODEL)

def context_attention(q, k, v):
    bsz, heads, seq, dh = q.shape
    n_blk = seq // Q_BLOCK
    qb = jnp.moveaxis((q * (dh ** -0.5)).reshape(bsz, heads, n_blk, Q_BLOCK, dh), 2, 0)

    def one_block(q_blk):
        s = jnp.einsum('bhqd,bhkd->bhqk', q_blk, k).astype(jnp.float32)
        pr = jax.nn.softmax(s, axis=-1).astype(v.dtype)
        return jnp.einsum('bhqk,bhkd->bhqd', pr, v)

    o = lax.map(one_block, qb)
    return jnp.moveaxis(o, 0, 2).reshape(bsz, heads, seq, dh)

def neighbourhood_attention(q, k, v, k_ctx, v_ctx, rpb_l):
    bsz, heads, n_tok, dh = q.shape
    rows = n_tok // GRID_W
    kr = min(WIN_R, rows)
    kc = WIN_C
    r_idx = jnp.arange(rows)
    col = jnp.arange(GRID_W)
    row_start = jnp.clip(r_idx - kr // 2, 0, rows - kr)
    key_rows = row_start[:, None] + jnp.arange(kr)
    col_start = jnp.clip(col - kc // 2, 0, GRID_W - kc)
    col_mask = (col[None, :] >= col_start[:, None]) & (col[None, :] < col_start[:, None] + kc)
    dr = key_rows - r_idx[:, None] + (WIN_R - 1)
    dc = jnp.clip(col[None, :] - col[:, None], -(kc - 1), kc - 1) + (WIN_C - 1)
    bias = rpb_l[:, dr[:, None, :, None], dc[None, :, None, :]]
    qg = (q * (dh ** -0.5)).reshape(bsz, heads, rows, GRID_W, dh)
    kg = k.reshape(bsz, heads, rows, GRID_W, dh)[:, :, key_rows]
    vg = v.reshape(bsz, heads, rows, GRID_W, dh)[:, :, key_rows]
    s_win = jnp.einsum('bhrqd,bhrkwd->bhrqkw', qg, kg).astype(jnp.float32) + bias.astype(jnp.float32)
    s_win = jnp.where(col_mask[:, None, :], s_win, NEG_INF).reshape(bsz, heads, rows, GRID_W, kr * GRID_W)
    s_ctx = jnp.einsum('bhrqd,bhld->bhrql', qg, k_ctx).astype(jnp.float32)
    pr = jax.nn.softmax(jnp.concatenate([s_win, s_ctx], axis=-1), axis=-1).astype(v.dtype)
    p_win = pr[..., :kr * GRID_W].reshape(bsz, heads, rows, GRID_W, kr, GRID_W)
    p_ctx = pr[..., kr * GRID_W:]
    o = (jnp.einsum('bhrqkw,bhrkwd->bhrqd', p_win, vg)
         + jnp.einsum('bhrql,bhld->bhrqd', p_ctx, v_ctx))
    return o.reshape(bsz, heads, n_tok, dh)

def swiglu(x, wg, wu, wd):
    return (jax.nn.silu(x @ wg) * (x @ wu)) @ wd

def moe(x, w_router_l, wg, wu, wd):
    logits = (x @ w_router_l).astype(jnp.float32)
    top_v, top_i = lax.top_k(logits, TOP_K)
    gates = jax.nn.softmax(top_v, axis=-1)
    combine = jnp.sum(jax.nn.one_hot(top_i, N_EXPERTS, dtype=jnp.float32) * gates[..., None], axis=-2)
    combine = combine.astype(x.dtype)
    out = jnp.zeros_like(x)
    for e in range(N_EXPERTS):
        out = out + combine[..., e:e + 1] * swiglu(x, wg[e], wu[e], wd[e])
    return out

def channel_mixer(hn, p, l):
    idx = l // 2
    if l % 2 == 0:
        return swiglu(hn, p['ffn_w_gate'][idx], p['ffn_w_up'][idx], p['ffn_w_down'][idx])
    return moe(hn, p['w_router'][idx], p['moe_w_gate'][idx], p['moe_w_up'][idx], p['moe_w_down'][idx])

def context_pass(x, c_ctx, p):
    cond = c_ctx[None, :]
    lru_states, ks, vs = [], [], []
    for l in range(DEPTH):
        idx = l // 2
        sh1, sc1, g1, sh2, sc2, g2 = adaln(cond, p['w_mod'][l], p['b_mod'][l])
        hn = modulate(rmsnorm(x, p['norm1_g'][l]), sh1, sc1)
        if l % 2 == 0:
            h0 = jnp.zeros((x.shape[0], 2, LRU_WIDTH), jnp.float32)
            mix, h_f, h_b = recurrent_conv_mixer(hn, p, idx, h0)
            lru_states.append(jnp.stack([h_f[:, -1], h_b[:, 0]], axis=1).astype(x.dtype))
        else:
            q, k, v = qkv_heads(hn, p['w_qkv'][idx])
            mix = merge_heads(context_attention(q, k, v)) @ p['w_o'][idx]
            ks.append(k)
            vs.append(v)
        x = x + g1 * mix
        hn = modulate(rmsnorm(x, p['norm2_g'][l]), sh2, sc2)
        x = x + g2 * channel_mixer(hn, p, l)
    y = rmsnorm(x, p['final_g'])
    return y, jnp.stack(lru_states, axis=1), jnp.stack(ks, axis=1), jnp.stack(vs, axis=1)

def denoise_pass(x, c, state_lru, cache_k, cache_v, p):
    for l in range(DEPTH):
        idx = l // 2
        sh1, sc1, g1, sh2, sc2, g2 = adaln(c, p['w_mod'][l], p['b_mod'][l])
        hn = modulate(rmsnorm(x, p['norm1_g'][l]), sh1, sc1)
        if l % 2 == 0:
            mix, _, _ = recurrent_conv_mixer(hn, p, idx, state_lru[:, idx])
        else:
            q, k, v = qkv_heads(hn, p['w_qkv'][idx])
            o = neighbourhood_attention(q, k, v, cache_k[:, idx], cache_v[:, idx], p['rpb'][idx])
            mix = merge_heads(o) @ p['w_o'][idx]
        x = x + g1 * mix
        hn = modulate(rmsnorm(x, p['norm2_g'][l]), sh2, sc2)
        x = x + g2 * channel_mixer(hn, p, l)
    return rmsnorm(x, p['final_g'])

def setup_inputs(seed: int = 0) -> dict:
    key = jax.random.key(seed)
    k = jax.random.split(key, 33)

    def nrm(i, shape, scale=1.0):
        return jax.random.normal(k[i], shape, jnp.float32) * scale

    d, f = D_MODEL, D_FF
    a_c = jax.random.uniform(k[21], (N_EVEN, 2, LRU_WIDTH), jnp.float32, 0.9, 0.999)
    sig = a_c ** (1.0 / LRU_C)
    lru_lam = jnp.log(sig) - jnp.log1p(-sig)
    mix_w = LRU_WIDTH + SC_WIDTH
    return {
        'x_prompt': nrm(0, (BATCH, SEQ, d)),
        'x_sample': nrm(1, (DEC_BATCH, DEC_SEQ, d)),
        'state_lru': nrm(2, (DEC_BATCH, N_EVEN, 2, LRU_WIDTH), 0.5),
        'cache_k': nrm(3, (DEC_BATCH, N_ODD, N_HEADS, PAST_LEN, HEAD_DIM)),
        'cache_v': nrm(4, (DEC_BATCH, N_ODD, N_HEADS, PAST_LEN, HEAD_DIM)),
        'c': nrm(5, (DEC_BATCH, d)),
        'c_ctx': nrm(6, (d,)),
        'norm1_g': 1.0 + nrm(7, (DEPTH, d), 0.05),
        'norm2_g': 1.0 + nrm(8, (DEPTH, d), 0.05),
        'w_mod': nrm(9, (DEPTH, d, 6 * d), 0.5 * d ** -0.5),
        'b_mod': nrm(10, (DEPTH, 6 * d), 0.02),
        'w_in': nrm(11, (N_EVEN, d, IN_WIDTH), d ** -0.5),
        'lru_conv_w': nrm(12, (N_EVEN, LRU_CONV, LRU_WIDTH), LRU_CONV ** -0.5),
        'lru_conv_b': nrm(13, (N_EVEN, LRU_WIDTH), 0.02),
        'lru_wa': nrm(14, (N_EVEN, 2, LRU_HEADS, LRU_BLOCK, LRU_BLOCK), LRU_BLOCK ** -0.5),
        'lru_ba': nrm(15, (N_EVEN, 2, LRU_WIDTH), 0.02),
        'lru_wx': nrm(16, (N_EVEN, 2, LRU_HEADS, LRU_BLOCK, LRU_BLOCK), LRU_BLOCK ** -0.5),
        'lru_bx': nrm(17, (N_EVEN, 2, LRU_WIDTH), 0.02),
        'lru_lam': lru_lam,
        'sc_conv_w': nrm(18, (N_EVEN, SC_CONV, SC_WIDTH), SC_CONV ** -0.5),
        'sc_conv_b': nrm(19, (N_EVEN, SC_WIDTH), 0.02),
        'w_out': nrm(20, (N_EVEN, mix_w, d), mix_w ** -0.5),
        'ffn_w_gate': nrm(22, (N_EVEN, d, f), d ** -0.5),
        'ffn_w_up': nrm(23, (N_EVEN, d, f), d ** -0.5),
        'ffn_w_down': nrm(24, (N_EVEN, f, d), f ** -0.5),
        'w_qkv': nrm(25, (N_ODD, d, 3 * d), d ** -0.5),
        'w_o': nrm(26, (N_ODD, d, d), d ** -0.5),
        'rpb': nrm(27, (N_ODD, N_HEADS, 2 * WIN_R - 1, 2 * WIN_C - 1), 0.2),
        'w_router': nrm(28, (N_ODD, d, N_EXPERTS), d ** -0.5),
        'moe_w_gate': nrm(29, (N_ODD, N_EXPERTS, d, f), d ** -0.5),
        'moe_w_up': nrm(30, (N_ODD, N_EXPERTS, d, f), d ** -0.5),
        'moe_w_down': nrm(31, (N_ODD, N_EXPERTS, f, d), f ** -0.5),
        'final_g': 1.0 + nrm(32, (d,), 0.05),
    }

def reference(x_prompt, x_sample, state_lru, cache_k, cache_v, c, c_ctx, norm1_g, norm2_g, w_mod, b_mod,
              w_in, lru_conv_w, lru_conv_b, lru_wa, lru_ba, lru_wx, lru_bx, lru_lam, sc_conv_w, sc_conv_b,
              w_out, ffn_w_gate, ffn_w_up, ffn_w_down, w_qkv, w_o, rpb, w_router, moe_w_gate, moe_w_up,
              moe_w_down, final_g):
    p = {
        'norm1_g': norm1_g, 'norm2_g': norm2_g, 'w_mod': w_mod, 'b_mod': b_mod,
        'w_in': w_in, 'lru_conv_w': lru_conv_w, 'lru_conv_b': lru_conv_b,
        'lru_wa': lru_wa, 'lru_ba': lru_ba, 'lru_wx': lru_wx, 'lru_bx': lru_bx, 'lru_lam': lru_lam,
        'sc_conv_w': sc_conv_w, 'sc_conv_b': sc_conv_b, 'w_out': w_out,
        'ffn_w_gate': ffn_w_gate, 'ffn_w_up': ffn_w_up, 'ffn_w_down': ffn_w_down,
        'w_qkv': w_qkv, 'w_o': w_o, 'rpb': rpb,
        'w_router': w_router, 'moe_w_gate': moe_w_gate, 'moe_w_up': moe_w_up, 'moe_w_down': moe_w_down,
        'final_g': final_g,
    }
    y_prompt, new_state_lru, new_cache_k, new_cache_v = context_pass(x_prompt, c_ctx, p)
    y_sample = denoise_pass(x_sample, c, state_lru, cache_k, cache_v, p)
    return (y_prompt, y_sample, new_state_lru, new_cache_k, new_cache_v)


_drawn_inputs = setup_inputs


def setup_inputs(seed=0):
    import zlib

    import numpy as np

    out = dict(_drawn_inputs(seed))
    spreads = {}
    factors = {'lru_ba': 8.0, 'lru_bx': 7.355, 'sc_conv_b': 7.785, 'rpb': 8.0, 'cache_k': 2.725}
    for name, (base, spread) in spreads.items():
        noise = np.random.default_rng([zlib.crc32(name.encode()), seed]).standard_normal(out[name].shape)
        drawn = base * np.exp(spread * noise) if base else spread * noise
        out[name] = __import__('jax').numpy.asarray(drawn.astype(out[name].dtype))
    for name, factor in factors.items():
        out[name] = (out[name] * factor).astype(out[name].dtype)
    return out
```

```python
from contextlib import ExitStack

import numpy as np
import concourse.bass as bass
from concourse import mybir

F32 = mybir.dt.float32
I32 = mybir.dt.int32
U32 = mybir.dt.uint32
ALU = mybir.AluOpType
ACT = mybir.ActivationFunctionType
AX_X = mybir.AxisListType.X

P = 128
D = 1024
KC = D // P
T_PROMPT, T_SAMPLE = 128, 256
TILES = (T_PROMPT + T_SAMPLE) // P
GRID_W = 64
HEADS, HD = 16, 64
WIN_C, RPB_R, RPB_C = 16, 15, 31
LRU_W = 512
LC = LRU_W // P
LRU_C = 8.0
D_FF = 2816
STEPS = 11
SF = D_FF // STEPS
EXPERTS = 8
EPS = 1e-6
NEG = -1e30
GAP = 2
W = T_PROMPT + GAP + T_SAMPLE
S0 = T_PROMPT + GAP
TOK = [0, S0, S0 + P]
SLOT = 6144
SLOTS = 3
UNIT = 2048

COL = {}


def columns():
    at = 0
    for name, n in (("b_mod", 96), ("c", 8), ("c_ctx", 8), ("norm1", 16),
                    ("norm2", 16), ("conv_w", 16), ("conv_b", 4), ("ba", 8), ("bx", 8), ("lam", 8),
                    ("sc_w", 12), ("sc_b", 4), ("state", 8)):
        COL[name] = at
        at += n
    return at


N_COLS = columns()
ROWS_B = N_COLS - P

C_ID, C_BEFORE, C_ONES, C_MASK, C_NEG, C_IOTA = 0, 128, 256, 384, 448, 512
C_TOKEN, C_EXP, C_ROW = C_IOTA + 384, C_IOTA + 387, C_IOTA + 395
N_CONST = C_ROW + 8
WORK = 18560


def shape_constants():
    k = np.zeros((P, N_CONST), np.float32)
    p = np.arange(P)
    k[:, C_ID:C_ID + P] = np.eye(P)
    k[:, C_BEFORE:C_BEFORE + P] = p[:, None] < p[None, :]
    k[:, C_ONES:C_ONES + P] = 1.0
    q, w = ((P - 1 - p) % GRID_W)[:, None], np.arange(GRID_W)[None, :]
    start = np.clip(q - WIN_C // 2, 0, GRID_W - WIN_C)
    inside = (w >= start) & (w < start + WIN_C)
    k[:, C_MASK:C_MASK + GRID_W] = inside
    k[:, C_NEG:C_NEG + GRID_W] = np.where(inside, 0.0, NEG)
    k[:, C_IOTA:C_IOTA + 384] = np.arange(384)
    for t in range(TILES):
        k[:, C_TOKEN + t] = p + P * t
    k[:, C_EXP:C_EXP + 8] = np.arange(8)
    k[:, C_ROW:C_ROW + 8] = np.arange(8) * (P * TILES)
    return k


def hybrid_step(nc, consts, x_prompt, x_sample, state_lru, cache_k, cache_v, c, c_ctx, norm1_g, norm2_g,
                w_mod, b_mod, w_in, lru_conv_w, lru_conv_b, lru_wa, lru_ba, lru_wx, lru_bx, lru_lam,
                sc_conv_w, sc_conv_b, w_out, ffn_w_gate, ffn_w_up, ffn_w_down, w_qkv, w_o, rpb, w_router,
                moe_w_gate, moe_w_up, moe_w_down, final_g,
                y_prompt, y_sample, new_state, new_k, new_v):
    ctx = ExitStack()
    with ctx:
        def sb(name, shape, dt=F32):
            return ctx.enter_context(nc.sbuf_tensor(name, shape, dt))

        def sem(name):
            return ctx.enter_context(nc.semaphore(name))

        hn_rows = nc.dram_tensor("hn_rows", (P * TILES, D), F32, kind="Internal").ap()
        y_rows = nc.dram_tensor("y_rows", (EXPERTS * P * TILES + P, D), F32, kind="Internal").ap()

        ring = sb("ring", [P, SLOTS, SLOT])
        mod_extra = sb("mod_extra", [P, UNIT])
        k_sb = sb("k_sb", [P, N_CONST])
        vec_rows = sb("vec_rows", [P, 2, P])
        cols = sb("cols", [P, 2 * P])
        cond = sb("cond", [P, KC, 2])
        modv = sb("modv", [P, 96, 2])
        gains = sb("gains", [P, KC, 2])
        x = sb("x", [P, TILES, D])
        xn = sb("xn", [P, KC * W])
        hn_t = sb("hn_t", [P, KC, W])
        gate_b = sb("gate_b", [P, 2, D])
        stats = sb("stats", [P, 8, 4])
        small = sb("small", [P, 32])
        zeros = sb("zeros", [P, 256])
        router = sb("router", [P, KC, EXPERTS])
        work = sb("work", [P, WORK])

        def at(off, *dims):
            n = int(np.prod(dims))
            v = work[:, off:off + n]
            if len(dims) == 2:
                v = v.rearrange("p (a b) -> p a b", a=dims[0])
            if len(dims) == 3:
                v = v.rearrange("p (a b c) -> p a b c", a=dims[0], b=dims[1])
            return v

        ident = k_sb[:, C_ID:C_ID + P]
        before = k_sb[:, C_BEFORE:C_BEFORE + P]
        ones = k_sb[:, C_ONES:C_ONES + P]
        xn_tok = xn[:, 0:TILES * D].rearrange("p (t d) -> p t d", t=TILES)
        y_t = xn[:, :].rearrange("p (c w) -> p c w", c=KC)

        PW = W + 3
        xpad = at(0, LC, PW)
        cvpad = at(LC * PW, LC, PW)
        o = 2 * LC * PW
        xc = at(o, LC, W)
        gr = [at(o + (1 + d) * LC * W, LC, W) for d in range(2)]
        gi = [at(o + (3 + d) * LC * W, LC, W) for d in range(2)]
        dec = at(o + 5 * LC * W, LC, W)
        tmp = at(o + 6 * LC * W, LC, W)
        o += 7 * LC * W
        bd = at(o, 16, P)
        o += 16 * P
        sc_conv = xpad[:, :, 0:W]
        lamk = at(o, 2 * LC)
        lamz = at(o + 8, 2 * LC)
        lamp = at(o + 16, 2 * LC)
        st8 = at(o + 24, 8)
        st_rows = at(o + 32, P)
        assert o + 160 <= WORK
        diag = mod_extra[:, :].rearrange("p (g c f) -> p g c f", g=2, c=KC)

        bias = at(0, HEADS * 6, GRID_W)
        o = HEADS * 6 * GRID_W
        q_t = at(o, KC, W)
        kk_t = at(o + KC * W, KC, W)
        v_tok = at(o + 2 * KC * W, TILES, D)
        o += 2 * KC * W + TILES * D
        kc_t = at(o, KC, P)
        vc = at(o + D, D)
        s_buf = mod_extra[:, 0:768].rearrange("p (a b) -> p a b", a=2)
        p_buf = mod_extra[:, 768:1536].rearrange("p (a b) -> p a b", a=2)
        pt_buf = at(o + 2 * D, 2, 384)
        kc_tok = at(o + 2 * D, D)
        k_out = xn[:, 0:D]
        sums = at(o + 3 * D, TILES, HEADS)
        mx = at(o + 3 * D + 48, 2, 1)
        nmx = at(o + 3 * D + 50, 2, 1)
        assert o + 3 * D + 52 <= WORK

        def step_buffers(off):
            return at(off, SF), at(off + SF, SF), at(off + 2 * SF, 2, P)

        xg = [at(0, D), at(D, D)]
        xg_t = [at(2 * D, KC, P), at(3 * D, KC, P)]
        y_out = [at(4 * D, D), at(5 * D, D)]
        got = [at(6 * D, TILES, D), at(9 * D, TILES, D)]
        fin_b = at(12 * D, D)
        slot_hot = at(13 * D, 2, TILES, 384)
        o = 13 * D + 6 * 384
        lg, m8, oh1, oh2, mask, rank, rankm, rk_e, pick = (at(o + 24 * n, TILES, EXPERTS) for n in range(9))
        o += 216
        w12 = at(o, 2, TILES)
        e12 = at(o + 6, 2, TILES)
        pos_f = at(o + 12, 2, TILES)
        dv = at(o + 18, TILES)
        cnt_f = at(o + 21, EXPERTS)
        idx_f = at(o + 32, 24)
        moe_buf = step_buffers(o + 64)
        ffn_buf = step_buffers(HEADS * 6 * GRID_W)
        assert o + 64 + 3 * SF <= WORK
        i8 = sb("i8", [P, TILES, 8], U32)
        pos_i = sb("pos_i", [P, 6], U32)
        idx_a = sb("idx_a", [P, 17], U32)
        idx_b = sb("idx_b", [P, 17], U32)
        idx_now = sb("idx_now", [P, 2], U32)
        over = sb("over", [1, 24], I32)

        ps = ctx.enter_context(nc.psum_tensor("ps", [P, 8, 512], F32))

        s_const, s_x, s_vec, s_bd, s_cache, s_bias, s_router = (sem("ld_" + n) for n in
            ("const", "x", "vec", "bd", "cache", "bias", "router"))
        s_vc, s_fin = sem("ld_vc"), sem("ld_fin")
        ring_full = [sem(f"ring_full{s}") for s in range(SLOTS)]
        ring_free = [sem(f"ring_free{s}") for s in range(SLOTS)]
        mod_full = [sem(f"mod_full{s}") for s in range(4)]
        mod_used = sem("mod_used")
        vec_t, cols_ok, cond_ok = sem("vec_turned"), sem("cols_ok"), sem("cond_ok")
        mod_ok = sem("mod_ok")
        gains_ok = sem("gains_ok")
        ssq_ok, std_ok, xn_ok = sem("ssq_ok"), sem("std_ok"), sem("xn_ok")
        var_ok = sem("var_ok")
        nt_done = sem("norm_turned")
        hn_dve, hn_act = sem("hn_dve"), sem("hn_act")
        gap_ok, bdz = sem("gap_ok"), sem("bd_zeroed")
        pj = sem("proj_done")
        ev_d, ev_a = sem("proj_evac_dve"), sem("proj_evac_act")
        lam_e, lam_ok = sem("lam_exp"), sem("lam_ok")
        xc_ok = sem("xc_ok")
        tanh_ok, m_ok, root_ok, mix_ok = sem("tanh_ok"), sem("m_ok"), sem("root_ok"), sem("mix_ok")
        st_ok, st_t, st_out = sem("st_ok"), sem("st_turned"), sem("st_out")
        diag_ok, gb_ps, gb_ok = sem("diag_ok"), sem("gate_spread"), sem("gate_b_ok")
        out_ps, res_ok = sem("mix_product"), sem("residual_ok")
        gu_ready = [sem(f"gu_ready{k}") for k in range(3)]
        silu_ok = [sem(f"silu_ok{k}") for k in range(3)]
        h_ok = [sem(f"h_ok{k}") for k in range(3)]
        h_turned = [sem(f"h_turned{k}") for k in range(3)]
        ht_ok = [sem(f"ht_ok{k}") for k in range(3)]
        ffn_done = sem("ffn_done")
        qk_ps, qk_ok, v_ps, v_ok = sem("qk_ps"), sem("qk_ok"), sem("v_ps"), sem("v_ok")
        kt_ps, kt_ok, ctx_t, ctx_ok = sem("kt_ps"), sem("kt_ok"), sem("ctx_turned"), sem("ctx_ok")
        st_kv = sem("st_kv")
        bias_ok = sem("bias_ok")
        sc_ps, s_ok, max_ok, p_ok, pt_ps, pt_ok, pv = (sem(n) for n in
            ("score_ps", "score_ok", "max_ok", "prob_ok", "prob_turned", "prob_t_ok", "pv_done"))
        o_ok, ot_ps, ot_ok = sem("o_ok"), sem("o_turned"), sem("o_t_ok")
        hk_ps, hk_ok, hk_st = sem("hn_tok_ps"), sem("hn_tok_ok"), sem("hn_tok_stored")
        lg_ps, mask_ok, rk_ps, rk_ok = sem("logit_ps"), sem("mask_ok"), sem("rank_ps"), sem("rank_ok")
        hot_ok, hot_used, route_ok = sem("hot_ok"), sem("hot_used"), sem("route_ok")
        idx_ok, gathered, xg_turned, xgt_d, xgt_a = (
            [sem(n + k) for k in "ab"] for n in ("idx_ok", "gathered", "xg_turned", "xg_t_dve_", "xg_t_act_"))
        done, y_d, y_a, y_st = ([sem(n + k) for k in "ab"] for n in ("expert_done_", "y_dve_", "y_act_", "y_stored_"))
        collected = sem("collected")
        rounds_over = sem("stores_over")
        y_fin, st_y = sem("y_fin"), sem("st_y")
        v_dve_ok, hk_dve, top_ok, y_ok = sem("v_dve_ok"), sem("hn_tok_dve"), sem("top_ok"), sem("mixer_y_ok")
        qk_dve, ctx_d, ot_d, ffn_ps = sem("qk_dve_ok"), sem("ctx_dve_ok"), sem("o_t_dve"), sem("ffn_ps")
        exp_v, st_r, gather_go = sem("gate_exp"), sem("state_rows"), sem("gather_go")
        zero_ok, y_zero = sem("zero_ok"), sem("y_rows_zeroed")
        chain_d, chain_a, chain_p = sem("dve_order"), sem("act_order"), sem("pool_order")

        F_IN, F_OUT, F_FFN, F_QKV, F_O, F_MOE = 0, 5, 7, 18, 24, 26
        n_dma = [1] * 7 + [3] * STEPS + [1] * 8

        def slot_of(n):
            return n % SLOTS

        def filled(n):
            return 16 * sum(n_dma[m] for m in range(n + 1) if m % SLOTS == n % SLOTS)

        def moe_slot(j):
            return (F_MOE + j) % SLOTS

        def frees(n):
            return n == F_OUT or F_FFN <= n < F_FFN + STEPS - 1 or n == F_O

        def last_use(n):
            if frees(n):
                return ring_free[slot_of(n)], sum(frees(m) for m in range(n + 1) if m % SLOTS == n % SLOTS)
            if n < F_OUT:
                return pj, first_item["xcvbg"[n]] + 4
            if F_QKV <= n < F_QKV + 4:
                return qk_ps, 4 * (n - F_QKV + 1)
            if F_QKV + 4 <= n < F_O:
                return v_ps, 3 * (n - F_QKV - 3)
            return out_ps, TILES * {F_OUT + 1: 1, F_FFN + STEPS - 1: 2, F_O + 1: 3}[n]

        PER = [sum(1 for j in range(STEPS) if moe_slot(j) == s) for s in range(SLOTS)]
        BASE_FULL = [16 * sum(n_dma[m] for m in range(F_MOE) if m % SLOTS == s) for s in range(SLOTS)]
        PER_FREE = [sum(1 for j in range(STEPS - 1) if moe_slot(j) == s) for s in range(SLOTS)]
        BASE_FREE = [sum(frees(m) for m in range(F_MOE) if m % SLOTS == s) for s in range(SLOTS)]

        def nth(j):
            return sum(1 for m in range(j) if moe_slot(m) == moe_slot(j))

        def nth_free(j):
            return sum(1 for m in range(max(j - SLOTS + 1, 0)) if moe_slot(m) == moe_slot(j))

        def mod_slot(s):
            return mod_extra[:, :] if s == 3 else ring[:, s, 2 * UNIT:3 * UNIT]

        def slab(n):
            return ring[:, slot_of(n), 0:4096].rearrange("p (k f) -> p k f", k=KC)

        def ff_slot(s):
            r = ring[:, s, :]
            return (r[:, 0:2048].rearrange("p (k f) -> p k f", k=KC),
                    r[:, 2048:4096].rearrange("p (k f) -> p k f", k=KC),
                    r[:, 4096:6144].rearrange("p (f d) -> p f d", f=2))

        kview = "(k p) f -> p k f"
        IN_ORDER = [0, 3, 4, 2, 1]
        QKV_ORDER = [2, 3, 0, 1, 4, 5]
        MOD_SPLIT = [(0, 2), (2, 4), (4, 6), (6, 8), (8, 10), (10, 12)]

        items = []
        for g, (kind, eng) in enumerate((("x", "d"), ("c", "a"), ("gate", "a"), ("v", "d"), ("b", "a"), ("g", "a"))):
            for m in range(16 if kind == "gate" else 4):
                items.append((kind, m, eng))
        ev_n = []
        nd = na = 0
        for kind, m, eng in items:
            nd, na = nd + (eng == "d"), na + (eng == "a")
            ev_n.append((ev_d, nd) if eng == "d" else (ev_a, na))
        first_item = {}
        for n, (kind, m, eng) in enumerate(items):
            first_item.setdefault(kind, n)
        PB = 6

        units = [(t, h) for t in (1, 2, 0) for h in range(HEADS)]

        def reverse(v):
            return v.rearrange("p (t q) -> p t q", t=2)[:, :, ::-1]

        def by_tile(v):
            return v.rearrange("p (t q) -> p t q", t=2)

        block = ctx.enter_context(nc.Block())

        @block.sync
        def _(sp):
            def fill(n, dst, src):
                if n >= SLOTS:
                    sp.wait_ge(*last_use(n - SLOTS))
                sp.dma_start(dst, src).then_inc(ring_full[slot_of(n)], 16)

            def mod_group(src, g, first):
                for s in range(4):
                    if not first:
                        sp.wait_ge(mod_used, g * 4 + (s - 3))
                    sp.dma_start(mod_slot(s).rearrange("p (k f) -> p k f", k=KC),
                                 src(s)).then_inc(mod_full[s], 16)

            w0, w1 = (w_mod[l].rearrange(kview, p=P) for l in range(2))
            mod_group(lambda s: w0[:, :, s * 256:(s + 1) * 256], 0, True)
            mod_group(lambda s: w0[:, :, (4 + s) * 256:(5 + s) * 256], 1, False)
            win = w_in[0].rearrange(kview, p=P)
            for f in range(5):
                g = IN_ORDER[f]
                fill(F_IN + f, slab(F_IN + f), win[:, :, g * 512:(g + 1) * 512])
                lo, hi = MOD_SPLIT[f + 1]
                wl, off = (w0, 0) if hi <= 6 else (w1, 6)
                with sp.Fori(lo, hi) as g:
                    mod_group(lambda s: wl[:, :, bass.ds(((g - off) * 4 + s) * 256, 256)], g, False)
            for f in range(2):
                fill(F_OUT + f, slab(F_OUT + f), w_out[0].rearrange(kview, p=P)[:, :, f * 512:(f + 1) * 512])
            sp.wait_ge(mod_used, 48)
            wg, wu = ffn_w_gate[0].rearrange(kview, p=P), ffn_w_up[0].rearrange(kview, p=P)
            wd = ffn_w_down[0].rearrange("(j f p) d -> p j f d", p=P, f=2)
            for j in range(STEPS):
                n = F_FFN + j
                g_s, u_s, d_s = ff_slot(slot_of(n))
                fill(n, g_s, wg[:, :, j * SF:(j + 1) * SF])
                sp.dma_start(u_s, wu[:, :, j * SF:(j + 1) * SF]).then_inc(ring_full[slot_of(n)], 16)
                sp.dma_start(d_s, wd[:, j]).then_inc(ring_full[slot_of(n)], 16)
            wq = w_qkv[0].rearrange(kview, p=P)
            for f in range(6):
                g = QKV_ORDER[f]
                fill(F_QKV + f, slab(F_QKV + f), wq[:, :, g * 512:(g + 1) * 512])
            for f in range(2):
                fill(F_O + f, slab(F_O + f), w_o[0].rearrange(kview, p=P)[:, :, f * 512:(f + 1) * 512])

            wge = moe_w_gate[0].rearrange("e (k p) f -> p e k f", p=P)
            wue = moe_w_up[0].rearrange("e (k p) f -> p e k f", p=P)
            wde = moe_w_down[0].rearrange("e (j f p) d -> p e j f d", p=P, f=2)

            def moe_fill(e, j):
                s = moe_slot(j)
                g_s, u_s, d_s = ff_slot(s)
                sp.dma_start(g_s, wge[:, bass.ds(e, 1), :, j * SF:(j + 1) * SF]
                             .rearrange("p e k f -> p (e k) f")).then_inc(ring_full[s], 16)
                sp.dma_start(u_s, wue[:, bass.ds(e, 1), :, j * SF:(j + 1) * SF]
                             .rearrange("p e k f -> p (e k) f")).then_inc(ring_full[s], 16)
                sp.dma_start(d_s, wde[:, bass.ds(e, 1), j].rearrange("p e f d -> p (e f) d"))\
                    .then_inc(ring_full[s], 16)

            for j in range(STEPS):
                if j < SLOTS:
                    sp.wait_ge(*last_use(F_MOE + j - SLOTS))
                else:
                    sp.wait_ge(ring_free[moe_slot(j)], BASE_FREE[moe_slot(j)] + nth(j))
                moe_fill(0, j)
            sp.wait_ge(route_ok, 1)
            rounds = sp.value_load(over[0:1, 20:21], min_val=EXPERTS, max_val=2 * EXPERTS)
            with sp.Fori(1, rounds) as i:
                e = sp.snap(i % EXPERTS, min_val=0, max_val=EXPERTS - 1)
                for j in range(STEPS):
                    s = moe_slot(j)
                    if j < SLOTS and s == moe_slot(STEPS - 1):
                        sp.wait_ge(done[0], i)
                        sp.wait_ge(done[1], i)
                    else:
                        sp.wait_ge(ring_free[s], i * PER_FREE[s] + (BASE_FREE[s] + nth_free(j)))
                    moe_fill(e, j)

        @block.gpsimd
        def _(pool):
            n_chain = [0]

            def ordered(ins):
                n_chain[0] += 1
                ins.then_inc(chain_p, 1)
                pool.wait_ge(chain_p, n_chain[0])

            pool.memset(zeros[:, :], 0.0).then_inc(zero_ok, 1)
            pool.memset(bd, 0.0).then_inc(bdz, 1)
            pool.memset(xpad, 0.0).then_inc(gap_ok, 1)
            pool.memset(cvpad, 0.0).then_inc(gap_ok, 1)
            pool.memset(hn_t[:, :, T_PROMPT:S0], 0.0).then_inc(gap_ok, 1)
            pool.wait_ge(s_bias, 16 * 2 * HEADS)
            inside = k_sb[:, C_MASK:C_MASK + GRID_W].unsqueeze(1).to_broadcast([P, HEADS * 6, GRID_W])
            outside = k_sb[:, C_NEG:C_NEG + GRID_W].unsqueeze(1).to_broadcast([P, HEADS * 6, GRID_W])
            ordered(pool.tensor_tensor(bias, bias, inside, ALU.mult))
            pool.tensor_tensor(bias, bias, outside, ALU.add).then_inc(bias_ok, 1)

            pool.wait_ge(route_ok, 1)
            pool.wait_ge(hk_st, 16 * TILES)
            rounds = pool.value_load(over[0:1, 20:21], min_val=EXPERTS, max_val=2 * EXPERTS)

            def gather(k, col):
                table = (idx_a, idx_b)[k]
                pool.tensor_copy(idx_now[:, k:k + 1], table[:, col]).then_inc(idx_ok[k], 1)

            def gather_rows(k):
                pool.indirect_dma_start(
                    out=xg[k], out_offset=None, in_=hn_rows,
                    in_offset=bass.IndirectOffsetOnAxis(ap=idx_now[:, k:k + 1], axis=0),
                ).then_inc(gathered[k], 16)

            for k in range(2):
                gather(k, slice(0, 1))
                pool.wait_ge(idx_ok[k], 1)
                gather_rows(k)
            with pool.Fori(0, rounds) as i:
                for k in range(2):
                    pool.wait_ge(gathered[k], i * 16 + 16)
                    pool.wait_ge(xg_turned[k], i + 1)
                    gather(k, bass.ds(i + 1, 1))
                    pool.wait_ge(idx_ok[k], i + 2)
                    pool.sem_inc(gather_go, 1)
                    gather_rows(k)
            pool.wait_ge(rounds_over, 1)
            for k in range(2):
                for t in range(TILES):
                    pool.indirect_dma_start(
                        out=got[k][:, t, :], out_offset=None, in_=y_rows,
                        in_offset=bass.IndirectOffsetOnAxis(ap=pos_i[:, 3 * k + t:3 * k + t + 1], axis=0),
                    ).then_inc(collected, 16)
            pool.wait_ge(collected, 16 * 2 * TILES)

        @block.scalar
        def _(act):
            n_chain = [0]

            def ordered(ins):
                n_chain[0] += 1
                ins.then_inc(chain_a, 1)
                act.wait_ge(chain_a, n_chain[0])

            act.dma_start(k_sb[:, :], consts).then_inc(s_const, 16)
            rows = [(vec_rows[0:96, 0, :], b_mod.rearrange("l (r p) -> (l r) p", p=P)),
                    (vec_rows[96:104, 0, :], c.rearrange("b (r p) -> (b r) p", p=P)),
                    (vec_rows[104:112, 0, :], c_ctx.rearrange("(r p) -> r p", p=P)),
                    (vec_rows[112:128, 0, :], norm1_g.rearrange("l (r p) -> (l r) p", p=P))]
            for name, src in (("norm2", norm2_g.rearrange("l (r p) -> (l r) p", p=P)),
                              ("conv_w", lru_conv_w[0].rearrange("k (r p) -> (k r) p", p=P)),
                              ("conv_b", lru_conv_b.rearrange("l (r p) -> (l r) p", p=P)),
                              ("ba", lru_ba[0].rearrange("d (r p) -> (d r) p", p=P)),
                              ("bx", lru_bx[0].rearrange("d (r p) -> (d r) p", p=P)),
                              ("lam", lru_lam[0].rearrange("d (r p) -> (d r) p", p=P)),
                              ("sc_w", sc_conv_w[0].rearrange("k (r p) -> (k r) p", p=P)),
                              ("sc_b", sc_conv_b.rearrange("l (r p) -> (l r) p", p=P)),
                              ("state", state_lru[0, 0].rearrange("d (r p) -> (d r) p", p=P))):
                r = COL[name] - P
                rows.append((vec_rows[r:r + src.shape[0], 1, :], src))
            for dst, src in rows:
                act.dma_start(dst, src).then_inc(s_vec, 16)
            act.dma_start(x[:, 0, :], x_prompt[0]).then_inc(s_x, 16)
            act.dma_start(x[:, 1:3, :], x_sample[0].rearrange("(t p) d -> p t d", p=P)).then_inc(s_x, 16)
            act.wait_ge(bdz, 1)
            for d in range(2):
                for g, wt in enumerate((lru_wa, lru_wx)):
                    for b in range(2):
                        dst = bd[64 * b:64 * b + 64, (2 * d + g) * LC:(2 * d + g + 1) * LC, 64 * b:64 * b + 64]
                        src = wt[0, d].rearrange("(c b) i j -> b i c j", b=2)[b]
                        act.dma_start(dst, src).then_inc(s_bd, 16)
            act.dma_start(router[:, :, :], w_router[0].rearrange("(k p) e -> p k e", p=P)).then_inc(s_router, 16)

            act.wait_ge(cols_ok, 1)
            act.activation(cond[:, :, 0], cols[:, COL["c_ctx"]:COL["c_ctx"] + 8], ACT.Silu).then_inc(cond_ok, 1)
            act.activation(cond[:, :, 1], cols[:, COL["c"]:COL["c"] + 8], ACT.Silu).then_inc(cond_ok, 1)

            def norm(n):
                if n == 0:
                    act.wait_ge(s_x, 32)
                else:
                    act.wait_ge(res_ok, n * TILES)
                for t in range(TILES):
                    act.activation(xn_tok[:, t, :], x[:, t, :], ACT.Square,
                                   accum_out=stats[:, n, t:t + 1]).then_inc(ssq_ok, 1)
                act.wait_ge(var_ok, n + 1)
                act.activation(stats[:, n, 0:3], stats[:, n, 0:3], ACT.Sqrt).then_inc(std_ok, 1)
                if n == 4:
                    return
                act.wait_ge(gains_ok, n + 1)
                base = (n // 2) * 48 + (n % 2) * 24
                for ci in range(KC):
                    if ci % 2:
                        act.wait_ge(nt_done, n * KC + ci + 1)
                        for g, (lo, hi, plo) in enumerate(((0, T_PROMPT, 0), (S0, W, P))):
                            ins = act.activation(hn_t[:, ci, lo:hi], ps[:, ci, plo:plo + hi - lo], ACT.Identity,
                                                 bias=modv[:, base + ci, g:g + 1], scale=gains[:, ci, g:g + 1])
                        ins.then_inc(hn_act, 1)

            def gate_in(n):
                for g in range(2):
                    for hf in range(2):
                        if n and g == 0 and hf == 0:
                            act.wait_ge(res_ok, n * TILES)
                        act.wait_ge(gb_ps, 4 * n + 2 * g + hf + 1)
                        act.activation(gate_b[:, g, hf * 512:(hf + 1) * 512], ps[:, 6 - 2 * g + hf, :],
                                       ACT.Copy).then_inc(gb_ok, 1)

            norm(0)
            act.wait_ge(lam_e, 1)
            act.activation(lamz, lamz, ACT.Exp).then_inc(lam_e, 1)

            for n, (kind, m, eng) in enumerate(items):
                if eng != "a":
                    continue
                act.wait_ge(pj, n + 1)
                src = ps[:, n % PB, 0:W]
                if kind == "c":
                    act.wait_ge(gap_ok, 3)
                    ins = act.activation(cvpad[:, m, 2:2 + W], src, ACT.Copy)
                elif kind == "gate":
                    d, g, ch = m // 8, m // 4 % 2, m % 4
                    dst = (gr, gi)[g][d]
                    col = COL[("ba", "bx")[g]] + d * LC + ch
                    ins = act.activation(dst[:, ch, :], src, ACT.Sigmoid, bias=cols[:, col:col + 1])
                elif kind == "b":
                    ins = act.activation(y_t[:, LC + m, :], src, ACT.Copy)
                else:
                    ins = act.activation(y_t[:, m, :], src, ACT.Gelu_apprx_tanh)
                ins.then_inc(ev_a, 1)
                if kind == "gate" and m == 15:
                    act.wait_ge(lam_ok, 1)
                    for d in range(2):
                        if d:
                            act.wait_ge(mix_ok, 1)
                        act.wait_ge(ev_a, [v for (s, v), it in zip(ev_n, items) if it[:2] == ("gate", 15)][0])
                        for ch in range(LC):
                            act.activation(dec[:, ch, :], gr[d][:, ch, :], ACT.Exp,
                                           scale=lamk[:, d * LC + ch:d * LC + ch + 1])
                        for ch in range(LC):
                            ins = act.activation(gr[d][:, ch, :], gr[d][:, ch, :], ACT.Tanh,
                                                 scale=lamk[:, d * LC + ch:d * LC + ch + 1])
                        ins.then_inc(tanh_ok, 1)
                        act.wait_ge(m_ok, d + 1)
                        act.activation(gr[d], gr[d], ACT.Sqrt).then_inc(root_ok, 1)

            gate_in(0)
            act.wait_ge(zero_ok, 1)
            busy = [y_rows[(e * TILES + 1) * P:(e + 1) * TILES * P, :] for e in range(EXPERTS)]
            for dst in (*busy, y_rows[EXPERTS * TILES * P:, :]):
                dst = dst.rearrange("(p r) (q f) -> p (r q) f", p=P, f=256)
                act.dma_start(dst, zeros[:, :].unsqueeze(1).to_broadcast([P, dst.shape[1], 256])).then_inc(y_zero, 16)
            act.wait_ge(y_ok, 1)
            for h in range(HEADS):
                for rl in range(2):
                    first = (h * RPB_R + 4 + rl) * RPB_C + (WIN_C - 1) - (GRID_W - 1)
                    src = bass.AP(rpb.tensor, first, [[1, GRID_W], [RPB_C, 6], [1, GRID_W]])
                    act.dma_start(bias[64 * rl:64 * rl + 64, 6 * h:6 * h + 6, :], src).then_inc(s_bias, 16)
            act.dma_start(kc_tok, cache_k[0, 0].rearrange("h s d -> s h d")).then_inc(s_cache, 16)
            act.dma_start(vc, cache_v[0, 0].rearrange("h s d -> s h d")).then_inc(s_vc, 16)

            act.wait_ge(st_r, 1)
            act.dma_start(new_state[0, 0].rearrange("d (r p) -> (d r) p", p=P), st_rows[0:8, :]).then_inc(st_out, 16)

            norm(1)

            gate_in(1)

            def silu(k, count, buf):
                act.wait_ge(gu_ready[k], count + 1)
                act.activation(buf[0], ps[:, 0, 0:SF], ACT.Silu).then_inc(silu_ok[k], 1)

            for j in range(STEPS):
                for k in range(TILES):
                    silu(k, j, ffn_buf)
            norm(2)
            gate_in(2)

            for n in range(16):
                if n % 2:
                    act.wait_ge(qk_ps, n + 1)
                    m = n % 8
                    if n < 8:
                        act.activation(kk_t[:, m, :], ps[:, n % 6, 0:W], ACT.Copy).then_inc(qk_ok, 1)
                    else:
                        act.activation(q_t[:, m, 0:P], ps[:, n % 6, 0:P], ACT.Copy, scale=HD ** -0.5)
                        act.activation(by_tile(q_t[:, m, S0:W]), reverse(ps[:, n % 6, S0:W]), ACT.Copy,
                                       scale=HD ** -0.5).then_inc(qk_ok, 1)
            for n in range(6):
                if n % 2:
                    act.wait_ge(v_ps, n + 1)
                    f, t = n // 3, n % 3
                    act.activation(v_tok[:, t, f * 512:(f + 1) * 512], ps[:, n, :], ACT.Copy).then_inc(v_ok, 1)
            act.wait_ge(v_ok, 3)
            act.wait_ge(v_dve_ok, 3)
            act.dma_start(new_v[0, 0].rearrange("h s d -> s h d"),
                          v_tok[:, 0, :].rearrange("p (h d) -> p h d", h=HEADS)).then_inc(st_kv, 16)
            act.wait_ge(kt_ok, 1)
            act.dma_start(new_k[0, 0].rearrange("h s d -> s h d"),
                          k_out.rearrange("p (h d) -> p h d", h=HEADS)).then_inc(st_kv, 16)

            act.wait_ge(ctx_t, 1)
            act.wait_ge(st_out, 16)
            act.activation(kc_t[:, 4:8, :], ps[:, 7, :].rearrange("p (a b) -> p a b", a=4), ACT.Copy).then_inc(ctx_ok, 1)
            for u, (t, h) in enumerate(units):
                n = 384 if t else P
                act.wait_ge(max_ok, u + 1)
                if u >= 2:
                    act.wait_ge(pt_ps, u - 1)
                act.activation(p_buf[:, u % 2, 0:n], s_buf[:, u % 2, 0:n], ACT.Exp, bias=nmx[:, u % 2, :],
                               accum_out=sums[:, t, h:h + 1]).then_inc(p_ok, 1)
                if u >= 1:
                    tp, _ = units[u - 1]
                    np_ = 384 if tp else P
                    act.wait_ge(pt_ps, u)
                    if u >= 3:
                        act.wait_ge(pv, u - 2)
                    act.activation(pt_buf[:, (u - 1) % 2, 0:np_], ps[:, 2 + (u - 1) % 2, 0:np_], ACT.Copy)\
                        .then_inc(pt_ok, 1)
            u = len(units)
            act.wait_ge(pt_ps, u)
            act.wait_ge(pv, u - 2)
            act.activation(pt_buf[:, (u - 1) % 2, 0:P], ps[:, 2 + (u - 1) % 2, 0:P], ACT.Copy).then_inc(pt_ok, 1)
            for ci in range(KC):
                if ci % 2:
                    act.wait_ge(ot_ps, ci + 1)
                    act.activation(hn_t[:, ci, 0:T_PROMPT], ps[:, ci, 0:P], ACT.Copy)
                    act.activation(by_tile(hn_t[:, ci, S0:W]), reverse(ps[:, ci, P:384]), ACT.Copy).then_inc(ot_ok, 1)

            norm(3)
            for n in range(6):
                if n % 2:
                    act.wait_ge(hk_ps, n + 1)
                    t, hf = n // 2, n % 2
                    act.activation(xn_tok[:, t, hf * 512:(hf + 1) * 512], ps[:, n, :], ACT.Copy).then_inc(hk_ok, 1)
                    act.wait_ge(hk_ok, t + 1)
                    act.wait_ge(hk_dve, t + 1)
                    act.dma_start(hn_rows[t * P:(t + 1) * P, :], xn_tok[:, t, :]).then_inc(hk_st, 16)
            act.wait_ge(st_kv, 32)
            act.dma_start(fin_b, final_g.partition_broadcast(P)).then_inc(s_fin, 16)
            act.wait_ge(top_ok, 1)
            act.activation(dv, dv, ACT.Exp).then_inc(exp_v, 1)
            gate_in(3)

            act.wait_ge(route_ok, 1)
            rounds = act.value_load(over[0:1, 20:21], min_val=EXPERTS, max_val=2 * EXPERTS)

            def turned_in(k, count):
                act.wait_ge(xg_turned[k], count)
                act.activation(xg_t[k][:, 4:8, :], ps[:, 7, :].rearrange("p (a b) -> p a b", a=4), ACT.Copy)\
                    .then_inc(xgt_a[k], 1)

            turned_in(0, 1)
            act.wait_ge(y_zero, 16 * (EXPERTS + 1))
            for k in range(2):
                act.sem_inc(y_a[k], 1)
                act.sem_inc(y_st[k], 16)
            with act.Fori(0, rounds) as i:
                e = act.snap(i % EXPERTS, min_val=0, max_val=EXPERTS - 1)
                row = act.snap(e * (P * TILES) + (i // EXPERTS) * (2 * P), min_val=0,
                               max_val=EXPERTS * P * TILES - P)
                more = act.value_load(over[0:1, bass.ds(i, 1)])

                def moe_round(ks):
                    if 1 in ks:
                        turned_in(1, i + 1)
                    for j in range(STEPS):
                        for k in ks:
                            silu(k, i * STEPS + (STEPS + j), moe_buf)
                    turned_in(0, i + 2)
                    for k in ks:
                        act.wait_ge(y_st[k], i * 16 + 16)
                        act.wait_ge(done[k], i + 1)
                        act.activation(y_out[k][:, 512:1024], ps[:, 3 + 2 * k, :], ACT.Copy).then_inc(y_a[k], 1)
                    for k in ks:
                        act.wait_ge(y_a[k], i + 2)
                        act.wait_ge(y_d[k], i + 2)
                        act.dma_start(y_rows[bass.ds(row + P * k, P), :], y_out[k]).then_inc(y_st[k], 16)

                with act.If(more > 0):
                    moe_round((0, 1))
                with act.Else():
                    moe_round((0,))
                    act.sem_inc(xgt_a[1], 1)
                    act.sem_inc(silu_ok[1], STEPS)
                    act.sem_inc(y_a[1], 1)
                    act.sem_inc(y_st[1], 16)
                act.nop()
            act.wait_ge(y_st[0], rounds * 16 + 16)
            act.wait_ge(y_st[1], rounds * 16 + 16)
            act.sem_inc(rounds_over, 1)
            norm(4)
            for t in range(TILES):
                act.wait_ge(y_fin, t + 1)
                dst = y_prompt[0] if t == 0 else y_sample[0, (t - 1) * P:t * P, :]
                act.dma_start(dst, xn_tok[:, t, :]).then_inc(st_y, 16)
            act.wait_ge(st_y, 16 * TILES)
            act.wait_ge(st_kv, 32)
            act.wait_ge(st_out, 16)

        @block.vector
        def _(dve):
            n_chain = [0]

            def ordered(ins):
                n_chain[0] += 1
                ins.then_inc(chain_d, 1)
                dve.wait_ge(chain_d, n_chain[0])

            def col(name, n):
                return cols[:, COL[name] + n:COL[name] + n + 1]

            def mod_in(a, b, used):
                dve.wait_ge(mod_used, used)
                dve.tensor_tensor(modv[:, a:b, :], ps[:, 7, 2 * a:2 * b].rearrange("p (m g) -> p m g", g=2),
                                  cols[:, a:b].unsqueeze(2).to_broadcast([P, b - a, 2]), ALU.add).then_inc(mod_ok, 1)

            def set_gains(n):
                base = (n // 2) * 48 + (n % 2) * 24 + 8
                name = ("norm1", "norm2")[n % 2]
                g0 = COL[name] + 8 * (n // 2)
                if n:
                    dve.wait_ge(hn_act, 4 * n)
                dve.scalar_tensor_tensor(out=gains[:, :, :], in0=modv[:, base:base + 8, :], scalar=1.0,
                                         in1=cols[:, g0:g0 + 8].unsqueeze(2).to_broadcast([P, 8, 2]),
                                         op0=ALU.add, op1=ALU.mult).then_inc(gains_ok, 1)

            def norm(n):
                if n < 4:
                    set_gains(n)
                dve.wait_ge(ssq_ok, TILES * (n + 1))
                st = stats[:, n, 0:3]
                dve.tensor_scalar(st, st, 1.0 / D, EPS, ALU.mult, ALU.add).then_inc(var_ok, 1)
                dve.wait_ge(std_ok, n + 1)
                ordered(dve.reciprocal(st, st))
                if n == 4:
                    return
                for t in range(TILES):
                    dve.tensor_scalar(xn_tok[:, t, :], x[:, t, :], stats[:, n, t:t + 1], None, ALU.mult).then_inc(xn_ok, 1)
                base = (n // 2) * 48 + (n % 2) * 24
                dve.wait_ge(gains_ok, n + 1)
                for ci in range(0, KC, 2):
                    dve.wait_ge(nt_done, n * KC + ci + 1)
                    for g, (lo, hi, plo) in enumerate(((0, T_PROMPT, 0), (S0, W, P))):
                        ins = dve.tensor_scalar(hn_t[:, ci, lo:hi], ps[:, ci, plo:plo + hi - lo],
                                                gains[:, ci, g:g + 1], modv[:, base + ci, g:g + 1], ALU.mult, ALU.add)
                    ins.then_inc(hn_dve, 1)

            def gate_diagonals(n, m):
                for g in range(2):
                    if n:
                        dve.wait_ge(gb_ps, 4 * n)
                    else:
                        dve.wait_ge(mod_used, 48)
                    dve.tensor_tensor(diag[:, g], ident.unsqueeze(1).to_broadcast([P, KC, P]),
                                      modv[:, m:m + 8, g:g + 1].to_broadcast([P, KC, P]), ALU.mult).then_inc(diag_ok, 1)

            def residual(n, bank):
                dve.wait_ge(gb_ok, 4 * (n + 1))
                for t in range(TILES):
                    dve.wait_ge(out_ps, n * TILES + t + 1)
                    for hf in range(2):
                        lo, hi = hf * 512, hf * 512 + 512
                        b = ps[:, bank(t, hf), :]
                        dve.tensor_tensor(b, b, gate_b[:, min(t, 1), lo:hi], ALU.mult).then_inc(chain_d, 1)
                        n_chain[0] += 1
                    dve.wait_ge(chain_d, n_chain[0])
                    for hf in range(2):
                        lo, hi = hf * 512, hf * 512 + 512
                        ins = dve.tensor_tensor(x[:, t, lo:hi], x[:, t, lo:hi], ps[:, bank(t, hf), :], ALU.add)
                        if hf == 0:
                            n_chain[0] += 1
                            ins.then_inc(chain_d, 1)
                        else:
                            ins.then_inc(res_ok, 1)

            dve.wait_ge(vec_t, 2)
            dve.tensor_copy(cols[:, 0:P + ROWS_B], ps[:, 0, 0:P + ROWS_B]).then_inc(cols_ok, 1)
            dve.wait_ge(cols_ok, 1)

            lam = cols[:, COL["lam"]:COL["lam"] + 2 * LC]
            ordered(dve.scalar_tensor_tensor(out=lamz, in0=lam, scalar=-1.0, in1=lam, op0=ALU.mult, op1=ALU.min))
            dve.tensor_scalar(lamp, lam, -1.0, 0.0, ALU.mult, ALU.max).then_inc(lam_e, 1)
            mod_in(0, 16, 8)
            dve.wait_ge(mod_ok, 1)
            dve.wait_ge(s_x, 32)
            norm(0)
            dve.wait_ge(lam_e, 2)
            ordered(dve.tensor_scalar(lamk, lamz, 2.0, None, ALU.add))
            ordered(dve.reciprocal(lamk, lamk))
            ordered(dve.tensor_tensor(lamz, lamz, lamk, ALU.mult))
            zz, acc = small[:, 0:8], small[:, 8:16]
            ordered(dve.tensor_tensor(zz, lamz, lamz, ALU.mult))
            ordered(dve.tensor_scalar(acc, zz, 1.0 / 17, 1.0 / 15, ALU.mult, ALU.add))
            for n in (13, 11, 9, 7, 5, 3, 1):
                ordered(dve.tensor_tensor(acc, acc, zz, ALU.mult))
                ordered(dve.tensor_scalar(acc, acc, 1.0 / n, None, ALU.add))
            ordered(dve.tensor_tensor(acc, acc, lamz, ALU.mult))
            ordered(dve.scalar_tensor_tensor(out=acc, in0=acc, scalar=2.0, in1=lamp, op0=ALU.mult, op1=ALU.add))
            dve.tensor_scalar(lamk, acc, -LRU_C, None, ALU.mult).then_inc(lam_ok, 1)

            dve.wait_ge(gap_ok, 3)
            for m in range(LC):
                n = first_item["x"] + m
                dve.wait_ge(pj, n + 1)
                dve.tensor_copy(xpad[:, m, 2:2 + W], ps[:, n % PB, 0:W]).then_inc(ev_d, 1)
                dve.wait_ge(ev_d, ev_n[n][1])
                ordered(dve.tensor_scalar(xc[:, m, :], xpad[:, m, 0:W], col("conv_w", m), col("conv_b", m),
                                          ALU.mult, ALU.add))
                for k in range(1, 4):
                    ins = dve.scalar_tensor_tensor(out=xc[:, m, :], in0=xpad[:, m, k:k + W],
                                                   scalar=col("conv_w", 4 * k + m), in1=xc[:, m, :],
                                                   op0=ALU.mult, op1=ALU.add)
                    if k < 3:
                        ordered(ins)
                ins.then_inc(xc_ok, 1)
            mod_in(16, 48, 24)
            dve.wait_ge(xc_ok, LC)
            for d in range(2):
                dve.wait_ge(tanh_ok, d + 1)
                ordered(dve.tensor_scalar(tmp, gr[d], -1.0, None, ALU.add))
                ordered(dve.reciprocal(tmp, tmp))
                dve.scalar_tensor_tensor(out=gr[d], in0=gr[d], scalar=2.0, in1=tmp,
                                         op0=ALU.mult, op1=ALU.mult).then_inc(m_ok, 1)
                ordered(dve.tensor_tensor(gi[d], gi[d], xc, ALU.mult))
                dve.wait_ge(root_ok, d + 1)
                ordered(dve.tensor_tensor(gi[d], gi[d], gr[d], ALU.mult))
                at_gap = S0 - 1 if d == 0 else T_PROMPT
                ordered(dve.memset(dec[:, :, at_gap:at_gap + 1], 0.0))
                if d == 0:
                    st0 = COL["state"]
                    ordered(dve.tensor_copy(gi[d][:, :, at_gap:at_gap + 1], cols[:, st0:st0 + LC].unsqueeze(2)))
                else:
                    ordered(dve.memset(gi[d][:, :, at_gap:at_gap + 1], 0.0))
                for m in range(LC):
                    if d == 0:
                        ins = dve.tensor_tensor_scan(gr[d][:, m, :], dec[:, m, :], gi[d][:, m, :], 0.0, ALU.mult, ALU.add)
                    else:
                        ins = dve.tensor_tensor_scan(gr[d][:, m, ::-1], dec[:, m, ::-1], gi[d][:, m, ::-1],
                                                     col("state", LC + m), ALU.mult, ALU.add)
                    ordered(ins)
                dve.sem_inc(mix_ok, 1)
            dve.tensor_copy(st8[:, 0:LC], gr[0][:, :, T_PROMPT - 1]).then_inc(st_ok, 1)
            dve.tensor_copy(st8[:, LC:2 * LC], gr[1][:, :, 0]).then_inc(st_ok, 1)
            ordered(dve.tensor_tensor(tmp, gr[0], gr[1], ALU.add))
            for m in range(LC):
                n = first_item["v"] + m
                dve.wait_ge(pj, n + 1)
                dve.wait_ge(ev_a, ev_n[first_item["c"] + m][1])
                dve.tensor_tensor(cvpad[:, m, 2:2 + W], cvpad[:, m, 2:2 + W], ps[:, n % PB, 0:W],
                                  ALU.mult).then_inc(ev_d, 1)
                dve.wait_ge(ev_d, ev_n[n][1])
                ordered(dve.tensor_scalar(sc_conv[:, m, :], cvpad[:, m, 1:1 + W], col("sc_w", m), col("sc_b", m),
                                          ALU.mult, ALU.add))
                for k in range(1, 3):
                    ordered(dve.scalar_tensor_tensor(out=sc_conv[:, m, :], in0=cvpad[:, m, 1 + k:1 + k + W],
                                                     scalar=col("sc_w", 4 * k + m), in1=sc_conv[:, m, :],
                                                     op0=ALU.mult, op1=ALU.add))
            dve.wait_ge(ev_a, ev_n[first_item["b"] + 3][1])
            ordered(dve.tensor_tensor(y_t[:, LC:KC, :], y_t[:, LC:KC, :], sc_conv, ALU.mult))
            dve.wait_ge(ev_a, ev_n[first_item["g"] + 3][1])
            dve.tensor_tensor(y_t[:, 0:LC, :], y_t[:, 0:LC, :], tmp, ALU.mult).then_inc(y_ok, 1)
            mod_in(48, 96, 48)
            dve.wait_ge(mod_ok, 3)
            gate_diagonals(0, 16)
            dve.wait_ge(st_t, 1)
            dve.tensor_copy(st_rows[0:8, :], ps[0:8, 7, 0:P]).then_inc(st_r, 1)
            residual(0, lambda t, hf: 3 * hf + t)

            norm(1)
            gate_diagonals(1, 40)

            def hidden(k, count, buf):
                dve.wait_ge(silu_ok[k], count + 1)
                dve.tensor_tensor(buf[1], buf[0], ps[:, 0, SF:2 * SF], ALU.mult).then_inc(h_ok[k], 1)
                dve.wait_ge(h_turned[k], count + 1)
                dve.tensor_copy(buf[2], ps[:, 1, 0:SF].rearrange("p (f t) -> p f t", f=2)).then_inc(ht_ok[k], 1)

            for j in range(STEPS):
                for k in range(TILES):
                    hidden(k, j, ffn_buf)
            residual(1, lambda t, hf: 2 + 2 * t + hf)

            norm(2)
            gate_diagonals(2, 48 + 16)
            for n in range(0, 16, 2):
                dve.wait_ge(qk_ps, n + 1)
                m = n % 8
                if n < 8:
                    dve.tensor_copy(kk_t[:, m, :], ps[:, n % 6, 0:W]).then_inc(qk_dve, 1)
                else:
                    dve.tensor_scalar(q_t[:, m, 0:P], ps[:, n % 6, 0:P], HD ** -0.5, None, ALU.mult)
                    dve.tensor_scalar(by_tile(q_t[:, m, S0:W]), reverse(ps[:, n % 6, S0:W]), HD ** -0.5, None,
                                      ALU.mult).then_inc(qk_dve, 1)
            dve.wait_ge(kt_ps, 1)
            dve.tensor_copy(k_out, ps[:, 6:8, :].rearrange("p a b -> p (a b)")).then_inc(kt_ok, 1)
            for n in range(0, 6, 2):
                dve.wait_ge(v_ps, n + 1)
                f, t = n // 3, n % 3
                dve.tensor_copy(v_tok[:, t, f * 512:(f + 1) * 512], ps[:, n, :]).then_inc(v_dve_ok, 1)
            dve.wait_ge(ctx_t, 1)
            dve.tensor_copy(kc_t[:, 0:4, :], ps[:, 6, :].rearrange("p (a b) -> p a b", a=4)).then_inc(ctx_d, 1)

            dve.wait_ge(bias_ok, 1)
            for u, (t, h) in enumerate(units):
                n = 384 if t else P
                dve.wait_ge(sc_ps, u + 1)
                if u >= 2:
                    dve.wait_ge(p_ok, u - 1)
                if t:
                    j0 = 6 * h + 2 - 2 * (t - 1)
                    dve.tensor_tensor(s_buf[:, u % 2, 0:256].rearrange("p (a b) -> p a b", a=4),
                                      ps[:, u % 2, 0:256].rearrange("p (a b) -> p a b", a=4),
                                      bias[:, j0:j0 + 4, :], ALU.add).then_inc(s_ok, 1)
                    dve.tensor_copy(s_buf[:, u % 2, 256:384], ps[:, u % 2, 256:384]).then_inc(s_ok, 1)
                else:
                    dve.sem_inc(s_ok, 1)
                    dve.tensor_copy(s_buf[:, u % 2, 0:P], ps[:, u % 2, 0:P]).then_inc(s_ok, 1)
                dve.wait_ge(s_ok, 2 * u + 2)
                ordered(dve.tensor_reduce(mx[:, u % 2, :], s_buf[:, u % 2, 0:n], AX_X, ALU.max))
                dve.tensor_scalar(nmx[:, u % 2, :], mx[:, u % 2, :], -1.0, None, ALU.mult).then_inc(max_ok, 1)
                for ti, tt in enumerate((1, 2)):
                    if u == HEADS * (ti + 1) + 4:
                        dve.wait_ge(p_ok, HEADS * (ti + 1))
                        ordered(dve.reciprocal(sums[:, tt, :], sums[:, tt, :]))
                        dve.wait_ge(pv, HEADS * (ti + 1))
                        dve.wait_ge(st_kv, 32)
                        dve.tensor_tensor(xn_tok[:, tt, :].rearrange("p (h d) -> p h d", h=HEADS),
                                          ps[:, 4 + 2 * ti:6 + 2 * ti, :].rearrange("p a (h d) -> p (a h) d", d=HD),
                                          sums[:, tt, :].unsqueeze(2).to_broadcast([P, HEADS, HD]),
                                          ALU.mult).then_inc(o_ok, 1)
            dve.wait_ge(p_ok, len(units))
            ordered(dve.reciprocal(sums[:, 0, :], sums[:, 0, :]))
            dve.wait_ge(pv, len(units))
            dve.tensor_tensor(xn_tok[:, 0, :].rearrange("p (h d) -> p h d", h=HEADS),
                              ps[:, 4:6, :].rearrange("p a (h d) -> p (a h) d", d=HD),
                              sums[:, 0, :].unsqueeze(2).to_broadcast([P, HEADS, HD]), ALU.mult).then_inc(o_ok, 1)
            for ci in range(0, KC, 2):
                dve.wait_ge(ot_ps, ci + 1)
                dve.tensor_copy(hn_t[:, ci, 0:T_PROMPT], ps[:, ci, 0:P])
                dve.tensor_copy(by_tile(hn_t[:, ci, S0:W]), reverse(ps[:, ci, P:384])).then_inc(ot_d, 1)
            residual(2, lambda t, hf: 3 * hf + t)

            norm(3)
            for n in range(0, 6, 2):
                dve.wait_ge(hk_ps, n + 1)
                t, hf = n // 2, n % 2
                dve.tensor_copy(xn_tok[:, t, hf * 512:(hf + 1) * 512], ps[:, n, :]).then_inc(hk_dve, 1)

            dve.wait_ge(lg_ps, 1)
            dve.wait_ge(st_kv, 32)
            ordered(dve.tensor_copy(lg, ps[:, 6, 0:24].rearrange("p (t e) -> p t e", t=TILES)))
            for t in range(TILES):
                ordered(dve.max(m8[:, t, :], lg[:, t, :]))
                ordered(dve.max_index(i8[:, t, :], m8[:, t, :], lg[:, t, :]))
            dve.tensor_tensor(dv, m8[:, :, 1], m8[:, :, 0], ALU.subtract).then_inc(top_ok, 1)
            experts = k_sb[:, C_EXP:C_EXP + 8].unsqueeze(1).to_broadcast([P, TILES, EXPERTS])
            for k, oh in enumerate((oh1, oh2)):
                ordered(dve.tensor_copy(e12[:, k, :], i8[:, :, k]))
                ordered(dve.tensor_tensor(oh, experts, e12[:, k, :].unsqueeze(2).to_broadcast([P, TILES, EXPERTS]),
                                          ALU.is_equal))
            dve.tensor_tensor(mask, oh1, oh2, ALU.add).then_inc(mask_ok, 1)
            dve.wait_ge(rk_ps, 1)
            ordered(dve.tensor_copy(rank, ps[:, 7, 0:24].rearrange("p (t e) -> p t e", t=TILES)))
            dve.tensor_copy(cnt_f, ps[:, 7, 24:32]).then_inc(rk_ok, 1)
            ordered(dve.scalar_tensor_tensor(out=rankm, in0=rank, scalar=1.0, in1=mask, op0=ALU.add, op1=ALU.mult))
            ordered(dve.tensor_scalar(rankm, rankm, -1.0, None, ALU.add))
            for e in range(EXPERTS):
                if e >= 2:
                    dve.wait_ge(hot_used, e - 1)
                for t in range(TILES):
                    dve.tensor_scalar(slot_hot[:, e % 2, t, :], k_sb[:, C_IOTA:C_IOTA + 384], rankm[:, t, e:e + 1],
                                      None, ALU.is_equal).then_inc(hot_ok, 1)
            rows_e = k_sb[:, C_ROW:C_ROW + 8].unsqueeze(1).to_broadcast([P, TILES, EXPERTS])
            ordered(dve.tensor_tensor(rk_e, rank, rows_e, ALU.add))
            for k, oh in enumerate((oh1, oh2)):
                ordered(dve.tensor_tensor(pick, oh, rk_e, ALU.mult))
                ordered(dve.tensor_reduce(pos_f[:, k, :], pick, AX_X, ALU.add))
            ordered(dve.tensor_copy(pos_i[:, :], pos_f.rearrange("p k t -> p (k t)")))
            dve.wait_ge(exp_v, 1)
            ordered(dve.tensor_scalar(w12[:, 0, :], dv, 1.0, None, ALU.add))
            ordered(dve.reciprocal(w12[:, 0, :], w12[:, 0, :]))
            ordered(dve.tensor_tensor(w12[:, 1, :], w12[:, 0, :], dv, ALU.mult))
            dve.wait_ge(rk_ok, 1)
            ordered(dve.tensor_reduce(small[:, 16:17], cnt_f, AX_X, ALU.max))
            ordered(dve.tensor_scalar(small[:, 17:18], small[:, 16:17], 256.5, 8.0, ALU.is_gt, ALU.mult))
            ordered(dve.tensor_scalar(small[:, 18:19], small[:, 17:18], 8.0, None, ALU.add))
            ordered(dve.memset(over[:, :], 0))
            ordered(dve.tensor_scalar(over[0:1, 0:8], cnt_f[0:1, :], -128.0, None, ALU.add))
            ordered(dve.tensor_copy(over[0:1, 20:21], small[0:1, 18:19]))
            ordered(dve.memset(idx_a[:, :], 0))
            ordered(dve.memset(idx_b[:, :], 0))
            dve.wait_ge(hot_used, EXPERTS)
            ordered(dve.tensor_copy(idx_f, ps[:, 7, 64:88]))
            by_chunk = idx_f.rearrange("p (e c) -> p e c", c=TILES)
            ordered(dve.tensor_copy(idx_a[:, 0:8], by_chunk[:, :, 0]))
            ordered(dve.tensor_copy(idx_a[:, 8:16], by_chunk[:, :, 2]))
            ordered(dve.tensor_copy(idx_b[:, 0:8], by_chunk[:, :, 1]))
            dve.sem_inc(route_ok, 1)
            gate_diagonals(3, 48 + 40)

            rounds = dve.value_load(over[0:1, 20:21], min_val=EXPERTS, max_val=2 * EXPERTS)

            def turned_in(k, count):
                dve.wait_ge(xg_turned[k], count)
                dve.tensor_copy(xg_t[k][:, 0:4, :], ps[:, 6, :].rearrange("p (a b) -> p a b", a=4)).then_inc(xgt_d[k], 1)

            turned_in(0, 1)
            for k in range(2):
                dve.sem_inc(y_d[k], 1)
            with dve.Fori(0, rounds) as i:
                more = dve.value_load(over[0:1, bass.ds(i, 1)])

                def moe_round(ks):
                    if 1 in ks:
                        turned_in(1, i + 1)
                    for j in range(STEPS):
                        for k in ks:
                            hidden(k, i * STEPS + (STEPS + j), moe_buf)
                    turned_in(0, i + 2)
                    for k in ks:
                        dve.wait_ge(y_st[k], i * 16 + 16)
                        dve.wait_ge(done[k], i + 1)
                        dve.tensor_copy(y_out[k][:, 0:512], ps[:, 2 + 2 * k, :]).then_inc(y_d[k], 1)

                with dve.If(more > 0):
                    moe_round((0, 1))
                with dve.Else():
                    moe_round((0,))
                    dve.sem_inc(xgt_d[1], 1)
                    dve.sem_inc(h_ok[1], STEPS)
                    dve.sem_inc(ht_ok[1], STEPS)
                    dve.sem_inc(y_d[1], 1)
                dve.nop()

            dve.wait_ge(gb_ok, 16)
            dve.wait_ge(collected, 16 * 2 * TILES)
            for t in range(TILES):
                a, b = got[0][:, t, :], got[1][:, t, :]
                ordered(dve.tensor_scalar(a, a, w12[:, 0, t:t + 1], None, ALU.mult))
                ordered(dve.scalar_tensor_tensor(out=a, in0=b, scalar=w12[:, 1, t:t + 1], in1=a,
                                                 op0=ALU.mult, op1=ALU.add))
                ordered(dve.tensor_tensor(a, a, gate_b[:, min(t, 1), :], ALU.mult))
                dve.tensor_tensor(x[:, t, :], x[:, t, :], a, ALU.add).then_inc(res_ok, 1)
            dve.wait_ge(res_ok, 4 * TILES)
            norm(4)
            dve.wait_ge(s_fin, 16)
            for t in range(TILES):
                dve.scalar_tensor_tensor(out=xn_tok[:, t, :], in0=x[:, t, :], scalar=stats[:, 4, t:t + 1], in1=fin_b,
                                         op0=ALU.mult, op1=ALU.mult).then_inc(y_fin, 1)

        @block.tensor
        def _(pe):
            def turn(dst, src):
                return pe.transpose(dst, src, ident[0:src.shape[0], 0:src.shape[0]])

            def norm(n):
                pe.wait_ge(xn_ok, TILES * (n + 1))
                for ci in range(KC):
                    for t in range(TILES):
                        ins = turn(ps[:, ci, t * P:(t + 1) * P], xn_tok[:, t, ci * P:(ci + 1) * P])
                    ins.then_inc(nt_done, 1)

            def hn_ready(n):
                pe.wait_ge(hn_dve, 4 * (n + 1))
                pe.wait_ge(hn_act, 4 * (n + 1))

            def spread(n):
                for g in range(2):
                    pe.wait_ge(diag_ok, 2 * n + g + 1)
                    for hf in range(2):
                        pe.matmul(ps[:, 6 - 2 * g + hf, :], ones, diag[:, g, 4 * hf:4 * hf + 4, :],
                                  start=True, stop=True).then_inc(gb_ps, 1)

            def mod_groups(lo, hi):
                with pe.Fori(lo, hi) as g:
                    for s in range(4):
                        pe.wait_ge(mod_full[s], g * 16 + 16)
                        wt = mod_slot(s).rearrange("p (k f) -> p k f", k=KC)
                        for b in range(2):
                            out = ps[:, 7, bass.ds(g * 16 + (4 * s + 2 * b), 2)]
                            for k in range(KC):
                                ins = pe.matmul(out, wt[:, k, b * P:(b + 1) * P], cond[:, k, :],
                                                start=(k == 0), stop=(k == KC - 1))
                        ins.then_inc(mod_used, 1)

            def full(n):
                pe.wait_ge(ring_full[slot_of(n)], filled(n))

            pe.wait_ge(s_const, 16)
            pe.wait_ge(s_vec, 16 * 13)
            turn(ps[:, 0, 0:P], vec_rows[:, 0, :]).then_inc(vec_t, 1)
            turn(ps[:, 0, P:P + ROWS_B], vec_rows[0:ROWS_B, 1, :]).then_inc(vec_t, 1)
            pe.wait_ge(cond_ok, 2)
            mod_groups(0, 2)
            pe.wait_ge(mod_ok, 1)
            norm(0)
            hn_ready(0)
            pe.wait_ge(gap_ok, 3)

            fill_n = {"x": 0, "c": 1, "v": 2, "b": 3, "g": 4}
            after = {"x": (2, 4), "c": (4, 6), "v": (6, 8), "b": (8, 10), "g": (10, 12)}
            for n, (kind, m, eng) in enumerate(items):
                if n >= PB:
                    pe.wait_ge(*ev_n[n - PB])
                if kind == "gate":
                    if n == first_item["gate"]:
                        pe.wait_ge(s_bd, 16 * 8)
                    pe.wait_ge(xc_ok, m % 4 + 1)
                    pe.matmul(ps[:, n % PB, 0:W], bd[:, m, :], xc[:, m % 4, :], start=True, stop=True).then_inc(pj, 1)
                    continue
                f = fill_n[kind]
                if m == 0:
                    full(F_IN + f)
                for k in range(KC):
                    ins = pe.matmul(ps[:, n % PB, 0:W], slab(F_IN + f)[:, k, m * P:(m + 1) * P], hn_t[:, k, :],
                                    start=(k == 0), stop=(k == KC - 1))
                ins.then_inc(pj, 1)
                if m == 3:
                    lo, hi = after[kind]
                    if lo == 6:
                        pe.wait_ge(mod_ok, 2)
                    mod_groups(lo, hi)

            def product(n_sub, base_fill, lhs, bank):
                for f in range(2):
                    n = base_fill + f
                    full(n)
                    for t in range(TILES):
                        for k in range(KC):
                            ins = pe.matmul(ps[:, bank(t, f), :], lhs[:, k, TOK[t]:TOK[t] + P], slab(n)[:, k, :],
                                            start=(k == 0), stop=(k == KC - 1))
                        if f == 1:
                            ins.then_inc(out_ps, 1)
                    if f == 0:
                        ins.then_inc(ring_free[slot_of(n)], 1)

            pe.wait_ge(mod_ok, 3)
            pe.wait_ge(ev_a, ev_n[-1][1])
            spread(0)
            pe.wait_ge(st_ok, 2)
            pe.wait_ge(gb_ok, 2)
            turn(ps[0:8, 7, 0:P], st8).then_inc(st_t, 1)
            pe.wait_ge(y_ok, 1)
            pe.wait_ge(gb_ok, 4)
            product(0, F_OUT, y_t, lambda t, f: 3 * f + t)

            def gate_up(s, xt, k, wait):
                g_s, u_s, _ = ff_slot(s)
                for half, wt in enumerate((g_s, u_s)):
                    for c_ in range(KC):
                        ins = pe.matmul(ps[:, 0, half * SF:(half + 1) * SF], xt(c_), wt[:, c_, :],
                                        start=(c_ == 0), stop=(c_ == KC - 1))
                ins.then_inc(gu_ready[k], 1)

            def turn_hidden(k, count, buf):
                pe.wait_ge(h_ok[k], count + 1)
                for f in range(2):
                    ins = turn(ps[:, 1, f * P:(f + 1) * P], buf[1][:, f * P:(f + 1) * P])
                ins.then_inc(h_turned[k], 1)

            def down(s, j, k, count, buf):
                pe.wait_ge(ht_ok[k], count + 1)
                d_s = ff_slot(s)[2]
                for f in range(2):
                    for hf in range(2):
                        ins = pe.matmul(ps[:, 2 + 2 * k + hf, :], buf[2][:, f, :], d_s[:, f, hf * 512:(hf + 1) * 512],
                                        start=(j == 0 and f == 0), stop=(j == STEPS - 1 and f == 1))
                return ins

            norm(1)
            hn_ready(1)
            spread(1)
            todo = [(j, k) for j in range(STEPS) for k in range(TILES)]
            for u in range(len(todo) + 1):
                if u:
                    pj_, pk = todo[u - 1]
                    turn_hidden(pk, pj_, ffn_buf)
                if u < len(todo):
                    j, k = todo[u]
                    if k == 0:
                        full(F_FFN + j)
                    gate_up(slot_of(F_FFN + j), lambda c_: hn_t[:, c_, TOK[k]:TOK[k] + P], k, None)
                if u:
                    if pj_ == 0 and pk:
                        pe.wait_ge(gb_ok, 8)
                    ins = down(slot_of(F_FFN + pj_), pj_, pk, pj_, ffn_buf)
                    if pj_ == STEPS - 1:
                        ins.then_inc(out_ps, 1)
                    elif pk == TILES - 1:
                        ins.then_inc(ring_free[slot_of(F_FFN + pj_)], 1)

            norm(2)
            hn_ready(2)
            spread(2)
            for n in range(16):
                f, m = n // 4, n % 4
                if m == 0:
                    full(F_QKV + f)
                if n in (4, 5):
                    pe.wait_ge(gb_ok, 12)
                if n >= 6:
                    pe.wait_ge((qk_dve, qk_ok)[n % 2], (n - 6) // 2 + 1)
                for k in range(KC):
                    ins = pe.matmul(ps[:, n % 6, 0:W], slab(F_QKV + f)[:, k, m * P:(m + 1) * P], hn_t[:, k, :],
                                    start=(k == 0), stop=(k == KC - 1))
                ins.then_inc(qk_ps, 1)
            pe.wait_ge(qk_dve, 8)
            pe.wait_ge(qk_ok, 8)
            pe.wait_ge(gb_ok, 12)
            for k in range(KC):
                ins = turn(ps[:, 6 + k // 4, (k % 4) * P:(k % 4 + 1) * P], kk_t[:, k, 0:P])
            ins.then_inc(kt_ps, 1)
            for n in range(6):
                f, t = n // 3, n % 3
                if t == 0:
                    full(F_QKV + 4 + f)
                for k in range(KC):
                    ins = pe.matmul(ps[:, n, :], hn_t[:, k, TOK[t]:TOK[t] + P], slab(F_QKV + 4 + f)[:, k, :],
                                    start=(k == 0), stop=(k == KC - 1))
                ins.then_inc(v_ps, 1)
            pe.wait_ge(kt_ok, 1)
            pe.wait_ge(s_cache, 16)
            for k in range(KC):
                ins = turn(ps[:, 6 + k // 4, (k % 4) * P:(k % 4 + 1) * P], kc_tok[:, k * P:(k + 1) * P])
            ins.then_inc(ctx_t, 1)
            pe.wait_ge(ctx_d, 1)
            pe.wait_ge(ctx_ok, 1)
            pe.wait_ge(v_dve_ok, 3)
            pe.wait_ge(v_ok, 3)
            pe.wait_ge(s_vc, 16)

            n_units = len(units)
            for u in range(n_units + 2):
                if u < n_units:
                    t, h = units[u]
                    r, ci = 64 * (h % 2), h // 2
                    if u >= 2:
                        pe.wait_ge(s_ok, 2 * (u - 1))
                    q = q_t[r:r + 64, ci, TOK[t]:TOK[t] + P]
                    if t:
                        pe.matmul(ps[:, u % 2, 0:256], q, kk_t[r:r + 64, ci, S0:W], start=True, stop=True)
                        ins = pe.matmul(ps[:, u % 2, 256:384], q, kc_t[r:r + 64, ci, :], start=True, stop=True)
                    else:
                        ins = pe.matmul(ps[:, u % 2, 0:P], q, kk_t[r:r + 64, ci, 0:P], start=True, stop=True)
                    ins.then_inc(sc_ps, 1)
                if 1 <= u <= n_units:
                    w_ = u - 1
                    tp = units[w_][0]
                    pe.wait_ge(p_ok, w_ + 1)
                    if w_ >= 2:
                        pe.wait_ge(pt_ok, w_ - 1)
                    for b in range(3 if tp else 1):
                        ins = turn(ps[:, 2 + w_ % 2, b * P:(b + 1) * P], p_buf[:, w_ % 2, b * P:(b + 1) * P])
                    ins.then_inc(pt_ps, 1)
                if u >= 2:
                    w_ = u - 2
                    tp, hp = units[w_]
                    ti = w_ // HEADS
                    if ti == 2 and hp == 0:
                        pe.wait_ge(o_ok, 1)
                    pe.wait_ge(pt_ok, w_ + 1)
                    vs = [v_tok[:, 1, :], v_tok[:, 2, :], vc] if tp else [v_tok[:, 0, :]]
                    b0 = 4 + 2 * (ti % 2) + hp // 8
                    for b, vv in enumerate(vs):
                        ins = pe.matmul(ps[:, b0, (hp % 8) * HD:(hp % 8 + 1) * HD], pt_buf[:, w_ % 2, b * P:(b + 1) * P],
                                        vv[:, hp * HD:(hp + 1) * HD], start=(b == 0), stop=(b == len(vs) - 1))
                    ins.then_inc(pv, 1)
            pe.wait_ge(o_ok, 3)
            for ci in range(KC):
                for t in range(TILES):
                    ins = turn(ps[:, ci, t * P:(t + 1) * P], xn_tok[:, t, ci * P:(ci + 1) * P])
                ins.then_inc(ot_ps, 1)
            pe.wait_ge(ot_d, 4)
            pe.wait_ge(ot_ok, 4)
            product(2, F_O, hn_t, lambda t, f: 3 * f + t)

            norm(3)
            hn_ready(3)
            pe.wait_ge(s_router, 16)
            for t in range(TILES):
                for k in range(KC):
                    ins = pe.matmul(ps[:, 6, t * 8:(t + 1) * 8], hn_t[:, k, TOK[t]:TOK[t] + P], router[:, k, :],
                                    start=(k == 0), stop=(k == KC - 1))
            ins.then_inc(lg_ps, 1)
            for n in range(6):
                t, hf = n // 2, n % 2
                for k in range(4):
                    ins = turn(ps[:, n, k * P:(k + 1) * P], hn_t[:, 4 * hf + k, TOK[t]:TOK[t] + P])
                ins.then_inc(hk_ps, 1)
            pe.wait_ge(mask_ok, 1)
            for t in range(TILES):
                for b in range(t + 1):
                    pe.matmul(ps[:, 7, t * 8:(t + 1) * 8], before if b == t else ones, mask[:, b, :],
                              start=(b == 0), stop=(b == t))
            for b in range(TILES):
                ins = pe.matmul(ps[:, 7, 24:32], ones, mask[:, b, :], start=(b == 0), stop=(b == TILES - 1))
            ins.then_inc(rk_ps, 1)
            pe.wait_ge(rk_ok, 1)
            for e in range(EXPERTS):
                pe.wait_ge(hot_ok, TILES * (e + 1))
                for ch in range(TILES):
                    for t in range(TILES):
                        ins = pe.matmul(ps[:, 7, 64 + TILES * e + ch:65 + TILES * e + ch],
                                        slot_hot[:, e % 2, t, ch * P:(ch + 1) * P], k_sb[:, C_TOKEN + t:C_TOKEN + t + 1],
                                        start=(t == 0), stop=(t == TILES - 1))
                ins.then_inc(hot_used, 1)
            pe.wait_ge(hk_dve, 3)
            pe.wait_ge(hk_ok, 3)
            pe.wait_ge(route_ok, 1)
            spread(3)
            pe.wait_ge(gb_ok, 16)

            def turn_gathered(k, count):
                pe.wait_ge(gathered[k], count)
                for c_ in range(KC):
                    ins = turn(ps[:, 6 + c_ // 4, (c_ % 4) * P:(c_ % 4 + 1) * P], xg[k][:, c_ * P:(c_ + 1) * P])
                ins.then_inc(xg_turned[k], 1)

            turn_gathered(0, 16)
            rounds = pe.value_load(over[0:1, 20:21], min_val=EXPERTS, max_val=2 * EXPERTS)
            with pe.Fori(0, rounds) as i:
                more = pe.value_load(over[0:1, bass.ds(i, 1)])

                def moe_round(ks):
                    pe.wait_ge(xgt_d[0], i + 1)
                    pe.wait_ge(xgt_a[0], i + 1)
                    if 1 in ks:
                        turn_gathered(1, i * 16 + 16)
                    todo = [(j, k) for j in range(STEPS) for k in ks]
                    for u in range(len(todo) + 1):
                        if u:
                            pj_, pk = todo[u - 1]
                            turn_hidden(pk, i * STEPS + (STEPS + pj_), moe_buf)
                        if u < len(todo):
                            j, k = todo[u]
                            s = moe_slot(j)
                            if k == 0:
                                pe.wait_ge(ring_full[s], i * (48 * PER[s]) + (BASE_FULL[s] + 48 * (nth(j) + 1)))
                            elif j == 0:
                                pe.wait_ge(xgt_d[1], i + 1)
                                pe.wait_ge(xgt_a[1], i + 1)
                            gate_up(s, lambda c_: xg_t[k][:, c_, :], k, None)
                        if u:
                            if pj_ == 0:
                                pe.wait_ge(y_d[pk], i + 1)
                                pe.wait_ge(y_a[pk], i + 1)
                            ins = down(moe_slot(pj_), pj_, pk, i * STEPS + (STEPS + pj_), moe_buf)
                            if pj_ == STEPS - 1:
                                ins.then_inc(done[pk], 1)
                            elif pk == ks[-1]:
                                ins.then_inc(ring_free[moe_slot(pj_)], 1)
                            if pj_ == 5 and pk == ks[-1]:
                                turn_gathered(0, i * 16 + 32)

                with pe.If(more > 0):
                    moe_round((0, 1))
                with pe.Else():
                    moe_round((0,))
                    pe.sem_inc(xg_turned[1], 1)
                    pe.sem_inc(gu_ready[1], STEPS)
                    pe.sem_inc(h_turned[1], STEPS)
                    pe.sem_inc(done[1], 1)
                pe.nop()


_INS = ['x_prompt', 'x_sample', 'state_lru', 'cache_k', 'cache_v', 'c', 'c_ctx', 'norm1_g', 'norm2_g', 'w_mod', 'b_mod',
        'w_in', 'lru_conv_w', 'lru_conv_b', 'lru_wa', 'lru_ba', 'lru_wx', 'lru_bx', 'lru_lam', 'sc_conv_w', 'sc_conv_b',
        'w_out', 'ffn_w_gate', 'ffn_w_up', 'ffn_w_down', 'w_qkv', 'w_o', 'rpb', 'w_router', 'moe_w_gate', 'moe_w_up',
        'moe_w_down', 'final_g']
_OUTS = [(1, 128, 1024), (1, 256, 1024), (1, 1, 2, 512), (1, 1, 16, 128, 64), (1, 1, 16, 128, 64)]


def kernel(**inputs):
    import concourse.bacc as _bacc
    from concourse.bass_utils import run_bass_kernel_spmd as _run

    nc = _bacc.Bacc("TRN2", target_bir_lowering=False, num_devices=1)
    arrays = {"shape_constants_dram": shape_constants()}
    args = [nc.dram_tensor("shape_constants_dram", (P, N_CONST), F32, kind="ExternalInput").ap()]
    for name in _INS:
        a = np.ascontiguousarray(inputs[name])
        arrays[f"in_{name}_dram"] = a
        args.append(nc.dram_tensor(f"in_{name}_dram", a.shape, mybir.dt.from_np(a.dtype), kind="ExternalInput").ap())
    for i, shape in enumerate(_OUTS):
        args.append(nc.dram_tensor(f"out_{i}_dram", shape, F32, kind="ExternalOutput").ap())
    hybrid_step(nc, *args)
    r = _run(nc, [arrays], core_ids=[0])
    return tuple(r.results[0][f"out_{i}_dram"] for i in range(len(_OUTS)))
```

```python
from contextlib import ExitStack

import numpy as np
import concourse.bass as bass
from concourse import mybir

F32 = mybir.dt.float32
F32R = mybir.dt.float32r
I32 = mybir.dt.int32
U32 = mybir.dt.uint32
ALU = mybir.AluOpType
ACT = mybir.ActivationFunctionType
AX_X = mybir.AxisListType.X

P = 128
D = 1024
KC = D // P
T_PROMPT, T_SAMPLE = 128, 256
TILES = (T_PROMPT + T_SAMPLE) // P
GRID_W = 64
HEADS, HD = 16, 64
WIN_C, RPB_R, RPB_C = 16, 15, 31
LRU_W = 512
LC = LRU_W // P
LRU_C = 8.0
D_FF = 2816
SF = 256
WIDTH = [SF] * (D_FF // SF - 1) + [SF // 2] * 2
START = [sum(WIDTH[:j]) for j in range(len(WIDTH))]
STEPS = len(WIDTH)
PIECES = 4
EXPERTS = 8
EPS = 1e-6
NEG = -1e30
GAP = 2
W = T_PROMPT + GAP + T_SAMPLE
S0 = T_PROMPT + GAP
TOK = [0, S0, S0 + P]
SLOT = 6144
SLOTS = 3
UNIT = 2048
SPLIT = 2 * 2 * KC * 2 * SF

COL = {}


def columns():
    at = 0
    for name, n in (("c", 8), ("c_ctx", 8), ("norm1", 16),
                    ("norm2", 16), ("conv_w", 16), ("conv_b", 4), ("ba", 8), ("bx", 8), ("lam", 8),
                    ("sc_w", 12), ("sc_b", 4), ("state", 8)):
        COL[name] = at
        at += n
    return at


N_COLS = columns()
assert N_COLS <= P
MODS = 6 * D
GROUP = 4 * 256
SHIFT_SCALE = 2 * KC

C_ID, C_BEFORE, C_ONES, C_MASK, C_NEG, C_IOTA = 0, 128, 256, 384, 448, 512
C_TOKEN, C_EXP, C_ROW = C_IOTA + 384, C_IOTA + 387, C_IOTA + 395
N_CONST = C_ROW + 8
WORK = 18560


def shape_constants():
    k = np.zeros((P, N_CONST), np.float32)
    p = np.arange(P)
    k[:, C_ID:C_ID + P] = np.eye(P)
    k[:, C_BEFORE:C_BEFORE + P] = p[:, None] < p[None, :]
    k[:, C_ONES:C_ONES + P] = 1.0
    q, w = ((P - 1 - p) % GRID_W)[:, None], np.arange(GRID_W)[None, :]
    start = np.clip(q - WIN_C // 2, 0, GRID_W - WIN_C)
    inside = (w >= start) & (w < start + WIN_C)
    k[:, C_MASK:C_MASK + GRID_W] = inside
    k[:, C_NEG:C_NEG + GRID_W] = np.where(inside, 0.0, NEG)
    k[:, C_IOTA:C_IOTA + 384] = np.arange(384)
    for t in range(TILES):
        k[:, C_TOKEN + t] = p + P * t
    k[:, C_EXP:C_EXP + 8] = np.arange(8)
    k[:, C_ROW:C_ROW + 8] = np.arange(8) * (P * TILES)
    return k


def hybrid_step(nc, consts, x_prompt, x_sample, state_lru, cache_k, cache_v, c, c_ctx, norm1_g, norm2_g,
                w_mod, b_mod, w_in, lru_conv_w, lru_conv_b, lru_wa, lru_ba, lru_wx, lru_bx, lru_lam,
                sc_conv_w, sc_conv_b, w_out, ffn_w_gate, ffn_w_up, ffn_w_down, w_qkv, w_o, rpb, w_router,
                moe_w_gate, moe_w_up, moe_w_down, final_g,
                y_prompt, y_sample, new_state, new_k, new_v):
    ctx = ExitStack()
    with ctx:
        def sb(name, shape, dt=F32):
            return ctx.enter_context(nc.sbuf_tensor(name, shape, dt))

        def sem(name):
            return ctx.enter_context(nc.semaphore(name))

        hn_rows = nc.dram_tensor("hn_rows", (P * TILES, D), F32, kind="Internal").ap()
        mod_rows = nc.dram_tensor("mod_rows", (2, 2 * MODS), F32, kind="Internal").ap()
        y_rows = nc.dram_tensor("y_rows", (EXPERTS * P * TILES + P, D), F32, kind="Internal").ap()

        ring = sb("ring", [P, SLOTS, SLOT])
        mod_extra = sb("mod_extra", [P, UNIT])
        k_sb = sb("k_sb", [P, N_CONST])
        vec_rows = sb("vec_rows", [P, 2, P])
        cols = sb("cols", [P, P])
        cond = sb("cond", [P, KC, 2])
        modv = sb("modv", [P, 96, 2])
        gains = sb("gains", [P, KC, 2])
        x = sb("x", [P, TILES, D])
        gate_b = sb("gate_b", [P, 2, D])
        stats = sb("stats", [P, 8, 4])
        small = sb("small", [P, 32])
        zeros = sb("zeros", [P, 256])
        router = sb("router", [P, KC, EXPERTS])
        with ExitStack() as first:
            work = first.enter_context(nc.sbuf_tensor("work", [P, WORK], F32))
            xn = first.enter_context(nc.sbuf_tensor("xn", [P, KC * W], F32))
            hn_t = first.enter_context(nc.sbuf_tensor("hn_t", [P, KC, W], F32))
        split = sb("split", [P, 2, 2, KC, 2 * SF], F32R)
        after_split = sb("after_split", [P, WORK - SPLIT])
        hi_x = sb("hi_x", [P, KC * W], F32R)
        lo_x = sb("lo_x", [P, KC * W], F32R)

        assert sum(WIDTH) == D_FF and STEPS % SLOTS == 0 and STEPS % 2 == 0

        def at(off, *dims):
            n = int(np.prod(dims))
            v = work[:, off:off + n]
            if len(dims) == 2:
                v = v.rearrange("p (a b) -> p a b", a=dims[0])
            if len(dims) == 3:
                v = v.rearrange("p (a b c) -> p a b c", a=dims[0], b=dims[1])
            return v

        ident = k_sb[:, C_ID:C_ID + P]
        before = k_sb[:, C_BEFORE:C_BEFORE + P]
        ones = k_sb[:, C_ONES:C_ONES + P]
        xn_tok = xn[:, 0:TILES * D].rearrange("p (t d) -> p t d", t=TILES)
        y_t = xn[:, :].rearrange("p (c w) -> p c w", c=KC)

        PW = W + 3
        xpad = at(0, LC, PW)
        cvpad = at(LC * PW, LC, PW)
        o = 2 * LC * PW
        xc = at(o, LC, W)
        gr = [at(o + (1 + d) * LC * W, LC, W) for d in range(2)]
        gi = [at(o + (3 + d) * LC * W, LC, W) for d in range(2)]
        dec = at(o + 5 * LC * W, LC, W)
        tmp = at(o + 6 * LC * W, LC, W)
        o += 7 * LC * W
        bd = at(o, 16, P)
        o += 16 * P
        sc_conv = xpad[:, :, 0:W]
        lamk = at(o, 2 * LC)
        lamz = at(o + 8, 2 * LC)
        lamp = at(o + 16, 2 * LC)
        st8 = at(o + 24, 8)
        assert o + 32 <= SPLIT
        mod_row = at(SPLIT, GROUP)[0:2, :]
        mod_bias = at(SPLIT + GROUP, GROUP)[0:2, :]
        st_rows = at(SPLIT + 2 * GROUP, P)

        bias = at(0, HEADS * 6, GRID_W)
        o = HEADS * 6 * GRID_W
        q_t = at(o, KC, W)
        kk_t = at(o + KC * W, KC, W)
        v_tok = at(o + 2 * KC * W, TILES, D)
        o += 2 * KC * W + TILES * D
        kc_t = at(o, KC, P)
        vc = at(o + D, D)
        s_buf = mod_extra[:, 0:768].rearrange("p (a b) -> p a b", a=2)
        p_buf = mod_extra[:, 768:1536].rearrange("p (a b) -> p a b", a=2)
        pt_buf = at(o + 2 * D, 2, 384)
        kc_tok = at(o + 2 * D, D)
        k_out = xn[:, 0:D]
        sums = at(o + 3 * D, TILES, HEADS)
        mx = at(o + 3 * D + 48, 2, 1)
        nmx = at(o + 3 * D + 50, 2, 1)
        assert o + 3 * D + 52 <= WORK

        def step_buffers(off):
            return at(off, SF), at(off + SF, SF), at(off + 2 * SF, 2, P)

        ffn_buf = step_buffers(SPLIT)
        hn_hi = hi_x[:, :].rearrange("p (k w) -> p k w", k=KC)
        hn_lo = lo_x[:, :].rearrange("p (k w) -> p k w", k=KC)

        xg = [mod_extra[:, k * D:(k + 1) * D] for k in range(2)]
        xg_hi, xg_lo = ([v[:, k * D:(k + 1) * D].rearrange("p (c t) -> p c t", c=KC) for k in range(2)]
                        for v in (hi_x, lo_x))
        y_out = [xn[:, 2 * D:3 * D], hn_t[:, :, :].rearrange("p k w -> p (k w)")[:, 2 * D:3 * D]]
        got = [at(0, TILES, D), at(TILES * D, TILES, D)]
        slot_hot = split[:, 1].rearrange("p h k f -> p (h k f)")[:, 0:2 * TILES * 384]\
            .rearrange("p (e t s) -> p e t s", e=2, t=TILES)
        o = SPLIT
        lg, m8, oh1, oh2, mask, rank, rankm, rk_e, pick = (at(o + 24 * n, TILES, EXPERTS) for n in range(9))
        o += 216
        w12 = at(o, 2, TILES)
        e12 = at(o + 6, 2, TILES)
        pos_f = at(o + 12, 2, TILES)
        dv = at(o + 18, TILES)
        cnt_f = at(o + 21, EXPERTS)
        idx_f = at(o + 32, 24)
        moe_buf = step_buffers(o + 64)
        fin_b = at(o + 64 + 3 * SF, D)
        assert o + 64 + 3 * SF + D <= WORK
        token_ids = sb("token_ids", [P, TILES, 2], F32R)
        i8 = sb("i8", [P, TILES, 8], U32)
        pos_i = sb("pos_i", [P, 6], U32)
        idx_a = sb("idx_a", [P, 17], U32)
        idx_b = sb("idx_b", [P, 17], U32)
        idx_now = sb("idx_now", [P, 2], U32)
        over = sb("over", [1, 24], I32)

        ps = ctx.enter_context(nc.psum_tensor("ps", [P, 8, 512], F32))

        s_const, s_x, s_vec, s_bd, s_cache, s_bias, s_router = (sem("ld_" + n) for n in
            ("const", "x", "vec", "bd", "cache", "bias", "router"))
        s_vc, s_fin = sem("ld_vc"), sem("ld_fin")
        ring_full = [sem(f"ring_full{s}") for s in range(SLOTS)]
        ring_free = [sem(f"ring_free{s}") for s in range(SLOTS)]
        down_full = [sem(f"down_full{s}") for s in range(SLOTS)]
        down_used = sem("down_used")
        hi_ok, lo_ok = sem("split_hi_ok"), sem("split_lo_ok")
        hx_hi, hx_lo = sem("tokens_hi_ok"), sem("tokens_lo_ok")
        mod_full = [sem(f"mod_full{s}") for s in range(4)]
        mod_used = sem("mod_used")
        vec_t, cols_ok, cond_ok = sem("vec_turned"), sem("cols_ok"), sem("cond_ok")
        mod_ok = sem("mod_ok")
        mod_copied, mod_bias_in, mod_row_ok, mod_stored, mod_in = (sem("mod_" + n) for n in
            ("copied", "bias_in", "row_ok", "stored", "rows_in"))
        gains_ok = sem("gains_ok")
        ssq_ok, std_ok, xn_ok = sem("ssq_ok"), sem("std_ok"), sem("xn_ok")
        var_ok = sem("var_ok")
        nt_done = sem("norm_turned")
        hn_dve, hn_act = sem("hn_dve"), sem("hn_act")
        gap_ok, bdz = sem("gap_ok"), sem("bd_zeroed")
        pj = sem("proj_done")
        ev_d, ev_a = sem("proj_evac_dve"), sem("proj_evac_act")
        lam_e, lam_ok = sem("lam_exp"), sem("lam_ok")
        xc_ok = sem("xc_ok")
        tanh_ok, m_ok, root_ok, mix_ok = sem("tanh_ok"), sem("m_ok"), sem("root_ok"), sem("mix_ok")
        st_ok, st_t, st_out = sem("st_ok"), sem("st_turned"), sem("st_out")
        gb_ok = sem("gate_b_in")
        out_ps, res_ok = sem("mix_product"), sem("residual_ok")
        gu_ready = [sem(f"gu_ready{k}") for k in range(3)]
        silu_ok = [sem(f"silu_ok{k}") for k in range(3)]
        h_ok = [sem(f"h_ok{k}") for k in range(3)]
        h_turned = [sem(f"h_turned{k}") for k in range(3)]
        ht_ok = [sem(f"ht_ok{k}") for k in range(3)]
        ffn_done = sem("ffn_done")
        qk_ps, qk_ok, v_ps, v_ok = sem("qk_ps"), sem("qk_ok"), sem("v_ps"), sem("v_ok")
        kt_ps, kt_ok, ctx_t, ctx_ok = sem("kt_ps"), sem("kt_ok"), sem("ctx_turned"), sem("ctx_ok")
        st_kv = sem("st_kv")
        bias_ok = sem("bias_ok")
        sc_ps, s_ok, max_ok, p_ok, pt_ps, pt_ok, pv = (sem(n) for n in
            ("score_ps", "score_ok", "max_ok", "prob_ok", "prob_turned", "prob_t_ok", "pv_done"))
        o_ok, ot_ps, ot_ok = sem("o_ok"), sem("o_turned"), sem("o_t_ok")
        hk_ps, hk_ok, hk_st = sem("hn_tok_ps"), sem("hn_tok_ok"), sem("hn_tok_stored")
        lg_ps, mask_ok, rk_ps, rk_ok = sem("logit_ps"), sem("mask_ok"), sem("rank_ps"), sem("rank_ok")
        hot_ok, hot_used, route_ok = sem("hot_ok"), sem("hot_used"), sem("route_ok")
        idx_ok, gathered, xg_turned, xgt_d, xgt_a = (
            [sem(n + k) for k in "ab"] for n in ("idx_ok", "gathered", "xg_turned", "xg_t_dve_", "xg_t_act_"))
        done, y_d, y_a, y_st = ([sem(n + k) for k in "ab"] for n in ("expert_done_", "y_dve_", "y_act_", "y_stored_"))
        collected = sem("collected")
        rounds_over = sem("stores_over")
        y_fin, st_y = sem("y_fin"), sem("st_y")
        v_dve_ok, hk_dve, top_ok, y_ok = sem("v_dve_ok"), sem("hn_tok_dve"), sem("top_ok"), sem("mixer_y_ok")
        qk_dve, ctx_d, ot_d, ffn_ps = sem("qk_dve_ok"), sem("ctx_dve_ok"), sem("o_t_dve"), sem("ffn_ps")
        exp_v, st_r, gather_go = sem("gate_exp"), sem("state_rows"), sem("gather_go")
        zero_ok, y_zero = sem("zero_ok"), sem("y_rows_zeroed")
        chain_d, chain_a, chain_p = sem("dve_order"), sem("act_order"), sem("pool_order")

        F_IN, F_OUT, F_FFN = 0, 5, 7
        F_QKV = F_FFN + STEPS
        F_O = F_QKV + 6
        F_MOE = F_O + 2
        n_dma = [1] * F_FFN + [2] * STEPS + [1] * (F_MOE - F_QKV)

        def slot_of(n):
            return n % SLOTS

        def filled(n):
            return 16 * sum(n_dma[m] for m in range(n + 1) if m % SLOTS == n % SLOTS)

        def frees(n):
            return n == F_OUT or n == F_O

        def last_use(n):
            if frees(n):
                return ring_free[slot_of(n)], sum(frees(m) for m in range(n + 1) if m % SLOTS == n % SLOTS)
            if n < F_OUT:
                return pj, first_item["xcvbg"[n]] + 4
            if F_FFN <= n < F_QKV:
                return lo_ok, PIECES * (n - F_FFN + 1)
            if F_QKV <= n < F_QKV + 4:
                return qk_ps, 4 * (n - F_QKV + 1)
            if F_QKV + 4 <= n < F_O:
                return v_ps, 3 * (n - F_QKV - 3)
            return out_ps, TILES * {F_OUT + 1: 1, F_O + 1: 3}[n]

        TURNS = STEPS // SLOTS
        BASE_FULL = [16 * sum(n_dma[m] for m in range(F_MOE) if m % SLOTS == s) for s in range(SLOTS)]

        def mod_slot(s):
            return mod_extra[:, :] if s == 3 else ring[:, s, 2 * UNIT:3 * UNIT]

        def slab(n):
            return ring[:, slot_of(n), 0:4096].rearrange("p (k f) -> p k f", k=KC)

        def gate_up_raw(s, j):
            return ring[:, s, 0:4096].rearrange("p (g x) -> p g x", g=2)[:, :, 0:KC * WIDTH[j]]\
                .rearrange("p g (k f) -> p g k f", k=KC)

        def down_raw(s, j):
            return ring[:, s, 4096:4096 + WIDTH[j] // P * D].rearrange("p (f d) -> p f d", d=D)

        def split_piece(j, s, part, n):
            k = slice(n * KC // PIECES, (n + 1) * KC // PIECES)
            return (gate_up_raw(s, j)[:, :, k, :],
                    split[:, j % 2, part, k, 0:2 * WIDTH[j]].rearrange("p k (g f) -> p g k f", g=2))

        def cols_of(j):
            return slice(START[j], START[j] + WIDTH[j])

        kview = "(k p) f -> p k f"
        IN_ORDER = [0, 3, 4, 2, 1]
        QKV_ORDER = [2, 3, 0, 1, 4, 5]
        MOD_SPLIT = [(0, 2), (2, 4), (4, 6), (6, 8), (8, 10), (10, 12)]

        items = []
        for g, (kind, eng) in enumerate((("x", "d"), ("c", "a"), ("gate", "a"), ("v", "d"), ("b", "a"), ("g", "a"))):
            for m in range(16 if kind == "gate" else 4):
                items.append((kind, m, eng))
        ev_n = []
        nd = na = 0
        for kind, m, eng in items:
            nd, na = nd + (eng == "d"), na + (eng == "a")
            ev_n.append((ev_d, nd) if eng == "d" else (ev_a, na))
        first_item = {}
        for n, (kind, m, eng) in enumerate(items):
            first_item.setdefault(kind, n)
        PB = 6

        units = [(t, h) for t in (1, 2, 0) for h in range(HEADS)]

        def reverse(v):
            return v.rearrange("p (t q) -> p t q", t=2)[:, :, ::-1]

        def by_tile(v):
            return v.rearrange("p (t q) -> p t q", t=2)

        block = ctx.enter_context(nc.Block())

        @block.sync
        def _(sp):
            def fill(n, dst, src):
                if n >= SLOTS:
                    sp.wait_ge(*last_use(n - SLOTS))
                sp.dma_start(dst, src).then_inc(ring_full[slot_of(n)], 16)

            def mod_group(src, g, first):
                for s in range(4):
                    if not first:
                        sp.wait_ge(mod_used, g * 4 + (s - 3))
                    sp.dma_start(mod_slot(s).rearrange("p (k f) -> p k f", k=KC),
                                 src(s)).then_inc(mod_full[s], 16)

            w0, w1 = (w_mod[l].rearrange(kview, p=P) for l in range(2))
            mod_group(lambda s: w0[:, :, s * 256:(s + 1) * 256], 0, True)
            mod_group(lambda s: w0[:, :, (4 + s) * 256:(5 + s) * 256], 1, False)
            win = w_in[0].rearrange(kview, p=P)
            for f in range(5):
                g = IN_ORDER[f]
                fill(F_IN + f, slab(F_IN + f), win[:, :, g * 512:(g + 1) * 512])
                lo, hi = MOD_SPLIT[f + 1]
                wl, off = (w0, 0) if hi <= 6 else (w1, 6)
                with sp.Fori(lo, hi) as g:
                    mod_group(lambda s: wl[:, :, bass.ds(((g - off) * 4 + s) * 256, 256)], g, False)
            for f in range(2):
                fill(F_OUT + f, slab(F_OUT + f), w_out[0].rearrange(kview, p=P)[:, :, f * 512:(f + 1) * 512])
            wg, wu = ffn_w_gate[0].rearrange(kview, p=P), ffn_w_up[0].rearrange(kview, p=P)
            wd = ffn_w_down[0].rearrange("(f p) d -> p f d", p=P)
            for j in range(STEPS):
                n = F_FFN + j
                s = slot_of(n)
                fill(n, gate_up_raw(s, j)[:, 0], wg[:, :, cols_of(j)])
                sp.dma_start(gate_up_raw(s, j)[:, 1], wu[:, :, cols_of(j)]).then_inc(ring_full[s], 16)
                if j == 0:
                    sp.wait_ge(mod_used, 48)
                if j >= SLOTS:
                    sp.wait_ge(down_used, j - SLOTS + 1)
                sp.dma_start(down_raw(s, j), wd[:, START[j] // P:(START[j] + WIDTH[j]) // P]).then_inc(down_full[s], 16)
            wq = w_qkv[0].rearrange(kview, p=P)
            for f in range(6):
                g = QKV_ORDER[f]
                fill(F_QKV + f, slab(F_QKV + f), wq[:, :, g * 512:(g + 1) * 512])
                if f == SLOTS - 1:
                    sp.wait_ge(out_ps, 2 * TILES)
                    sp.wait_ge(lo_ok, PIECES * STEPS)
                    for h in range(HEADS):
                        for rl in range(2):
                            first = (h * RPB_R + 4 + rl) * RPB_C + (WIN_C - 1) - (GRID_W - 1)
                            src = bass.AP(rpb.tensor, first, [[1, GRID_W], [RPB_C, 6], [1, GRID_W]])
                            sp.dma_start(bias[64 * rl:64 * rl + 64, 6 * h:6 * h + 6, :], src).then_inc(s_bias, 16)
                    sp.wait_ge(st_out, 16)
                    sp.dma_start(kc_tok, cache_k[0, 0].rearrange("h s d -> s h d")).then_inc(s_cache, 16)
                    sp.dma_start(vc, cache_v[0, 0].rearrange("h s d -> s h d")).then_inc(s_vc, 16)
            for f in range(2):
                fill(F_O + f, slab(F_O + f), w_o[0].rearrange(kview, p=P)[:, :, f * 512:(f + 1) * 512])

            wge = moe_w_gate[0].rearrange("e (k p) f -> p e k f", p=P)
            wue = moe_w_up[0].rearrange("e (k p) f -> p e k f", p=P)
            wde = moe_w_down[0].rearrange("e (f p) d -> p e f d", p=P)

            def gate_up_fill(e, j):
                s = slot_of(F_MOE + j)
                for g, wt in enumerate((wge, wue)):
                    sp.dma_start(gate_up_raw(s, j)[:, g], wt[:, bass.ds(e, 1), :, cols_of(j)]
                                 .rearrange("p e k f -> p (e k) f")).then_inc(ring_full[s], 16)

            def down_fill(e, j):
                s = slot_of(F_FFN + j)
                sp.dma_start(down_raw(s, j), wde[:, bass.ds(e, 1), START[j] // P:(START[j] + WIDTH[j]) // P]
                             .rearrange("p e f d -> p (e f) d")).then_inc(down_full[s], 16)

            for j in range(STEPS):
                if j < SLOTS:
                    sp.wait_ge(*last_use(F_MOE + j - SLOTS))
                else:
                    sp.wait_ge(lo_ok, PIECES * (STEPS + j - SLOTS + 1))
                gate_up_fill(0, j)
                if j == 0:
                    sp.wait_ge(out_ps, 2 * TILES)
                else:
                    if j - 1 >= SLOTS:
                        sp.wait_ge(down_used, STEPS - 1 + j - SLOTS)
                    down_fill(0, j - 1)
            sp.wait_ge(route_ok, 1)
            rounds = sp.value_load(over[0:1, 20:21], min_val=EXPERTS, max_val=2 * EXPERTS)
            with sp.Fori(1, rounds) as i:
                e = sp.snap(i % EXPERTS, min_val=0, max_val=EXPERTS - 1)
                e_before = sp.snap((i + (EXPERTS - 1)) % EXPERTS, min_val=0, max_val=EXPERTS - 1)
                for j in range(STEPS):
                    sp.wait_ge(lo_ok, i * (PIECES * STEPS) + PIECES * (STEPS + j - SLOTS + 1))
                    gate_up_fill(e, j)
                    if j == 0:
                        sp.wait_ge(down_used, i * (STEPS - 1) + (STEPS - SLOTS))
                        down_fill(e_before, STEPS - 1)
                        continue
                    d = j - 1
                    if d == SLOTS - 1:
                        sp.wait_ge(done[0], i)
                        sp.wait_ge(done[1], i)
                    else:
                        before_d = d - SLOTS + 1 if d >= SLOTS else d - SLOTS + 2
                        sp.wait_ge(down_used, i * (STEPS - 1) + (STEPS - 1 + before_d))
                    down_fill(e, d)
            sp.wait_ge(down_used, rounds * (STEPS - 1) + (STEPS - SLOTS))
            last_expert = EXPERTS - 1
            s = slot_of(F_FFN + STEPS - 1)
            sp.dma_start(down_raw(s, STEPS - 1), wde[:, last_expert, START[-1] // P:]).then_inc(down_full[s], 16)

        @block.gpsimd
        def _(pool):
            n_chain = [0]

            def ordered(ins):
                n_chain[0] += 1
                ins.then_inc(chain_p, 1)
                pool.wait_ge(chain_p, n_chain[0])

            pool.memset(zeros[:, :], 0.0).then_inc(zero_ok, 1)
            pool.memset(bd, 0.0).then_inc(bdz, 1)
            pool.memset(xpad, 0.0).then_inc(gap_ok, 1)
            pool.memset(cvpad, 0.0).then_inc(gap_ok, 1)
            pool.memset(hn_t[:, :, T_PROMPT:S0], 0.0).then_inc(gap_ok, 1)
            groups = 2 * MODS // GROUP
            bias_rows = b_mod.rearrange("l f -> (l f)")

            def load_mod_bias(g):
                pool.dma_start(mod_bias, bias_rows[g * GROUP:(g + 1) * GROUP].partition_broadcast(2))\
                    .then_inc(mod_bias_in, 16)

            def load_mod_rows(a, b, count):
                pool.wait_ge(mod_stored, 16 * count)
                for g in range(2):
                    pool.dma_start(vec_rows[0:b - a, g, :],
                                   mod_rows[g, a * P:b * P].rearrange("(r p) -> r p", p=P)).then_inc(mod_in, 16)

            load_mod_bias(0)
            for g in range(groups):
                pool.wait_ge(mod_bias_in, 16 * (g + 1))
                pool.wait_ge(mod_copied, 2 * g + 4)
                pool.tensor_tensor(mod_row, mod_row, mod_bias, ALU.add).then_inc(mod_row_ok, 1)
                pool.wait_ge(mod_row_ok, g + 1)
                pool.dma_start(mod_rows[:, g * GROUP:(g + 1) * GROUP], mod_row).then_inc(mod_stored, 16)
                if g + 1 < groups:
                    load_mod_bias(g + 1)
                if (g + 1) * GROUP == SHIFT_SCALE * P:
                    pool.wait_ge(vec_t, 1)
                    load_mod_rows(0, SHIFT_SCALE, g + 1)
            pool.wait_ge(mod_ok, 1)
            load_mod_rows(SHIFT_SCALE, 96, groups)

            pool.wait_ge(s_bias, 16 * 2 * HEADS)
            inside = k_sb[:, C_MASK:C_MASK + GRID_W].unsqueeze(1).to_broadcast([P, HEADS * 6, GRID_W])
            outside = k_sb[:, C_NEG:C_NEG + GRID_W].unsqueeze(1).to_broadcast([P, HEADS * 6, GRID_W])
            ordered(pool.tensor_tensor(bias, bias, inside, ALU.mult))
            pool.tensor_tensor(bias, bias, outside, ALU.add).then_inc(bias_ok, 1)

            pool.wait_ge(route_ok, 1)
            pool.wait_ge(hk_st, 16 * TILES)
            rounds = pool.value_load(over[0:1, 20:21], min_val=EXPERTS, max_val=2 * EXPERTS)

            def gather(k, col):
                table = (idx_a, idx_b)[k]
                pool.tensor_copy(idx_now[:, k:k + 1], table[:, col]).then_inc(idx_ok[k], 1)

            def gather_rows(k):
                pool.indirect_dma_start(
                    out=xg[k], out_offset=None, in_=hn_rows,
                    in_offset=bass.IndirectOffsetOnAxis(ap=idx_now[:, k:k + 1], axis=0),
                ).then_inc(gathered[k], 16)

            for k in range(2):
                gather(k, slice(0, 1))
                pool.wait_ge(idx_ok[k], 1)
                gather_rows(k)
            with pool.Fori(0, rounds) as i:
                for k in range(2):
                    pool.wait_ge(gathered[k], i * 16 + 16)
                    pool.wait_ge(xg_turned[k], i + 1)
                    gather(k, bass.ds(i + 1, 1))
                    pool.wait_ge(idx_ok[k], i + 2)
                    pool.sem_inc(gather_go, 1)
                    gather_rows(k)
            pool.wait_ge(rounds_over, 1)
            for k in range(2):
                for t in range(TILES):
                    pool.indirect_dma_start(
                        out=got[k][:, t, :], out_offset=None, in_=y_rows,
                        in_offset=bass.IndirectOffsetOnAxis(ap=pos_i[:, 3 * k + t:3 * k + t + 1], axis=0),
                    ).then_inc(collected, 16)
            pool.wait_ge(collected, 16 * 2 * TILES)

        @block.scalar
        def _(act):
            n_chain = [0]

            def ordered(ins):
                n_chain[0] += 1
                ins.then_inc(chain_a, 1)
                act.wait_ge(chain_a, n_chain[0])

            act.dma_start(k_sb[:, :], consts).then_inc(s_const, 16)
            rows = []
            for name, src in (("c", c.rearrange("b (r p) -> (b r) p", p=P)),
                              ("c_ctx", c_ctx.rearrange("(r p) -> r p", p=P)),
                              ("norm1", norm1_g.rearrange("l (r p) -> (l r) p", p=P)),
                              ("norm2", norm2_g.rearrange("l (r p) -> (l r) p", p=P)),
                              ("conv_w", lru_conv_w[0].rearrange("k (r p) -> (k r) p", p=P)),
                              ("conv_b", lru_conv_b.rearrange("l (r p) -> (l r) p", p=P)),
                              ("ba", lru_ba[0].rearrange("d (r p) -> (d r) p", p=P)),
                              ("bx", lru_bx[0].rearrange("d (r p) -> (d r) p", p=P)),
                              ("lam", lru_lam[0].rearrange("d (r p) -> (d r) p", p=P)),
                              ("sc_w", sc_conv_w[0].rearrange("k (r p) -> (k r) p", p=P)),
                              ("sc_b", sc_conv_b.rearrange("l (r p) -> (l r) p", p=P)),
                              ("state", state_lru[0, 0].rearrange("d (r p) -> (d r) p", p=P))):
                rows.append((vec_rows[COL[name]:COL[name] + src.shape[0], 0, :], src))
            for dst, src in rows:
                act.dma_start(dst, src).then_inc(s_vec, 16)
            act.dma_start(x[:, 0, :], x_prompt[0]).then_inc(s_x, 16)
            act.dma_start(x[:, 1:3, :], x_sample[0].rearrange("(t p) d -> p t d", p=P)).then_inc(s_x, 16)
            act.wait_ge(bdz, 1)
            for d in range(2):
                for g, wt in enumerate((lru_wa, lru_wx)):
                    for b in range(2):
                        dst = bd[64 * b:64 * b + 64, (2 * d + g) * LC:(2 * d + g + 1) * LC, 64 * b:64 * b + 64]
                        src = wt[0, d].rearrange("(c b) i j -> b i c j", b=2)[b]
                        act.dma_start(dst, src).then_inc(s_bd, 16)
            act.dma_start(router[:, :, :], w_router[0].rearrange("(k p) e -> p k e", p=P)).then_inc(s_router, 16)

            act.wait_ge(cols_ok, 1)
            act.activation(cond[:, :, 0], cols[:, COL["c_ctx"]:COL["c_ctx"] + 8], ACT.Silu).then_inc(cond_ok, 1)
            act.activation(cond[:, :, 1], cols[:, COL["c"]:COL["c"] + 8], ACT.Silu).then_inc(cond_ok, 1)

            def mod_out(*groups):
                for g in groups:
                    if g:
                        act.wait_ge(mod_stored, 16 * g)
                    for hf in range(2):
                        act.wait_ge(mod_used, 4 * g + 2 * hf + 2)
                        act.activation(mod_row[:, 512 * hf:512 * hf + 512], ps[0:2, 6 + hf, :],
                                       ACT.Copy).then_inc(mod_copied, 1)

            def squares(n):
                if n == 0:
                    act.wait_ge(s_x, 32)
                else:
                    act.wait_ge(res_ok, n * TILES)
                for t in range(TILES):
                    act.activation(xn_tok[:, t, :], x[:, t, :], ACT.Square,
                                   accum_out=stats[:, n, t:t + 1]).then_inc(ssq_ok, 1)

            def norm(n):
                if n:
                    squares(n)
                act.wait_ge(var_ok, n + 1)
                act.activation(stats[:, n, 0:3], stats[:, n, 0:3], ACT.Sqrt).then_inc(std_ok, 1)
                if n == 4:
                    return
                act.wait_ge(gains_ok, n + 1)
                base = (n // 2) * 48 + (n % 2) * 24
                for ci in range(KC):
                    if ci % 2:
                        act.wait_ge(nt_done, n * KC + ci + 1)
                        for g, (lo, hi, plo) in enumerate(((0, T_PROMPT, 0), (S0, W, P))):
                            ins = act.activation(hn_t[:, ci, lo:hi], ps[:, ci, plo:plo + hi - lo], ACT.Identity,
                                                 bias=modv[:, base + ci, g:g + 1], scale=gains[:, ci, g:g + 1])
                        ins.then_inc(hn_act, 1)

            def gate_in(n):
                at_ = (n // 2) * MODS + (3 * (n % 2) + 2) * D
                if n:
                    act.wait_ge(res_ok, n * TILES)
                else:
                    act.wait_ge(mod_stored, 16 * (2 * MODS // GROUP))
                for g in range(2):
                    act.dma_start(gate_b[:, g, :], mod_rows[g, at_:at_ + D].partition_broadcast(P)).then_inc(gb_ok, 16)

            act.sem_inc(mod_copied, 2)
            squares(0)
            mod_out(0, 1)
            norm(0)
            act.wait_ge(lam_e, 1)
            act.activation(lamz, lamz, ACT.Exp).then_inc(lam_e, 1)

            mods_before = {"c": (2, 3), "gate": (4, 5), "g": (8, 9)}
            for n, (kind, m, eng) in enumerate(items):
                if eng != "a":
                    continue
                if m == 0 and kind in mods_before:
                    mod_out(*mods_before[kind])
                act.wait_ge(pj, n + 1)
                src = ps[:, n % PB, 0:W]
                if kind == "c":
                    act.wait_ge(gap_ok, 3)
                    ins = act.activation(cvpad[:, m, 2:2 + W], src, ACT.Copy)
                elif kind == "gate":
                    d, g, ch = m // 8, m // 4 % 2, m % 4
                    dst = (gr, gi)[g][d]
                    col = COL[("ba", "bx")[g]] + d * LC + ch
                    ins = act.activation(dst[:, ch, :], src, ACT.Sigmoid, bias=cols[:, col:col + 1])
                elif kind == "b":
                    ins = act.activation(y_t[:, LC + m, :], src, ACT.Copy)
                else:
                    ins = act.activation(y_t[:, m, :], src, ACT.Gelu_apprx_tanh)
                ins.then_inc(ev_a, 1)
                if kind == "gate" and m == 15:
                    act.wait_ge(lam_ok, 1)
                    for d in range(2):
                        if d:
                            act.wait_ge(mix_ok, 1)
                        act.wait_ge(ev_a, [v for (s, v), it in zip(ev_n, items) if it[:2] == ("gate", 15)][0])
                        for ch in range(LC):
                            act.activation(dec[:, ch, :], gr[d][:, ch, :], ACT.Exp,
                                           scale=lamk[:, d * LC + ch:d * LC + ch + 1])
                        for ch in range(LC):
                            ins = act.activation(gr[d][:, ch, :], gr[d][:, ch, :], ACT.Tanh,
                                                 scale=lamk[:, d * LC + ch:d * LC + ch + 1])
                        ins.then_inc(tanh_ok, 1)
                        act.wait_ge(m_ok, d + 1)
                        act.activation(gr[d], gr[d], ACT.Sqrt).then_inc(root_ok, 1)
                        mod_out(6 + d)

            mod_out(10, 11)
            gate_in(0)
            act.wait_ge(zero_ok, 1)
            busy = [y_rows[(e * TILES + 1) * P:(e + 1) * TILES * P, :] for e in range(EXPERTS)]
            for dst in (*busy, y_rows[EXPERTS * TILES * P:, :]):
                dst = dst.rearrange("(p r) (q f) -> p (r q) f", p=P, f=256)
                act.dma_start(dst, zeros[:, :].unsqueeze(1).to_broadcast([P, dst.shape[1], 256])).then_inc(y_zero, 16)
            act.wait_ge(st_r, 1)
            act.dma_start(new_state[0, 0].rearrange("d (r p) -> (d r) p", p=P), st_rows[0:8, :]).then_inc(st_out, 16)

            def split_high(j, s):
                for n in range(PIECES):
                    raw, high = split_piece(j, s, 0, n)
                    act.activation(high, raw, ACT.Copy).then_inc(hi_ok, 1)

            def split_high_ffn(j):
                n = F_FFN + j
                act.wait_ge(ring_full[slot_of(n)], filled(n))
                split_high(j, slot_of(n))

            act.wait_ge(y_ok, 1)
            act.wait_ge(st_t, 1)
            split_high_ffn(0)
            split_high_ffn(1)
            norm(1)
            act.wait_ge(nt_done, 2 * KC)
            act.wait_ge(hn_dve, 2 * 4)
            act.wait_ge(hn_act, 2 * 4)
            for t in range(TILES):
                act.activation(hn_hi[:, :, TOK[t]:TOK[t] + P], hn_t[:, :, TOK[t]:TOK[t] + P],
                               ACT.Copy).then_inc(hx_hi, 1)

            gate_in(1)

            def silu(k, j, count, buf):
                act.wait_ge(gu_ready[k], count + 1)
                act.activation(buf[0][:, 0:WIDTH[j]], ps[:, 0, 0:WIDTH[j]], ACT.Silu).then_inc(silu_ok[k], 1)

            for j in range(STEPS):
                for k in range(TILES):
                    silu(k, j, j, ffn_buf)
                if j + 2 < STEPS:
                    split_high_ffn(j + 2)

            norm(2)
            gate_in(2)

            for n in range(16):
                if n % 2:
                    act.wait_ge(qk_ps, n + 1)
                    m = n % 8
                    if n < 8:
                        act.activation(kk_t[:, m, :], ps[:, n % 6, 0:W], ACT.Copy).then_inc(qk_ok, 1)
                    else:
                        act.activation(q_t[:, m, 0:P], ps[:, n % 6, 0:P], ACT.Copy, scale=HD ** -0.5)
                        act.activation(by_tile(q_t[:, m, S0:W]), reverse(ps[:, n % 6, S0:W]), ACT.Copy,
                                       scale=HD ** -0.5).then_inc(qk_ok, 1)
            for n in range(6):
                if n % 2:
                    act.wait_ge(v_ps, n + 1)
                    f, t = n // 3, n % 3
                    act.activation(v_tok[:, t, f * 512:(f + 1) * 512], ps[:, n, :], ACT.Copy).then_inc(v_ok, 1)
            act.wait_ge(v_ok, 3)
            act.wait_ge(v_dve_ok, 3)
            act.dma_start(new_v[0, 0].rearrange("h s d -> s h d"),
                          v_tok[:, 0, :].rearrange("p (h d) -> p h d", h=HEADS)).then_inc(st_kv, 16)
            act.wait_ge(kt_ok, 1)
            act.dma_start(new_k[0, 0].rearrange("h s d -> s h d"),
                          k_out.rearrange("p (h d) -> p h d", h=HEADS)).then_inc(st_kv, 16)

            act.wait_ge(ctx_t, 1)
            act.activation(kc_t[:, 4:8, :], ps[:, 7, :].rearrange("p (a b) -> p a b", a=4), ACT.Copy).then_inc(ctx_ok, 1)
            for u, (t, h) in enumerate(units):
                n = 384 if t else P
                act.wait_ge(max_ok, u + 1)
                if u >= 2:
                    act.wait_ge(pt_ps, u - 1)
                act.activation(p_buf[:, u % 2, 0:n], s_buf[:, u % 2, 0:n], ACT.Exp, bias=nmx[:, u % 2, :],
                               accum_out=sums[:, t, h:h + 1]).then_inc(p_ok, 1)
                if u >= 1:
                    tp, _ = units[u - 1]
                    np_ = 384 if tp else P
                    act.wait_ge(pt_ps, u)
                    if u >= 3:
                        act.wait_ge(pv, u - 2)
                    act.activation(pt_buf[:, (u - 1) % 2, 0:np_], ps[:, 2 + (u - 1) % 2, 0:np_], ACT.Copy)\
                        .then_inc(pt_ok, 1)
            u = len(units)
            act.wait_ge(pt_ps, u)
            act.wait_ge(pv, u - 2)
            act.activation(pt_buf[:, (u - 1) % 2, 0:P], ps[:, 2 + (u - 1) % 2, 0:P], ACT.Copy).then_inc(pt_ok, 1)
            for ci in range(KC):
                if ci % 2:
                    act.wait_ge(ot_ps, ci + 1)
                    act.activation(hn_t[:, ci, 0:T_PROMPT], ps[:, ci, 0:P], ACT.Copy)
                    act.activation(by_tile(hn_t[:, ci, S0:W]), reverse(ps[:, ci, P:384]), ACT.Copy).then_inc(ot_ok, 1)

            norm(3)
            for n in range(6):
                if n % 2:
                    act.wait_ge(hk_ps, n + 1)
                    t, hf = n // 2, n % 2
                    act.activation(xn_tok[:, t, hf * 512:(hf + 1) * 512], ps[:, n, :], ACT.Copy).then_inc(hk_ok, 1)
                    act.wait_ge(hk_ok, t + 1)
                    act.wait_ge(hk_dve, t + 1)
                    act.dma_start(hn_rows[t * P:(t + 1) * P, :], xn_tok[:, t, :]).then_inc(hk_st, 16)
            act.wait_ge(st_kv, 32)
            act.wait_ge(ring_full[slot_of(F_MOE)], BASE_FULL[slot_of(F_MOE)] + 32)
            split_high(0, slot_of(F_MOE))
            act.dma_start(fin_b, final_g.partition_broadcast(P)).then_inc(s_fin, 16)
            act.wait_ge(top_ok, 1)
            act.activation(dv, dv, ACT.Exp).then_inc(exp_v, 1)
            gate_in(3)

            act.wait_ge(route_ok, 1)
            act.wait_ge(ring_full[slot_of(F_MOE + 1)], BASE_FULL[slot_of(F_MOE + 1)] + 32)
            split_high(1, slot_of(F_MOE + 1))
            rounds = act.value_load(over[0:1, 20:21], min_val=EXPERTS, max_val=2 * EXPERTS)

            def turned_in(k, count):
                act.wait_ge(xg_turned[k], count)
                for hf in range(2):
                    ins = act.activation(xg_hi[k][:, 4 * hf:4 * hf + 4, :],
                                         ps[:, 6 + hf, :].rearrange("p (a b) -> p a b", a=4), ACT.Copy)
                ins.then_inc(xgt_a[k], 1)

            turned_in(0, 1)
            act.wait_ge(y_zero, 16 * (EXPERTS + 1))
            for k in range(2):
                act.sem_inc(y_a[k], 1)
                act.sem_inc(y_st[k], 16)
            with act.Fori(0, rounds) as i:
                e = act.snap(i % EXPERTS, min_val=0, max_val=EXPERTS - 1)
                row = act.snap(e * (P * TILES) + (i // EXPERTS) * (2 * P), min_val=0,
                               max_val=EXPERTS * P * TILES - P)
                more = act.value_load(over[0:1, bass.ds(i, 1)])

                left = act.snap(rounds - i, min_val=1, max_val=2 * EXPERTS)

                def split_ahead(j, of_round):
                    s = slot_of(F_MOE + j)
                    act.wait_ge(ring_full[s], of_round * (32 * TURNS) + (BASE_FULL[s] + 32 * (j // SLOTS + 1)))
                    split_high(j, s)

                def moe_round(ks):
                    if 1 in ks:
                        turned_in(1, i + 1)
                    for j in range(STEPS):
                        for k in ks:
                            silu(k, j, i * STEPS + (STEPS + j), moe_buf)
                        if j + 2 < STEPS:
                            split_ahead(j + 2, i)
                        else:
                            if j == STEPS - 1:
                                turned_in(0, i + 2)
                            with act.If(left > 1):
                                split_ahead(j + 2 - STEPS, i + 1)
                    for k in ks:
                        act.wait_ge(y_st[k], i * 16 + 16)
                        act.wait_ge(done[k], i + 1)
                        act.activation(y_out[k][:, 512:1024], ps[:, 3 + 2 * k, :], ACT.Copy).then_inc(y_a[k], 1)
                    for k in ks:
                        act.wait_ge(y_a[k], i + 2)
                        act.wait_ge(y_d[k], i + 2)
                        act.dma_start(y_rows[bass.ds(row + P * k, P), :], y_out[k]).then_inc(y_st[k], 16)

                with act.If(more > 0):
                    moe_round((0, 1))
                with act.Else():
                    moe_round((0,))
                    act.sem_inc(xgt_a[1], 1)
                    act.sem_inc(silu_ok[1], STEPS)
                    act.sem_inc(y_a[1], 1)
                    act.sem_inc(y_st[1], 16)
                act.nop()
            act.wait_ge(y_st[0], rounds * 16 + 16)
            act.wait_ge(y_st[1], rounds * 16 + 16)
            act.sem_inc(rounds_over, 1)
            norm(4)
            for t in range(TILES):
                act.wait_ge(y_fin, t + 1)
                dst = y_prompt[0] if t == 0 else y_sample[0, (t - 1) * P:t * P, :]
                act.dma_start(dst, xn_tok[:, t, :]).then_inc(st_y, 16)
            act.wait_ge(st_y, 16 * TILES)
            act.wait_ge(st_kv, 32)
            act.wait_ge(st_out, 16)

        @block.vector
        def _(dve):
            n_chain = [0]

            def ordered(ins):
                n_chain[0] += 1
                ins.then_inc(chain_d, 1)
                dve.wait_ge(chain_d, n_chain[0])

            def col(name, n):
                return cols[:, COL[name] + n:COL[name] + n + 1]

            def mod_columns(a, b, bank):
                dve.wait_ge(vec_t, 2 if a == 0 else 3)
                dve.tensor_copy(modv[:, a:b, :],
                                ps[:, bank, 0:2 * P].rearrange("p (g m) -> p m g", g=2)[:, 0:b - a, :]).then_inc(mod_ok, 1)

            def set_gains(n):
                base = (n // 2) * 48 + (n % 2) * 24 + 8
                name = ("norm1", "norm2")[n % 2]
                g0 = COL[name] + 8 * (n // 2)
                if n:
                    dve.wait_ge(hn_act, 4 * n)
                dve.scalar_tensor_tensor(out=gains[:, :, :], in0=modv[:, base:base + 8, :], scalar=1.0,
                                         in1=cols[:, g0:g0 + 8].unsqueeze(2).to_broadcast([P, 8, 2]),
                                         op0=ALU.add, op1=ALU.mult).then_inc(gains_ok, 1)

            def norm(n):
                if n < 4:
                    set_gains(n)
                dve.wait_ge(ssq_ok, TILES * (n + 1))
                st = stats[:, n, 0:3]
                dve.tensor_scalar(st, st, 1.0 / D, EPS, ALU.mult, ALU.add).then_inc(var_ok, 1)
                dve.wait_ge(std_ok, n + 1)
                ordered(dve.reciprocal(st, st))
                if n == 4:
                    return
                for t in range(TILES):
                    dve.tensor_scalar(xn_tok[:, t, :], x[:, t, :], stats[:, n, t:t + 1], None, ALU.mult).then_inc(xn_ok, 1)
                base = (n // 2) * 48 + (n % 2) * 24
                dve.wait_ge(gains_ok, n + 1)
                for ci in range(0, KC, 2):
                    dve.wait_ge(nt_done, n * KC + ci + 1)
                    for g, (lo, hi, plo) in enumerate(((0, T_PROMPT, 0), (S0, W, P))):
                        ins = dve.tensor_scalar(hn_t[:, ci, lo:hi], ps[:, ci, plo:plo + hi - lo],
                                                gains[:, ci, g:g + 1], modv[:, base + ci, g:g + 1], ALU.mult, ALU.add)
                    ins.then_inc(hn_dve, 1)

            def residual(n, bank):
                dve.wait_ge(gb_ok, 32 * (n + 1))
                for t in range(TILES):
                    dve.wait_ge(out_ps, n * TILES + t + 1)
                    for hf in range(2):
                        lo, hi = hf * 512, hf * 512 + 512
                        b = ps[:, bank(t, hf), :]
                        dve.tensor_tensor(b, b, gate_b[:, min(t, 1), lo:hi], ALU.mult).then_inc(chain_d, 1)
                        n_chain[0] += 1
                    dve.wait_ge(chain_d, n_chain[0])
                    for hf in range(2):
                        lo, hi = hf * 512, hf * 512 + 512
                        ins = dve.tensor_tensor(x[:, t, lo:hi], x[:, t, lo:hi], ps[:, bank(t, hf), :], ALU.add)
                        if hf == 0:
                            n_chain[0] += 1
                            ins.then_inc(chain_d, 1)
                        else:
                            ins.then_inc(res_ok, 1)

            dve.wait_ge(vec_t, 1)
            dve.tensor_copy(cols[:, 0:N_COLS], ps[:, 0, 0:N_COLS]).then_inc(cols_ok, 1)
            dve.wait_ge(cols_ok, 1)

            lam = cols[:, COL["lam"]:COL["lam"] + 2 * LC]
            ordered(dve.scalar_tensor_tensor(out=lamz, in0=lam, scalar=-1.0, in1=lam, op0=ALU.mult, op1=ALU.min))
            dve.tensor_scalar(lamp, lam, -1.0, 0.0, ALU.mult, ALU.max).then_inc(lam_e, 1)
            mod_columns(0, SHIFT_SCALE, 6)
            dve.wait_ge(mod_ok, 1)
            dve.wait_ge(s_x, 32)
            norm(0)
            dve.wait_ge(lam_e, 2)
            ordered(dve.tensor_scalar(lamk, lamz, 2.0, None, ALU.add))
            ordered(dve.reciprocal(lamk, lamk))
            ordered(dve.tensor_tensor(lamz, lamz, lamk, ALU.mult))
            zz, acc = small[:, 0:8], small[:, 8:16]
            ordered(dve.tensor_tensor(zz, lamz, lamz, ALU.mult))
            ordered(dve.tensor_scalar(acc, zz, 1.0 / 17, 1.0 / 15, ALU.mult, ALU.add))
            for n in (13, 11, 9, 7, 5, 3, 1):
                ordered(dve.tensor_tensor(acc, acc, zz, ALU.mult))
                ordered(dve.tensor_scalar(acc, acc, 1.0 / n, None, ALU.add))
            ordered(dve.tensor_tensor(acc, acc, lamz, ALU.mult))
            ordered(dve.scalar_tensor_tensor(out=acc, in0=acc, scalar=2.0, in1=lamp, op0=ALU.mult, op1=ALU.add))
            dve.tensor_scalar(lamk, acc, -LRU_C, None, ALU.mult).then_inc(lam_ok, 1)

            dve.wait_ge(gap_ok, 3)
            for m in range(LC):
                n = first_item["x"] + m
                dve.wait_ge(pj, n + 1)
                dve.tensor_copy(xpad[:, m, 2:2 + W], ps[:, n % PB, 0:W]).then_inc(ev_d, 1)
                dve.wait_ge(ev_d, ev_n[n][1])
                ordered(dve.tensor_scalar(xc[:, m, :], xpad[:, m, 0:W], col("conv_w", m), col("conv_b", m),
                                          ALU.mult, ALU.add))
                for k in range(1, 4):
                    ins = dve.scalar_tensor_tensor(out=xc[:, m, :], in0=xpad[:, m, k:k + W],
                                                   scalar=col("conv_w", 4 * k + m), in1=xc[:, m, :],
                                                   op0=ALU.mult, op1=ALU.add)
                    if k < 3:
                        ordered(ins)
                ins.then_inc(xc_ok, 1)
            dve.wait_ge(xc_ok, LC)
            for d in range(2):
                dve.wait_ge(tanh_ok, d + 1)
                ordered(dve.tensor_scalar(tmp, gr[d], -1.0, None, ALU.add))
                ordered(dve.reciprocal(tmp, tmp))
                dve.scalar_tensor_tensor(out=gr[d], in0=gr[d], scalar=2.0, in1=tmp,
                                         op0=ALU.mult, op1=ALU.mult).then_inc(m_ok, 1)
                ordered(dve.tensor_tensor(gi[d], gi[d], xc, ALU.mult))
                dve.wait_ge(root_ok, d + 1)
                ordered(dve.tensor_tensor(gi[d], gi[d], gr[d], ALU.mult))
                at_gap = S0 - 1 if d == 0 else T_PROMPT
                ordered(dve.memset(dec[:, :, at_gap:at_gap + 1], 0.0))
                if d == 0:
                    st0 = COL["state"]
                    ordered(dve.tensor_copy(gi[d][:, :, at_gap:at_gap + 1], cols[:, st0:st0 + LC].unsqueeze(2)))
                else:
                    ordered(dve.memset(gi[d][:, :, at_gap:at_gap + 1], 0.0))
                for m in range(LC):
                    if d == 0:
                        ins = dve.tensor_tensor_scan(gr[d][:, m, :], dec[:, m, :], gi[d][:, m, :], 0.0, ALU.mult, ALU.add)
                    else:
                        ins = dve.tensor_tensor_scan(gr[d][:, m, ::-1], dec[:, m, ::-1], gi[d][:, m, ::-1],
                                                     col("state", LC + m), ALU.mult, ALU.add)
                    ordered(ins)
                dve.sem_inc(mix_ok, 1)
            dve.tensor_copy(st8[:, 0:LC], gr[0][:, :, T_PROMPT - 1]).then_inc(st_ok, 1)
            dve.tensor_copy(st8[:, LC:2 * LC], gr[1][:, :, 0]).then_inc(st_ok, 1)
            ordered(dve.tensor_tensor(tmp, gr[0], gr[1], ALU.add))
            for m in range(LC):
                n = first_item["v"] + m
                dve.wait_ge(pj, n + 1)
                dve.wait_ge(ev_a, ev_n[first_item["c"] + m][1])
                dve.tensor_tensor(cvpad[:, m, 2:2 + W], cvpad[:, m, 2:2 + W], ps[:, n % PB, 0:W],
                                  ALU.mult).then_inc(ev_d, 1)
                dve.wait_ge(ev_d, ev_n[n][1])
                ordered(dve.tensor_scalar(sc_conv[:, m, :], cvpad[:, m, 1:1 + W], col("sc_w", m), col("sc_b", m),
                                          ALU.mult, ALU.add))
                for k in range(1, 3):
                    ordered(dve.scalar_tensor_tensor(out=sc_conv[:, m, :], in0=cvpad[:, m, 1 + k:1 + k + W],
                                                     scalar=col("sc_w", 4 * k + m), in1=sc_conv[:, m, :],
                                                     op0=ALU.mult, op1=ALU.add))
            dve.wait_ge(ev_a, ev_n[first_item["b"] + 3][1])
            ordered(dve.tensor_tensor(y_t[:, LC:KC, :], y_t[:, LC:KC, :], sc_conv, ALU.mult))
            dve.wait_ge(ev_a, ev_n[first_item["g"] + 3][1])
            dve.tensor_tensor(y_t[:, 0:LC, :], y_t[:, 0:LC, :], tmp, ALU.mult).then_inc(y_ok, 1)
            dve.wait_ge(st_t, 1)
            dve.tensor_copy(st_rows[0:8, :], ps[0:8, 7, 0:P]).then_inc(st_r, 1)

            def split_low(j, s, count, pieces):
                for n in pieces:
                    raw, high = split_piece(j, s, 0, n)
                    _, low = split_piece(j, s, 1, n)
                    dve.wait_ge(hi_ok, count + (n + 1))
                    dve.tensor_tensor(low, raw, high.bitcast(F32), ALU.subtract).then_inc(lo_ok, 1)

            def split_low_ffn(j, pieces):
                split_low(j, slot_of(F_FFN + j), PIECES * j, pieces)

            for j in range(2):
                split_low_ffn(j, range(PIECES))
            mod_columns(SHIFT_SCALE, 96, 6)
            residual(0, lambda t, hf: 3 * hf + t)
            dve.wait_ge(mod_ok, 2)

            norm(1)
            dve.wait_ge(nt_done, 2 * KC)
            for t in range(TILES):
                tok = slice(TOK[t], TOK[t] + P)
                dve.wait_ge(hx_hi, t + 1)
                dve.tensor_tensor(hn_lo[:, :, tok], hn_t[:, :, tok], hn_hi[:, :, tok].bitcast(F32),
                                  ALU.subtract).then_inc(hx_lo, 1)

            def hidden(k, j, count, buf):
                w = WIDTH[j]
                dve.wait_ge(silu_ok[k], count + 1)
                dve.tensor_tensor(buf[1][:, 0:w], buf[0][:, 0:w], ps[:, 0, w:2 * w], ALU.mult).then_inc(h_ok[k], 1)

            def hidden_turned(k, j, count, buf):
                w = WIDTH[j]
                dve.wait_ge(h_turned[k], count + 1)
                dve.tensor_copy(buf[2][:, 0:w // P, :], ps[:, 1, 0:w].rearrange("p (f t) -> p f t", t=P))\
                    .then_inc(ht_ok[k], 1)

            for j in range(STEPS):
                for k in range(TILES):
                    ahead = k == TILES - 1 and j + 2 < STEPS
                    hidden(k, j, j, ffn_buf)
                    if ahead:
                        split_low_ffn(j + 2, range(0, PIECES // 2))
                    hidden_turned(k, j, j, ffn_buf)
                    if ahead:
                        split_low_ffn(j + 2, range(PIECES // 2, PIECES))
            residual(1, lambda t, hf: 2 + 2 * t + hf)

            norm(2)
            for n in range(0, 16, 2):
                dve.wait_ge(qk_ps, n + 1)
                m = n % 8
                if n < 8:
                    dve.tensor_copy(kk_t[:, m, :], ps[:, n % 6, 0:W]).then_inc(qk_dve, 1)
                else:
                    dve.tensor_scalar(q_t[:, m, 0:P], ps[:, n % 6, 0:P], HD ** -0.5, None, ALU.mult)
                    dve.tensor_scalar(by_tile(q_t[:, m, S0:W]), reverse(ps[:, n % 6, S0:W]), HD ** -0.5, None,
                                      ALU.mult).then_inc(qk_dve, 1)
            dve.wait_ge(kt_ps, 1)
            dve.tensor_copy(k_out, ps[:, 6:8, :].rearrange("p a b -> p (a b)")).then_inc(kt_ok, 1)
            for n in range(0, 6, 2):
                dve.wait_ge(v_ps, n + 1)
                f, t = n // 3, n % 3
                dve.tensor_copy(v_tok[:, t, f * 512:(f + 1) * 512], ps[:, n, :]).then_inc(v_dve_ok, 1)
            dve.wait_ge(ctx_t, 1)
            dve.tensor_copy(kc_t[:, 0:4, :], ps[:, 6, :].rearrange("p (a b) -> p a b", a=4)).then_inc(ctx_d, 1)

            dve.wait_ge(bias_ok, 1)
            for u, (t, h) in enumerate(units):
                n = 384 if t else P
                dve.wait_ge(sc_ps, u + 1)
                if u >= 2:
                    dve.wait_ge(p_ok, u - 1)
                if t:
                    j0 = 6 * h + 2 - 2 * (t - 1)
                    dve.tensor_tensor(s_buf[:, u % 2, 0:256].rearrange("p (a b) -> p a b", a=4),
                                      ps[:, u % 2, 0:256].rearrange("p (a b) -> p a b", a=4),
                                      bias[:, j0:j0 + 4, :], ALU.add).then_inc(s_ok, 1)
                    dve.tensor_copy(s_buf[:, u % 2, 256:384], ps[:, u % 2, 256:384]).then_inc(s_ok, 1)
                else:
                    dve.sem_inc(s_ok, 1)
                    dve.tensor_copy(s_buf[:, u % 2, 0:P], ps[:, u % 2, 0:P]).then_inc(s_ok, 1)
                dve.wait_ge(s_ok, 2 * u + 2)
                ordered(dve.tensor_reduce(mx[:, u % 2, :], s_buf[:, u % 2, 0:n], AX_X, ALU.max))
                dve.tensor_scalar(nmx[:, u % 2, :], mx[:, u % 2, :], -1.0, None, ALU.mult).then_inc(max_ok, 1)
                for ti, tt in enumerate((1, 2)):
                    if u == HEADS * (ti + 1) + 4:
                        dve.wait_ge(p_ok, HEADS * (ti + 1))
                        ordered(dve.reciprocal(sums[:, tt, :], sums[:, tt, :]))
                        dve.wait_ge(pv, HEADS * (ti + 1))
                        dve.wait_ge(st_kv, 32)
                        dve.tensor_tensor(xn_tok[:, tt, :].rearrange("p (h d) -> p h d", h=HEADS),
                                          ps[:, 4 + 2 * ti:6 + 2 * ti, :].rearrange("p a (h d) -> p (a h) d", d=HD),
                                          sums[:, tt, :].unsqueeze(2).to_broadcast([P, HEADS, HD]),
                                          ALU.mult).then_inc(o_ok, 1)
            dve.wait_ge(p_ok, len(units))
            ordered(dve.reciprocal(sums[:, 0, :], sums[:, 0, :]))
            dve.wait_ge(pv, len(units))
            dve.tensor_tensor(xn_tok[:, 0, :].rearrange("p (h d) -> p h d", h=HEADS),
                              ps[:, 4:6, :].rearrange("p a (h d) -> p (a h) d", d=HD),
                              sums[:, 0, :].unsqueeze(2).to_broadcast([P, HEADS, HD]), ALU.mult).then_inc(o_ok, 1)
            for ci in range(0, KC, 2):
                dve.wait_ge(ot_ps, ci + 1)
                dve.tensor_copy(hn_t[:, ci, 0:T_PROMPT], ps[:, ci, 0:P])
                dve.tensor_copy(by_tile(hn_t[:, ci, S0:W]), reverse(ps[:, ci, P:384])).then_inc(ot_d, 1)
            residual(2, lambda t, hf: 3 * hf + t)

            norm(3)
            for n in range(0, 6, 2):
                dve.wait_ge(hk_ps, n + 1)
                t, hf = n // 2, n % 2
                dve.tensor_copy(xn_tok[:, t, hf * 512:(hf + 1) * 512], ps[:, n, :]).then_inc(hk_dve, 1)

            dve.wait_ge(lg_ps, 1)
            dve.wait_ge(st_kv, 32)
            ordered(dve.tensor_copy(lg, ps[:, 6, 0:24].rearrange("p (t e) -> p t e", t=TILES)))
            for t in range(TILES):
                ordered(dve.max(m8[:, t, :], lg[:, t, :]))
                ordered(dve.max_index(i8[:, t, :], m8[:, t, :], lg[:, t, :]))
            dve.tensor_tensor(dv, m8[:, :, 1], m8[:, :, 0], ALU.subtract).then_inc(top_ok, 1)
            experts = k_sb[:, C_EXP:C_EXP + 8].unsqueeze(1).to_broadcast([P, TILES, EXPERTS])
            for k, oh in enumerate((oh1, oh2)):
                ordered(dve.tensor_copy(e12[:, k, :], i8[:, :, k]))
                ordered(dve.tensor_tensor(oh, experts, e12[:, k, :].unsqueeze(2).to_broadcast([P, TILES, EXPERTS]),
                                          ALU.is_equal))
            dve.tensor_tensor(mask, oh1, oh2, ALU.add).then_inc(mask_ok, 1)
            dve.wait_ge(rk_ps, 1)
            ordered(dve.tensor_copy(rank, ps[:, 7, 0:24].rearrange("p (t e) -> p t e", t=TILES)))
            dve.tensor_copy(token_ids[:, :, :], k_sb[:, C_TOKEN:C_TOKEN + TILES].unsqueeze(2)
                            .to_broadcast([P, TILES, 2]))
            dve.tensor_copy(cnt_f, ps[:, 7, 24:32]).then_inc(rk_ok, 1)
            ordered(dve.scalar_tensor_tensor(out=rankm, in0=rank, scalar=1.0, in1=mask, op0=ALU.add, op1=ALU.mult))
            ordered(dve.tensor_scalar(rankm, rankm, -1.0, None, ALU.add))
            for e in range(EXPERTS):
                if e >= 2:
                    dve.wait_ge(hot_used, e - 1)
                for t in range(TILES):
                    dve.tensor_scalar(slot_hot[:, e % 2, t, :], k_sb[:, C_IOTA:C_IOTA + 384], rankm[:, t, e:e + 1],
                                      None, ALU.is_equal).then_inc(hot_ok, 1)
            split_low(0, slot_of(F_MOE), PIECES * STEPS, range(PIECES))
            rows_e = k_sb[:, C_ROW:C_ROW + 8].unsqueeze(1).to_broadcast([P, TILES, EXPERTS])
            ordered(dve.tensor_tensor(rk_e, rank, rows_e, ALU.add))
            for k, oh in enumerate((oh1, oh2)):
                ordered(dve.tensor_tensor(pick, oh, rk_e, ALU.mult))
                ordered(dve.tensor_reduce(pos_f[:, k, :], pick, AX_X, ALU.add))
            ordered(dve.tensor_copy(pos_i[:, :], pos_f.rearrange("p k t -> p (k t)")))
            dve.wait_ge(exp_v, 1)
            ordered(dve.tensor_scalar(w12[:, 0, :], dv, 1.0, None, ALU.add))
            ordered(dve.reciprocal(w12[:, 0, :], w12[:, 0, :]))
            ordered(dve.tensor_tensor(w12[:, 1, :], w12[:, 0, :], dv, ALU.mult))
            dve.wait_ge(rk_ok, 1)
            ordered(dve.tensor_reduce(small[:, 16:17], cnt_f, AX_X, ALU.max))
            ordered(dve.tensor_scalar(small[:, 17:18], small[:, 16:17], 256.5, 8.0, ALU.is_gt, ALU.mult))
            ordered(dve.tensor_scalar(small[:, 18:19], small[:, 17:18], 8.0, None, ALU.add))
            ordered(dve.memset(over[:, :], 0))
            ordered(dve.tensor_scalar(over[0:1, 0:8], cnt_f[0:1, :], -128.0, None, ALU.add))
            ordered(dve.tensor_copy(over[0:1, 20:21], small[0:1, 18:19]))
            ordered(dve.memset(idx_a[:, :], 0))
            ordered(dve.memset(idx_b[:, :], 0))
            dve.wait_ge(hot_used, EXPERTS)
            ordered(dve.tensor_copy(idx_f, ps[:, 7, 64:112:2]))
            by_chunk = idx_f.rearrange("p (e c) -> p e c", c=TILES)
            ordered(dve.tensor_copy(idx_a[:, 0:8], by_chunk[:, :, 0]))
            ordered(dve.tensor_copy(idx_a[:, 8:16], by_chunk[:, :, 2]))
            ordered(dve.tensor_copy(idx_b[:, 0:8], by_chunk[:, :, 1]))
            dve.sem_inc(route_ok, 1)
            split_low(1, slot_of(F_MOE + 1), PIECES * (STEPS + 1), range(PIECES))

            rounds = dve.value_load(over[0:1, 20:21], min_val=EXPERTS, max_val=2 * EXPERTS)

            def turned_in(k, count):
                dve.wait_ge(xgt_a[k], count)
                for hf in range(2):
                    c_ = slice(4 * hf, 4 * hf + 4)
                    ins = dve.tensor_tensor(xg_lo[k][:, c_, :], ps[:, 6 + hf, :].rearrange("p (a b) -> p a b", a=4),
                                            xg_hi[k][:, c_, :].bitcast(F32), ALU.subtract)
                ins.then_inc(xgt_d[k], 1)

            turned_in(0, 1)
            for k in range(2):
                dve.sem_inc(y_d[k], 1)
            with dve.Fori(0, rounds) as i:
                more = dve.value_load(over[0:1, bass.ds(i, 1)])

                left = dve.snap(rounds - i, min_val=1, max_val=2 * EXPERTS)

                def split_ahead(j, of_round, pieces):
                    split_low(j, slot_of(F_MOE + j), of_round * (PIECES * STEPS) + PIECES * (STEPS + j), pieces)

                def moe_round(ks):
                    if 1 in ks:
                        turned_in(1, i + 1)
                    for j in range(STEPS):
                        for k in ks:
                            ahead = k == ks[-1] and j + 2 < STEPS
                            hidden(k, j, i * STEPS + (STEPS + j), moe_buf)
                            if ahead:
                                split_ahead(j + 2, i, range(0, PIECES // 2))
                            hidden_turned(k, j, i * STEPS + (STEPS + j), moe_buf)
                            if ahead:
                                split_ahead(j + 2, i, range(PIECES // 2, PIECES))
                        if j == STEPS - 1:
                            turned_in(0, i + 2)
                        if j + 2 >= STEPS:
                            with dve.If(left > 1):
                                split_ahead(j + 2 - STEPS, i + 1, range(PIECES))
                    for k in ks:
                        dve.wait_ge(y_st[k], i * 16 + 16)
                        dve.wait_ge(done[k], i + 1)
                        dve.tensor_copy(y_out[k][:, 0:512], ps[:, 2 + 2 * k, :]).then_inc(y_d[k], 1)

                with dve.If(more > 0):
                    moe_round((0, 1))
                with dve.Else():
                    moe_round((0,))
                    dve.sem_inc(xgt_d[1], 1)
                    dve.sem_inc(h_ok[1], STEPS)
                    dve.sem_inc(ht_ok[1], STEPS)
                    dve.sem_inc(y_d[1], 1)
                dve.nop()

            dve.wait_ge(gb_ok, 32 * 4)
            dve.wait_ge(collected, 16 * 2 * TILES)
            for t in range(TILES):
                a, b = got[0][:, t, :], got[1][:, t, :]
                ordered(dve.tensor_scalar(a, a, w12[:, 0, t:t + 1], None, ALU.mult))
                ordered(dve.scalar_tensor_tensor(out=a, in0=b, scalar=w12[:, 1, t:t + 1], in1=a,
                                                 op0=ALU.mult, op1=ALU.add))
                ordered(dve.tensor_tensor(a, a, gate_b[:, min(t, 1), :], ALU.mult))
                dve.tensor_tensor(x[:, t, :], x[:, t, :], a, ALU.add).then_inc(res_ok, 1)
            dve.wait_ge(res_ok, 4 * TILES)
            norm(4)
            dve.wait_ge(s_fin, 16)
            for t in range(TILES):
                dve.scalar_tensor_tensor(out=xn_tok[:, t, :], in0=x[:, t, :], scalar=stats[:, 4, t:t + 1], in1=fin_b,
                                         op0=ALU.mult, op1=ALU.mult).then_inc(y_fin, 1)

        @block.tensor
        def _(pe):
            def turn(dst, src):
                return pe.transpose(dst, src, ident[0:src.shape[0], 0:src.shape[0]])

            def norm(n):
                pe.wait_ge(xn_ok, TILES * (n + 1))
                for ci in range(KC):
                    for t in range(TILES):
                        ins = turn(ps[:, ci, t * P:(t + 1) * P], xn_tok[:, t, ci * P:(ci + 1) * P])
                    ins.then_inc(nt_done, 1)

            def hn_ready(n):
                pe.wait_ge(hn_dve, 4 * (n + 1))
                pe.wait_ge(hn_act, 4 * (n + 1))

            def mod_groups(lo, hi):
                with pe.Fori(lo, hi) as g:
                    for s in range(4):
                        if s % 2 == 0:
                            pe.wait_ge(mod_copied, g * 2 + (s // 2 + 1))
                        pe.wait_ge(mod_full[s], g * 16 + 16)
                        wt = mod_slot(s).rearrange("p (k f) -> p k f", k=KC)
                        for k in range(KC):
                            ins = pe.matmul(ps[0:2, 6 + s // 2, (s % 2) * 256:(s % 2 + 1) * 256], cond[:, k, :],
                                            wt[:, k, :], start=(k == 0), stop=(k == KC - 1))
                        ins.then_inc(mod_used, 1)

            def turn_mod_rows(n_rows, count):
                pe.wait_ge(mod_in, count)
                for g in range(2):
                    ins = turn(ps[:, 6, g * P:g * P + n_rows], vec_rows[0:n_rows, g, :])
                ins.then_inc(vec_t, 1)

            def full(n):
                pe.wait_ge(ring_full[slot_of(n)], filled(n))

            pe.wait_ge(s_const, 16)
            pe.wait_ge(s_vec, 16 * 12)
            turn(ps[:, 0, 0:N_COLS], vec_rows[0:N_COLS, 0, :]).then_inc(vec_t, 1)
            pe.wait_ge(cond_ok, 2)
            mod_groups(0, 2)
            turn_mod_rows(SHIFT_SCALE, 32)
            pe.wait_ge(mod_ok, 1)
            norm(0)
            hn_ready(0)
            pe.wait_ge(gap_ok, 3)

            fill_n = {"x": 0, "c": 1, "v": 2, "b": 3, "g": 4}
            after = {"x": (2, 4), "c": (4, 6), "v": (6, 8), "b": (8, 10), "g": (10, 12)}
            for n, (kind, m, eng) in enumerate(items):
                if n >= PB:
                    pe.wait_ge(*ev_n[n - PB])
                if kind == "gate":
                    if n == first_item["gate"]:
                        pe.wait_ge(s_bd, 16 * 8)
                    pe.wait_ge(xc_ok, m % 4 + 1)
                    pe.matmul(ps[:, n % PB, 0:W], bd[:, m, :], xc[:, m % 4, :], start=True, stop=True).then_inc(pj, 1)
                    continue
                f = fill_n[kind]
                if m == 0:
                    full(F_IN + f)
                for k in range(KC):
                    ins = pe.matmul(ps[:, n % PB, 0:W], slab(F_IN + f)[:, k, m * P:(m + 1) * P], hn_t[:, k, :],
                                    start=(k == 0), stop=(k == KC - 1))
                ins.then_inc(pj, 1)
                if m == 3:
                    mod_groups(*after[kind])

            def product(n_sub, base_fill, lhs, bank):
                for f in range(2):
                    n = base_fill + f
                    full(n)
                    for t in range(TILES):
                        for k in range(KC):
                            ins = pe.matmul(ps[:, bank(t, f), :], lhs[:, k, TOK[t]:TOK[t] + P], slab(n)[:, k, :],
                                            start=(k == 0), stop=(k == KC - 1))
                        if f == 1:
                            ins.then_inc(out_ps, 1)
                    if f == 0:
                        ins.then_inc(ring_free[slot_of(n)], 1)
                        if n == F_OUT:
                            turn_mod_rows(96 - SHIFT_SCALE, 64)

            pe.wait_ge(ev_a, ev_n[-1][1])
            pe.wait_ge(st_ok, 2)
            pe.wait_ge(mod_copied, 2 + 2 * (2 * MODS // GROUP))
            turn(ps[0:8, 7, 0:P], st8).then_inc(st_t, 1)
            pe.wait_ge(y_ok, 1)
            product(0, F_OUT, y_t, lambda t, f: 3 * f + t)

            def gate_up(j, hi, lo, k):
                w = WIDTH[j]
                for c_ in range(KC):
                    for n, (xt, part) in enumerate(((hi, 0), (hi, 1), (lo, 0))):
                        ins = pe.matmul(ps[:, 0, 0:2 * w], xt(c_), split[:, j % 2, part, c_, 0:2 * w],
                                        start=(c_ == 0 and n == 0), stop=(c_ == KC - 1 and n == 2))
                ins.then_inc(gu_ready[k], 1)

            def turn_hidden(k, j, count, buf):
                pe.wait_ge(h_ok[k], count + 1)
                for f in range(WIDTH[j] // P):
                    ins = turn(ps[:, 1, f * P:(f + 1) * P], buf[1][:, f * P:(f + 1) * P])
                ins.then_inc(h_turned[k], 1)

            def down(s, j, k, count, buf):
                pe.wait_ge(ht_ok[k], count + 1)
                last = WIDTH[j] // P - 1
                for f in range(last + 1):
                    for hf in range(2):
                        ins = pe.matmul(ps[:, 2 + 2 * k + hf, :], buf[2][:, f, :],
                                        down_raw(s, j)[:, f, hf * 512:(hf + 1) * 512],
                                        start=(j == 0 and f == 0), stop=(j == STEPS - 1 and f == last))
                return ins

            norm(1)
            hn_ready(1)
            todo = [(j, k) for j in range(STEPS) for k in range(TILES)]
            for u in range(len(todo) + 1):
                if u:
                    pj_, pk = todo[u - 1]
                    turn_hidden(pk, pj_, pj_, ffn_buf)
                if u < len(todo):
                    j, k = todo[u]
                    if k == 0:
                        pe.wait_ge(lo_ok, PIECES * (j + 1))
                    if j == 0:
                        pe.wait_ge(hx_lo, k + 1)
                    tok = slice(TOK[k], TOK[k] + P)
                    gate_up(j, lambda c_: hn_hi[:, c_, tok], lambda c_: hn_lo[:, c_, tok], k)
                if u:
                    s = slot_of(F_FFN + pj_)
                    if pk == 0:
                        pe.wait_ge(down_full[s], 16 * (pj_ // SLOTS + 1))
                    ins = down(s, pj_, pk, pj_, ffn_buf)
                    if pj_ == STEPS - 1:
                        ins.then_inc(out_ps, 1)
                    elif pk == TILES - 1:
                        ins.then_inc(down_used, 1)

            norm(2)
            hn_ready(2)
            for n in range(16):
                f, m = n // 4, n % 4
                if m == 0:
                    full(F_QKV + f)
                if n >= 6:
                    pe.wait_ge((qk_dve, qk_ok)[n % 2], (n - 6) // 2 + 1)
                for k in range(KC):
                    ins = pe.matmul(ps[:, n % 6, 0:W], slab(F_QKV + f)[:, k, m * P:(m + 1) * P], hn_t[:, k, :],
                                    start=(k == 0), stop=(k == KC - 1))
                ins.then_inc(qk_ps, 1)
            pe.wait_ge(qk_dve, 8)
            pe.wait_ge(qk_ok, 8)
            for k in range(KC):
                ins = turn(ps[:, 6 + k // 4, (k % 4) * P:(k % 4 + 1) * P], kk_t[:, k, 0:P])
            ins.then_inc(kt_ps, 1)
            for n in range(6):
                f, t = n // 3, n % 3
                if t == 0:
                    full(F_QKV + 4 + f)
                for k in range(KC):
                    ins = pe.matmul(ps[:, n, :], hn_t[:, k, TOK[t]:TOK[t] + P], slab(F_QKV + 4 + f)[:, k, :],
                                    start=(k == 0), stop=(k == KC - 1))
                ins.then_inc(v_ps, 1)
            pe.wait_ge(kt_ok, 1)
            pe.wait_ge(s_cache, 16)
            for k in range(KC):
                ins = turn(ps[:, 6 + k // 4, (k % 4) * P:(k % 4 + 1) * P], kc_tok[:, k * P:(k + 1) * P])
            ins.then_inc(ctx_t, 1)
            pe.wait_ge(ctx_d, 1)
            pe.wait_ge(ctx_ok, 1)
            pe.wait_ge(v_dve_ok, 3)
            pe.wait_ge(v_ok, 3)
            pe.wait_ge(s_vc, 16)

            n_units = len(units)
            for u in range(n_units + 2):
                if u < n_units:
                    t, h = units[u]
                    r, ci = 64 * (h % 2), h // 2
                    if u >= 2:
                        pe.wait_ge(s_ok, 2 * (u - 1))
                    q = q_t[r:r + 64, ci, TOK[t]:TOK[t] + P]
                    if t:
                        pe.matmul(ps[:, u % 2, 0:256], q, kk_t[r:r + 64, ci, S0:W], start=True, stop=True)
                        ins = pe.matmul(ps[:, u % 2, 256:384], q, kc_t[r:r + 64, ci, :], start=True, stop=True)
                    else:
                        ins = pe.matmul(ps[:, u % 2, 0:P], q, kk_t[r:r + 64, ci, 0:P], start=True, stop=True)
                    ins.then_inc(sc_ps, 1)
                if 1 <= u <= n_units:
                    w_ = u - 1
                    tp = units[w_][0]
                    pe.wait_ge(p_ok, w_ + 1)
                    if w_ >= 2:
                        pe.wait_ge(pt_ok, w_ - 1)
                    for b in range(3 if tp else 1):
                        ins = turn(ps[:, 2 + w_ % 2, b * P:(b + 1) * P], p_buf[:, w_ % 2, b * P:(b + 1) * P])
                    ins.then_inc(pt_ps, 1)
                if u >= 2:
                    w_ = u - 2
                    tp, hp = units[w_]
                    ti = w_ // HEADS
                    if ti == 2 and hp == 0:
                        pe.wait_ge(o_ok, 1)
                    pe.wait_ge(pt_ok, w_ + 1)
                    vs = [v_tok[:, 1, :], v_tok[:, 2, :], vc] if tp else [v_tok[:, 0, :]]
                    b0 = 4 + 2 * (ti % 2) + hp // 8
                    for b, vv in enumerate(vs):
                        ins = pe.matmul(ps[:, b0, (hp % 8) * HD:(hp % 8 + 1) * HD], pt_buf[:, w_ % 2, b * P:(b + 1) * P],
                                        vv[:, hp * HD:(hp + 1) * HD], start=(b == 0), stop=(b == len(vs) - 1))
                    ins.then_inc(pv, 1)
            pe.wait_ge(o_ok, 3)
            for ci in range(KC):
                for t in range(TILES):
                    ins = turn(ps[:, ci, t * P:(t + 1) * P], xn_tok[:, t, ci * P:(ci + 1) * P])
                ins.then_inc(ot_ps, 1)
            pe.wait_ge(ot_d, 4)
            pe.wait_ge(ot_ok, 4)
            product(2, F_O, hn_t, lambda t, f: 3 * f + t)

            norm(3)
            hn_ready(3)
            pe.wait_ge(s_router, 16)
            for t in range(TILES):
                for k in range(KC):
                    ins = pe.matmul(ps[:, 6, t * 8:(t + 1) * 8], hn_t[:, k, TOK[t]:TOK[t] + P], router[:, k, :],
                                    start=(k == 0), stop=(k == KC - 1))
            ins.then_inc(lg_ps, 1)
            for n in range(6):
                t, hf = n // 2, n % 2
                for k in range(4):
                    ins = turn(ps[:, n, k * P:(k + 1) * P], hn_t[:, 4 * hf + k, TOK[t]:TOK[t] + P])
                ins.then_inc(hk_ps, 1)
            pe.wait_ge(mask_ok, 1)
            for t in range(TILES):
                for b in range(t + 1):
                    pe.matmul(ps[:, 7, t * 8:(t + 1) * 8], before if b == t else ones, mask[:, b, :],
                              start=(b == 0), stop=(b == t))
            for b in range(TILES):
                ins = pe.matmul(ps[:, 7, 24:32], ones, mask[:, b, :], start=(b == 0), stop=(b == TILES - 1))
            ins.then_inc(rk_ps, 1)
            pe.wait_ge(rk_ok, 1)
            for e in range(EXPERTS):
                pe.wait_ge(hot_ok, TILES * (e + 1))
                for ch in range(TILES):
                    for t in range(TILES):
                        o = 64 + 2 * (TILES * e + ch)
                        ins = pe.matmul(ps[:, 7, o:o + 2], slot_hot[:, e % 2, t, ch * P:(ch + 1) * P],
                                        token_ids[:, t, :],
                                        start=(t == 0), stop=(t == TILES - 1))
                ins.then_inc(hot_used, 1)
            pe.wait_ge(hk_dve, 3)
            pe.wait_ge(hk_ok, 3)
            pe.wait_ge(route_ok, 1)

            def turn_gathered(k, count):
                pe.wait_ge(gathered[k], count)
                for c_ in range(KC):
                    ins = turn(ps[:, 6 + c_ // 4, (c_ % 4) * P:(c_ % 4 + 1) * P], xg[k][:, c_ * P:(c_ + 1) * P])
                ins.then_inc(xg_turned[k], 1)

            turn_gathered(0, 16)
            rounds = pe.value_load(over[0:1, 20:21], min_val=EXPERTS, max_val=2 * EXPERTS)
            with pe.Fori(0, rounds) as i:
                more = pe.value_load(over[0:1, bass.ds(i, 1)])

                def moe_round(ks):
                    pe.wait_ge(xgt_d[0], i + 1)
                    if 1 in ks:
                        turn_gathered(1, i * 16 + 16)
                    todo = [(j, k) for j in range(STEPS) for k in ks]
                    for u in range(len(todo) + 1):
                        if u:
                            pj_, pk = todo[u - 1]
                            turn_hidden(pk, pj_, i * STEPS + (STEPS + pj_), moe_buf)
                        if u < len(todo):
                            j, k = todo[u]
                            if k == 0:
                                pe.wait_ge(lo_ok, i * (PIECES * STEPS) + PIECES * (STEPS + j + 1))
                            elif j == 0:
                                pe.wait_ge(xgt_d[1], i + 1)
                            gate_up(j, lambda c_: xg_hi[k][:, c_, :], lambda c_: xg_lo[k][:, c_, :], k)
                        if u:
                            s = slot_of(F_FFN + pj_)
                            if pk == 0:
                                pe.wait_ge(down_full[s], i * (16 * TURNS) + 16 * (TURNS + pj_ // SLOTS + 1))
                            if pj_ == 0:
                                pe.wait_ge(y_d[pk], i + 1)
                                pe.wait_ge(y_a[pk], i + 1)
                            ins = down(s, pj_, pk, i * STEPS + (STEPS + pj_), moe_buf)
                            if pj_ == STEPS - 1:
                                ins.then_inc(done[pk], 1)
                            elif pk == ks[-1]:
                                ins.then_inc(down_used, 1)
                            if pj_ == 5 and pk == ks[-1]:
                                turn_gathered(0, i * 16 + 32)

                with pe.If(more > 0):
                    moe_round((0, 1))
                with pe.Else():
                    pe.sem_inc(xg_turned[1], 1)
                    moe_round((0,))
                    pe.sem_inc(gu_ready[1], STEPS)
                    pe.sem_inc(h_turned[1], STEPS)
                    pe.sem_inc(done[1], 1)
                pe.nop()


_INS = ['x_prompt', 'x_sample', 'state_lru', 'cache_k', 'cache_v', 'c', 'c_ctx', 'norm1_g', 'norm2_g', 'w_mod', 'b_mod',
        'w_in', 'lru_conv_w', 'lru_conv_b', 'lru_wa', 'lru_ba', 'lru_wx', 'lru_bx', 'lru_lam', 'sc_conv_w', 'sc_conv_b',
        'w_out', 'ffn_w_gate', 'ffn_w_up', 'ffn_w_down', 'w_qkv', 'w_o', 'rpb', 'w_router', 'moe_w_gate', 'moe_w_up',
        'moe_w_down', 'final_g']
_OUTS = [(1, 128, 1024), (1, 256, 1024), (1, 1, 2, 512), (1, 1, 16, 128, 64), (1, 1, 16, 128, 64)]


def kernel(**inputs):
    import concourse.bacc as _bacc
    from concourse.bass_utils import run_bass_kernel_spmd as _run

    nc = _bacc.Bacc("TRN2", target_bir_lowering=False, num_devices=1)
    arrays = {"shape_constants_dram": shape_constants()}
    args = [nc.dram_tensor("shape_constants_dram", (P, N_CONST), F32, kind="ExternalInput").ap()]
    for name in _INS:
        a = np.ascontiguousarray(inputs[name])
        arrays[f"in_{name}_dram"] = a
        args.append(nc.dram_tensor(f"in_{name}_dram", a.shape, mybir.dt.from_np(a.dtype), kind="ExternalInput").ap())
    for i, shape in enumerate(_OUTS):
        args.append(nc.dram_tensor(f"out_{i}_dram", shape, F32, kind="ExternalOutput").ap())
    hybrid_step(nc, *args)
    r = _run(nc, [arrays], core_ids=[0])
    return tuple(r.results[0][f"out_{i}_dram"] for i in range(len(_OUTS)))
```

```python
from contextlib import ExitStack

import numpy as np
import concourse.bass as bass
from concourse import mybir

F32 = mybir.dt.float32
F32R = mybir.dt.float32r
I32 = mybir.dt.int32
U32 = mybir.dt.uint32
ALU = mybir.AluOpType
ACT = mybir.ActivationFunctionType
AX_X = mybir.AxisListType.X

P = 128
D = 1024
KC = D // P
T_PROMPT, T_SAMPLE = 128, 256
TILES = (T_PROMPT + T_SAMPLE) // P
GRID_W = 64
HEADS, HD = 16, 64
WIN_C, RPB_R, RPB_C = 16, 15, 31
LRU_W = 512
LC = LRU_W // P
LRU_C = 8.0
D_FF = 2816
SF = 256
WIDTH = [SF] * (D_FF // SF - 1) + [SF // 2] * 2
START = [sum(WIDTH[:j]) for j in range(len(WIDTH))]
STEPS = len(WIDTH)
PIECES = 4
EXPERTS = 8
EPS = 1e-6
NEG = -1e30
GAP = 2
W = T_PROMPT + GAP + T_SAMPLE
S0 = T_PROMPT + GAP
TOK = [0, S0, S0 + P]
SLOT = 6144
SLOTS = 3
UNIT = 2048
SPLIT = 2 * 2 * KC * 2 * SF

COL = {}


def columns():
    at = 0
    for name, n in (("c", 8), ("c_ctx", 8), ("norm1", 16),
                    ("norm2", 16), ("conv_w", 16), ("conv_b", 4), ("ba", 8), ("bx", 8), ("lam", 8),
                    ("sc_w", 12), ("sc_b", 4), ("state", 8)):
        COL[name] = at
        at += n
    return at


N_COLS = columns()
assert N_COLS <= P
MODS = 6 * D
GROUP = 4 * 256
SHIFT_SCALE = 2 * KC

C_ID, C_BEFORE, C_ONES, C_MASK, C_NEG, C_IOTA = 0, 128, 256, 384, 448, 512
C_TOKEN, C_EXP, C_ROW = C_IOTA + 384, C_IOTA + 387, C_IOTA + 395
N_CONST = C_ROW + 8
WORK = 18560


def shape_constants():
    k = np.zeros((P, N_CONST), np.float32)
    p = np.arange(P)
    k[:, C_ID:C_ID + P] = np.eye(P)
    k[:, C_BEFORE:C_BEFORE + P] = p[:, None] < p[None, :]
    k[:, C_ONES:C_ONES + P] = 1.0
    q, w = ((P - 1 - p) % GRID_W)[:, None], np.arange(GRID_W)[None, :]
    start = np.clip(q - WIN_C // 2, 0, GRID_W - WIN_C)
    inside = (w >= start) & (w < start + WIN_C)
    k[:, C_MASK:C_MASK + GRID_W] = inside
    k[:, C_NEG:C_NEG + GRID_W] = np.where(inside, 0.0, NEG)
    k[:, C_IOTA:C_IOTA + 384] = np.arange(384)
    for t in range(TILES):
        k[:, C_TOKEN + t] = p + P * t
    k[:, C_EXP:C_EXP + 8] = np.arange(8)
    k[:, C_ROW:C_ROW + 8] = np.arange(8) * (P * TILES)
    return k


def hybrid_step(nc, consts, x_prompt, x_sample, state_lru, cache_k, cache_v, c, c_ctx, norm1_g, norm2_g,
                w_mod, b_mod, w_in, lru_conv_w, lru_conv_b, lru_wa, lru_ba, lru_wx, lru_bx, lru_lam,
                sc_conv_w, sc_conv_b, w_out, ffn_w_gate, ffn_w_up, ffn_w_down, w_qkv, w_o, rpb, w_router,
                moe_w_gate, moe_w_up, moe_w_down, final_g,
                y_prompt, y_sample, new_state, new_k, new_v):
    ctx = ExitStack()
    with ctx:
        def sb(name, shape, dt=F32):
            return ctx.enter_context(nc.sbuf_tensor(name, shape, dt))

        def sem(name):
            return ctx.enter_context(nc.semaphore(name))

        hn_rows = nc.dram_tensor("hn_rows", (P * TILES, D), F32, kind="Internal").ap()
        mod_rows = nc.dram_tensor("mod_rows", (2, 2 * MODS), F32, kind="Internal").ap()
        y_rows = nc.dram_tensor("y_rows", (EXPERTS * P * TILES + P, D), F32, kind="Internal").ap()

        with ExitStack() as first:
            ring = first.enter_context(nc.sbuf_tensor("ring", [P, SLOTS, SLOT], F32))
            mod_extra = first.enter_context(nc.sbuf_tensor("mod_extra", [P, UNIT], F32))
        ring_split = sb("ring_split", [P, SLOTS, SLOT], F32R)
        extra_split = sb("extra_split", [P, UNIT], F32R)
        k_sb = sb("k_sb", [P, N_CONST])
        vec_rows = sb("vec_rows", [P, 2, P])
        cols = sb("cols", [P, P])
        cond = sb("cond", [P, KC, 2])
        modv = sb("modv", [P, 96, 2])
        gains = sb("gains", [P, KC, 2])
        x = sb("x", [P, TILES, D])
        gate_b = sb("gate_b", [P, 2, D])
        stats = sb("stats", [P, 8, 4])
        small = sb("small", [P, 32])
        zeros = sb("zeros", [P, 256])
        router = sb("router", [P, KC, EXPERTS])
        with ExitStack() as first:
            work = first.enter_context(nc.sbuf_tensor("work", [P, WORK], F32))
            xn = first.enter_context(nc.sbuf_tensor("xn", [P, KC * W], F32))
            hn_t = first.enter_context(nc.sbuf_tensor("hn_t", [P, KC, W], F32))
        split = sb("split", [P, 2, 2, KC, 2 * SF], F32R)
        after_split = sb("after_split", [P, WORK - SPLIT])
        hi_x = sb("hi_x", [P, KC * W], F32R)
        lo_x = sb("lo_x", [P, KC * W], F32R)

        assert sum(WIDTH) == D_FF and STEPS % SLOTS == 0 and STEPS % 2 == 0

        def at(off, *dims):
            n = int(np.prod(dims))
            v = work[:, off:off + n]
            if len(dims) == 2:
                v = v.rearrange("p (a b) -> p a b", a=dims[0])
            if len(dims) == 3:
                v = v.rearrange("p (a b c) -> p a b c", a=dims[0], b=dims[1])
            return v

        ident = k_sb[:, C_ID:C_ID + P]
        before = k_sb[:, C_BEFORE:C_BEFORE + P]
        ones = k_sb[:, C_ONES:C_ONES + P]
        xn_tok = xn[:, 0:TILES * D].rearrange("p (t d) -> p t d", t=TILES)
        y_t = xn[:, :].rearrange("p (c w) -> p c w", c=KC)

        PW = W + 3
        xpad = at(0, LC, PW)
        cvpad = at(LC * PW, LC, PW)
        o = 2 * LC * PW
        xc = at(o, LC, W)
        gr = [at(o + (1 + d) * LC * W, LC, W) for d in range(2)]
        gi = [at(o + (3 + d) * LC * W, LC, W) for d in range(2)]
        dec = at(o + 5 * LC * W, LC, W)
        tmp = at(o + 6 * LC * W, LC, W)
        o += 7 * LC * W
        bd = at(o, 16, P)
        o += 16 * P
        sc_conv = xpad[:, :, 0:W]
        lamk = at(o, 2 * LC)
        lamz = at(o + 8, 2 * LC)
        lamp = at(o + 16, 2 * LC)
        st8 = at(o + 24, 8)
        assert o + 32 <= SPLIT
        mod_row = at(SPLIT, GROUP)[0:2, :]
        mod_bias = at(SPLIT + GROUP, GROUP)[0:2, :]
        st_rows = at(SPLIT + 2 * GROUP, P)

        bias = at(0, HEADS * 6, GRID_W)
        o = HEADS * 6 * GRID_W
        q_t = at(o, KC, W)
        kk_t = at(o + KC * W, KC, W + P)
        kc_t = kk_t[:, :, W:W + P]
        v_tok = at(o + 2 * KC * W + D, TILES, D)
        o += 2 * KC * W + TILES * D
        vc = at(o + D, D)
        s_buf = mod_extra[:, 0:768].rearrange("p (a b) -> p a b", a=2)
        p_buf = mod_extra[:, 768:1920].rearrange("p (a b) -> p a b", a=3)
        pt_buf = at(o + 2 * D, 2, 384)
        kc_tok = at(o + 2 * D, D)
        k_out = xn[:, 0:D]
        sums = at(o + 3 * D, TILES, HEADS)
        mx = at(o + 3 * D + 48, 2, 1)
        nmx = at(o + 3 * D + 50, 2, 1)
        assert o + 3 * D + 52 <= WORK

        def step_buffers(off):
            return at(off, SF), at(off + SF, SF), at(off + 2 * SF, 2, P)

        ffn_buf = step_buffers(SPLIT)
        hn_hi = hi_x[:, :].rearrange("p (k w) -> p k w", k=KC)
        hn_lo = lo_x[:, :].rearrange("p (k w) -> p k w", k=KC)

        xg = [mod_extra[:, k * D:(k + 1) * D] for k in range(2)]
        xg_hi, xg_lo = ([v[:, k * D:(k + 1) * D].rearrange("p (c t) -> p c t", c=KC) for k in range(2)]
                        for v in (hi_x, lo_x))
        y_out = [xn[:, 2 * D:3 * D], hn_t[:, :, :].rearrange("p k w -> p (k w)")[:, 2 * D:3 * D]]
        got = [at(0, TILES, D), at(TILES * D, TILES, D)]
        slot_hot = split[:, 1].rearrange("p h k f -> p (h k f)")[:, 0:2 * TILES * 384]\
            .rearrange("p (e t s) -> p e t s", e=2, t=TILES)
        o = SPLIT
        lg, m8, oh1, oh2, mask, rank, rankm, rk_e, pick = (at(o + 24 * n, TILES, EXPERTS) for n in range(9))
        o += 216
        w12 = at(o, 2, TILES)
        e12 = at(o + 6, 2, TILES)
        pos_f = at(o + 12, 2, TILES)
        dv = at(o + 18, TILES)
        cnt_f = at(o + 21, EXPERTS)
        idx_f = at(o + 32, 24)
        moe_buf = step_buffers(o + 64)
        fin_b = at(o + 64 + 3 * SF, D)
        assert o + 64 + 3 * SF + D <= WORK
        h_split = sb("h_split", [P, 2, 2, P], F32R)
        token_ids = sb("token_ids", [P, TILES, 2], F32R)
        i8 = sb("i8", [P, TILES, 8], U32)
        pos_i = sb("pos_i", [P, 6], U32)
        idx_a = sb("idx_a", [P, 17], U32)
        idx_b = sb("idx_b", [P, 17], U32)
        idx_now = sb("idx_now", [P, 2], U32)
        over = sb("over", [1, 24], I32)

        ps = ctx.enter_context(nc.psum_tensor("ps", [P, 8, 512], F32))

        s_const, s_x, s_vec, s_bd, s_cache, s_bias, s_router = (sem("ld_" + n) for n in
            ("const", "x", "vec", "bd", "cache", "bias", "router"))
        s_vc, s_fin = sem("ld_vc"), sem("ld_fin")
        ring_full = [sem(f"ring_full{s}") for s in range(SLOTS)]
        ring_free = [sem(f"ring_free{s}") for s in range(SLOTS)]
        down_full = [sem(f"down_full{s}") for s in range(SLOTS)]
        down_used = sem("down_used")
        hi_ok, lo_ok = sem("split_hi_ok"), sem("split_lo_ok")
        down_hi, down_lo = sem("down_hi_ok"), sem("down_lo_ok")
        ht_hi = sem("hidden_hi_ok")
        hx_hi, hx_lo = sem("tokens_hi_ok"), sem("tokens_lo_ok")
        qkv_hi, qkv_lo = sem("qkv_hi_ok"), sem("qkv_lo_ok")
        mod_full = [sem(f"mod_full{s}") for s in range(4)]
        mod_used = sem("mod_used")
        vec_t, cols_ok, cond_ok = sem("vec_turned"), sem("cols_ok"), sem("cond_ok")
        mod_ok = sem("mod_ok")
        mod_copied, mod_bias_in, mod_row_ok, mod_stored, mod_in = (sem("mod_" + n) for n in
            ("copied", "bias_in", "row_ok", "stored", "rows_in"))
        gains_ok = sem("gains_ok")
        ssq_ok, std_ok, rms_ok = sem("ssq_ok"), sem("std_ok"), sem("rms_ok")
        xn_ok, xn_act = sem("xn_ok"), sem("xn_act_ok")
        var_ok = sem("var_ok")
        nt_done = sem("norm_turned")
        hn_dve, hn_act = sem("hn_dve"), sem("hn_act")
        gap_ok, bdz = sem("gap_ok"), sem("bd_zeroed")
        pj = sem("proj_done")
        ev_d, ev_a = sem("proj_evac_dve"), sem("proj_evac_act")
        lam_e, lam_ok = sem("lam_exp"), sem("lam_ok")
        xc_ok = sem("xc_ok")
        tanh_ok, m_ok, root_ok, mix_ok = sem("tanh_ok"), sem("m_ok"), sem("root_ok"), sem("mix_ok")
        st_ok, st_t, st_out = sem("st_ok"), sem("st_turned"), sem("st_out")
        gb_ok = sem("gate_b_in")
        out_ps, res_ok = sem("mix_product"), sem("residual_ok")
        gu_ready = [sem(f"gu_ready{k}") for k in range(3)]
        silu_ok = [sem(f"silu_ok{k}") for k in range(3)]
        h_ok = [sem(f"h_ok{k}") for k in range(3)]
        h_turned = [sem(f"h_turned{k}") for k in range(3)]
        ht_ok = [sem(f"ht_ok{k}") for k in range(3)]
        ffn_done = sem("ffn_done")
        qk_ps, qk_ok, v_ps, v_ok = sem("qk_ps"), sem("qk_ok"), sem("v_ps"), sem("v_ok")
        kt_ps, kt_ok, ctx_t, ctx_ok = sem("kt_ps"), sem("kt_ok"), sem("ctx_turned"), sem("ctx_ok")
        st_kv = sem("st_kv")
        bias_ok = sem("bias_ok")
        sc_ps, s_ok, max_ok, p_ok, pn_ok, pt_ps, pt_ok, pv = (sem(n) for n in
            ("score_ps", "score_ok", "max_ok", "exp_ok", "prob_ok", "prob_turned", "prob_t_ok", "pv_done"))
        o_ok = sem("o_ok")
        hk_ps, hk_ok, hk_st = sem("hn_tok_ps"), sem("hn_tok_ok"), sem("hn_tok_stored")
        lg_ps, mask_ok, rk_ps, rk_ok = sem("logit_ps"), sem("mask_ok"), sem("rank_ps"), sem("rank_ok")
        hot_ok, hot_used, route_ok = sem("hot_ok"), sem("hot_used"), sem("route_ok")
        idx_ok, gathered, xg_turned, xgt_d, xgt_a = (
            [sem(n + k) for k in "ab"] for n in ("idx_ok", "gathered", "xg_turned", "xg_t_dve_", "xg_t_act_"))
        done, y_d, y_a, y_st = ([sem(n + k) for k in "ab"] for n in ("expert_done_", "y_dve_", "y_act_", "y_stored_"))
        collected = [sem(f"collected{t}") for t in range(TILES)]
        first_ok, pos_ok, weights_ok = sem("first_result_ok"), sem("pos_ok"), sem("weights_ok")
        rounds_over = sem("stores_over")
        y_fin, st_y = sem("y_fin"), sem("st_y")
        v_dve_ok, hk_dve, top_ok, y_ok = sem("v_dve_ok"), sem("hn_tok_dve"), sem("top_ok"), sem("mixer_y_ok")
        qk_dve, ctx_d = sem("qk_dve_ok"), sem("ctx_dve_ok")
        exp_v, st_r, gather_go = sem("gate_exp"), sem("state_rows"), sem("gather_go")
        zero_ok, y_zero = sem("zero_ok"), sem("y_rows_zeroed")
        chain_d, chain_a, chain_p = sem("dve_order"), sem("act_order"), sem("pool_order")

        F_IN, F_OUT, F_FFN = 0, 5, 7
        F_QKV = F_FFN + STEPS
        F_O = F_QKV + 6
        F_MOE = F_O + 2
        n_dma = [1] * F_FFN + [2] * STEPS + [1] * (F_MOE - F_QKV)

        def slot_of(n):
            return n % SLOTS

        def filled(n):
            return 16 * sum(n_dma[m] for m in range(n + 1) if m % SLOTS == n % SLOTS)

        def frees(n):
            return n == F_OUT or n == F_O

        def last_use(n):
            if frees(n):
                return ring_free[slot_of(n)], sum(frees(m) for m in range(n + 1) if m % SLOTS == n % SLOTS)
            if n < F_OUT:
                return pj, first_item["xcvbg"[n]] + 4
            if F_FFN <= n < F_QKV:
                return lo_ok, PIECES * (n - F_FFN + 1)
            if F_QKV <= n < F_QKV + 4:
                return qk_ps, 4 * (n - F_QKV + 1)
            if F_QKV + 4 <= n < F_O:
                return v_ps, 6 * (n - F_QKV - 3)
            return out_ps, TILES * {F_OUT + 1: 1, F_O + 1: 3}[n]

        TURNS = STEPS // SLOTS
        BASE_FULL = [16 * sum(n_dma[m] for m in range(F_MOE) if m % SLOTS == s) for s in range(SLOTS)]

        def mod_slot(s):
            return mod_extra[:, :] if s == 3 else ring[:, s, 2 * UNIT:3 * UNIT]

        def slab(n):
            return ring[:, slot_of(n), 0:4096].rearrange("p (k f) -> p k f", k=KC)

        def gate_up_raw(s, j):
            return ring[:, s, 0:4096].rearrange("p (g x) -> p g x", g=2)[:, :, 0:KC * WIDTH[j]]\
                .rearrange("p g (k f) -> p g k f", k=KC)

        def down_raw(s, j):
            return ring[:, s, 4096:4096 + WIDTH[j] // P * D].rearrange("p (f d) -> p f d", d=D)

        def split_piece(j, s, part, n):
            k = slice(n * KC // PIECES, (n + 1) * KC // PIECES)
            return (gate_up_raw(s, j)[:, :, k, :],
                    split[:, j % 2, part, k, 0:2 * WIDTH[j]].rearrange("p k (g f) -> p g k f", g=2))

        areas = [ring_split[:, s, 4096:6144] for s in range(SLOTS)] + [extra_split[:, :]]

        def qk_split(n, part):
            return areas[n % 4][:, part * D:(part + 1) * D].rearrange("p (k f) -> p k f", k=KC)

        def v_split(n, part):
            return areas[2 * (n % 2) + part].rearrange("p (k f) -> p k f", k=KC)

        def qk_raw(n):
            return slab(F_QKV + n // 4)[:, :, n % 4 * P:(n % 4 + 1) * P]

        def v_raw(n):
            return slab(F_QKV + 4 + n // 2)[:, :, n % 2 * SF:(n % 2 + 1) * SF]

        def down_high(j):
            return extra_split[:, 0:WIDTH[j] // P * D].rearrange("p (f d) -> p f d", d=D)

        def down_low(s, j):
            return ring_split[:, s, 4096:4096 + WIDTH[j] // P * D].rearrange("p (f d) -> p f d", d=D)

        def columns_of(n, t):
            return slice(0, S0) if n == 2 and t == 0 else slice(TOK[t], TOK[t] + P)

        def cols_of(j):
            return slice(START[j], START[j] + WIDTH[j])

        kview = "(k p) f -> p k f"
        IN_ORDER = [0, 3, 4, 2, 1]
        QKV_ORDER = [2, 3, 0, 1, 4, 5]
        MOD_SPLIT = {"x": (4, 6), "c": (6, 8), "v": (8, 10), "b": (10, 12), "g": ()}

        items = []
        for g, (kind, eng) in enumerate((("x", "d"), ("c", "a"), ("gate", "a"), ("v", "d"), ("b", "a"), ("g", "a"))):
            for m in range(16 if kind == "gate" else 4):
                items.append((kind, m, eng))
        ev_n = []
        nd = na = 0
        for kind, m, eng in items:
            nd, na = nd + (eng == "d"), na + (eng == "a")
            ev_n.append((ev_d, nd) if eng == "d" else (ev_a, na))
        first_item = {}
        for n, (kind, m, eng) in enumerate(items):
            first_item.setdefault(kind, n)
        PB = 6

        units = [(t, h) for t in (1, 2, 0) for h in range(HEADS)]

        def reverse(v):
            return v.rearrange("p (t q) -> p t q", t=2)[:, :, ::-1]

        def by_tile(v):
            return v.rearrange("p (t q) -> p t q", t=2)

        block = ctx.enter_context(nc.Block())

        @block.sync
        def _(sp):
            def fill(n, dst, src):
                if n >= SLOTS:
                    sp.wait_ge(*last_use(n - SLOTS))
                sp.dma_start(dst, src).then_inc(ring_full[slot_of(n)], 16)

            def mod_group(src, g, first):
                for s in range(4):
                    if not first:
                        sp.wait_ge(mod_used, g * 4 + (s - 3))
                    sp.dma_start(mod_slot(s).rearrange("p (k f) -> p k f", k=KC),
                                 src(s)).then_inc(mod_full[s], 16)

            sp.wait_ge(s_vec, 16 * 12)
            w0, w1 = (w_mod[l].rearrange(kview, p=P) for l in range(2))
            mod_group(lambda s: w0[:, :, s * 256:(s + 1) * 256], 0, True)
            with sp.Fori(1, 4) as g:
                mod_group(lambda s: w0[:, :, bass.ds((g * 4 + s) * 256, 256)], g, False)
            win = w_in[0].rearrange(kview, p=P)
            for f in range(5):
                g = IN_ORDER[f]
                fill(F_IN + f, slab(F_IN + f), win[:, :, g * 512:(g + 1) * 512])
                if not MOD_SPLIT["xcvbg"[f]]:
                    continue
                lo, hi = MOD_SPLIT["xcvbg"[f]]
                wl, off = (w0, 0) if hi <= 6 else (w1, 6)
                with sp.Fori(lo, hi) as g:
                    mod_group(lambda s: wl[:, :, bass.ds(((g - off) * 4 + s) * 256, 256)], g, False)
            for f in range(2):
                fill(F_OUT + f, slab(F_OUT + f), w_out[0].rearrange(kview, p=P)[:, :, f * 512:(f + 1) * 512])
            wg, wu = ffn_w_gate[0].rearrange(kview, p=P), ffn_w_up[0].rearrange(kview, p=P)
            wd = ffn_w_down[0].rearrange("(f p) d -> p f d", p=P)
            for j in range(STEPS):
                n = F_FFN + j
                s = slot_of(n)
                fill(n, gate_up_raw(s, j)[:, 0], wg[:, :, cols_of(j)])
                sp.dma_start(gate_up_raw(s, j)[:, 1], wu[:, :, cols_of(j)]).then_inc(ring_full[s], 16)
                if j == 0:
                    sp.wait_ge(mod_used, 48)
                if j >= SLOTS:
                    sp.wait_ge(down_used, j - SLOTS + 1)
                sp.dma_start(down_raw(s, j), wd[:, START[j] // P:(START[j] + WIDTH[j]) // P]).then_inc(down_full[s], 16)
            wq = w_qkv[0].rearrange(kview, p=P)
            for f in range(6):
                g = QKV_ORDER[f]
                fill(F_QKV + f, slab(F_QKV + f), wq[:, :, g * 512:(g + 1) * 512])
                if f == SLOTS - 1:
                    sp.wait_ge(out_ps, 2 * TILES)
                    sp.wait_ge(lo_ok, PIECES * STEPS)
                    for h in range(HEADS):
                        for rl in range(2):
                            first = (h * RPB_R + 4 + rl) * RPB_C + (WIN_C - 1) - (GRID_W - 1)
                            src = bass.AP(rpb.tensor, first, [[1, GRID_W], [RPB_C, 6], [1, GRID_W]])
                            sp.dma_start(bias[64 * rl:64 * rl + 64, 6 * h:6 * h + 6, :], src).then_inc(s_bias, 16)
                    sp.wait_ge(st_out, 16)
                    sp.dma_start(kc_tok, cache_k[0, 0].rearrange("h s d -> s h d")).then_inc(s_cache, 16)
                    sp.dma_start(vc, cache_v[0, 0].rearrange("h s d -> s h d")).then_inc(s_vc, 16)
            for f in range(2):
                fill(F_O + f, slab(F_O + f), w_o[0].rearrange(kview, p=P)[:, :, f * 512:(f + 1) * 512])

            wge = moe_w_gate[0].rearrange("e (k p) f -> p e k f", p=P)
            wue = moe_w_up[0].rearrange("e (k p) f -> p e k f", p=P)
            wde = moe_w_down[0].rearrange("e (f p) d -> p e f d", p=P)

            def gate_up_fill(e, j):
                s = slot_of(F_MOE + j)
                for g, wt in enumerate((wge, wue)):
                    sp.dma_start(gate_up_raw(s, j)[:, g], wt[:, bass.ds(e, 1), :, cols_of(j)]
                                 .rearrange("p e k f -> p (e k) f")).then_inc(ring_full[s], 16)

            def down_fill(e, j):
                s = slot_of(F_FFN + j)
                sp.dma_start(down_raw(s, j), wde[:, bass.ds(e, 1), START[j] // P:(START[j] + WIDTH[j]) // P]
                             .rearrange("p e f d -> p (e f) d")).then_inc(down_full[s], 16)

            for j in range(STEPS):
                if j < SLOTS:
                    sp.wait_ge(*last_use(F_MOE + j - SLOTS))
                else:
                    sp.wait_ge(lo_ok, PIECES * (STEPS + j - SLOTS + 1))
                gate_up_fill(0, j)
                if j == 0:
                    sp.wait_ge(out_ps, 2 * TILES)
                else:
                    if j - 1 >= SLOTS:
                        sp.wait_ge(down_used, STEPS - 1 + j - SLOTS)
                    down_fill(0, j - 1)
            sp.wait_ge(route_ok, 1)
            rounds = sp.value_load(over[0:1, 20:21], min_val=EXPERTS, max_val=2 * EXPERTS)
            with sp.Fori(1, rounds) as i:
                e = sp.snap(i % EXPERTS, min_val=0, max_val=EXPERTS - 1)
                e_before = sp.snap((i + (EXPERTS - 1)) % EXPERTS, min_val=0, max_val=EXPERTS - 1)
                for j in range(STEPS):
                    sp.wait_ge(lo_ok, i * (PIECES * STEPS) + PIECES * (STEPS + j - SLOTS + 1))
                    gate_up_fill(e, j)
                    if j == 0:
                        sp.wait_ge(down_used, i * (STEPS - 1) + (STEPS - SLOTS))
                        down_fill(e_before, STEPS - 1)
                        continue
                    d = j - 1
                    if d == SLOTS - 1:
                        sp.wait_ge(done[0], i)
                        sp.wait_ge(done[1], i)
                    else:
                        before_d = d - SLOTS + 1 if d >= SLOTS else d - SLOTS + 2
                        sp.wait_ge(down_used, i * (STEPS - 1) + (STEPS - 1 + before_d))
                    down_fill(e, d)
            sp.wait_ge(down_used, rounds * (STEPS - 1) + (STEPS - SLOTS))
            last_expert = EXPERTS - 1
            s = slot_of(F_FFN + STEPS - 1)
            sp.dma_start(down_raw(s, STEPS - 1), wde[:, last_expert, START[-1] // P:]).then_inc(down_full[s], 16)

        @block.gpsimd
        def _(pool):
            n_chain = [0]

            def ordered(ins):
                n_chain[0] += 1
                ins.then_inc(chain_p, 1)
                pool.wait_ge(chain_p, n_chain[0])

            pool.memset(zeros[:, :], 0.0).then_inc(zero_ok, 1)
            pool.memset(bd, 0.0).then_inc(bdz, 1)
            pool.memset(xpad, 0.0).then_inc(gap_ok, 1)
            pool.memset(cvpad, 0.0).then_inc(gap_ok, 1)
            pool.memset(hn_t[:, :, T_PROMPT:S0], 0.0).then_inc(gap_ok, 1)
            groups = 2 * MODS // GROUP
            bias_rows = b_mod.rearrange("l f -> (l f)")

            def load_mod_bias(g):
                pool.dma_start(mod_bias, bias_rows[g * GROUP:(g + 1) * GROUP].partition_broadcast(2))\
                    .then_inc(mod_bias_in, 16)

            def load_mod_rows(a, b, count):
                pool.wait_ge(mod_stored, 16 * count)
                for g in range(2):
                    pool.dma_start(vec_rows[0:b - a, g, :],
                                   mod_rows[g, a * P:b * P].rearrange("(r p) -> r p", p=P)).then_inc(mod_in, 16)

            load_mod_bias(0)
            for g in range(groups):
                pool.wait_ge(mod_bias_in, 16 * (g + 1))
                pool.wait_ge(mod_copied, 2 * g + 4)
                pool.tensor_tensor(mod_row, mod_row, mod_bias, ALU.add).then_inc(mod_row_ok, 1)
                pool.wait_ge(mod_row_ok, g + 1)
                pool.dma_start(mod_rows[:, g * GROUP:(g + 1) * GROUP], mod_row).then_inc(mod_stored, 16)
                if g + 1 < groups:
                    load_mod_bias(g + 1)
                if (g + 1) * GROUP == SHIFT_SCALE * P:
                    pool.wait_ge(vec_t, 1)
                    load_mod_rows(0, SHIFT_SCALE, g + 1)
            pool.wait_ge(mod_ok, 1)
            load_mod_rows(SHIFT_SCALE, 96, groups)

            pool.wait_ge(s_bias, 16 * 2 * HEADS)
            inside = k_sb[:, C_MASK:C_MASK + GRID_W].unsqueeze(1).to_broadcast([P, HEADS * 6, GRID_W])
            outside = k_sb[:, C_NEG:C_NEG + GRID_W].unsqueeze(1).to_broadcast([P, HEADS * 6, GRID_W])
            ordered(pool.tensor_tensor(bias, bias, inside, ALU.mult))
            pool.tensor_tensor(bias, bias, outside, ALU.add).then_inc(bias_ok, 1)

            pool.wait_ge(route_ok, 1)
            pool.wait_ge(hk_st, 16 * TILES)
            rounds = pool.value_load(over[0:1, 20:21], min_val=EXPERTS, max_val=2 * EXPERTS)

            def gather(k, col):
                table = (idx_a, idx_b)[k]
                pool.tensor_copy(idx_now[:, k:k + 1], table[:, col]).then_inc(idx_ok[k], 1)

            def gather_rows(k):
                pool.indirect_dma_start(
                    out=xg[k], out_offset=None, in_=hn_rows,
                    in_offset=bass.IndirectOffsetOnAxis(ap=idx_now[:, k:k + 1], axis=0),
                ).then_inc(gathered[k], 16)

            for k in range(2):
                gather(k, slice(0, 1))
                pool.wait_ge(idx_ok[k], 1)
                gather_rows(k)
            with pool.Fori(0, rounds) as i:
                for k in range(2):
                    pool.wait_ge(gathered[k], i * 16 + 16)
                    pool.wait_ge(xg_turned[k], i + 1)
                    gather(k, bass.ds(i + 1, 1))
                    pool.wait_ge(idx_ok[k], i + 2)
                    pool.sem_inc(gather_go, 1)
                    gather_rows(k)
            pool.wait_ge(rounds_over, 1)
            pool.wait_ge(pos_ok, 1)
            for t in range(TILES):
                for k in range(2):
                    pool.indirect_dma_start(
                        out=got[k][:, t, :], out_offset=None, in_=y_rows,
                        in_offset=bass.IndirectOffsetOnAxis(ap=pos_i[:, 3 * k + t:3 * k + t + 1], axis=0),
                    ).then_inc(collected[t], 16)
            for t in range(TILES):
                pool.wait_ge(collected[t], 16 * 2)

        @block.scalar
        def _(act):
            n_chain = [0]

            def ordered(ins):
                n_chain[0] += 1
                ins.then_inc(chain_a, 1)
                act.wait_ge(chain_a, n_chain[0])

            act.dma_start(k_sb[:, :], consts).then_inc(s_const, 16)
            rows = []
            for name, src in (("c", c.rearrange("b (r p) -> (b r) p", p=P)),
                              ("c_ctx", c_ctx.rearrange("(r p) -> r p", p=P)),
                              ("norm1", norm1_g.rearrange("l (r p) -> (l r) p", p=P)),
                              ("norm2", norm2_g.rearrange("l (r p) -> (l r) p", p=P)),
                              ("conv_w", lru_conv_w[0].rearrange("k (r p) -> (k r) p", p=P)),
                              ("conv_b", lru_conv_b.rearrange("l (r p) -> (l r) p", p=P)),
                              ("ba", lru_ba[0].rearrange("d (r p) -> (d r) p", p=P)),
                              ("bx", lru_bx[0].rearrange("d (r p) -> (d r) p", p=P)),
                              ("lam", lru_lam[0].rearrange("d (r p) -> (d r) p", p=P)),
                              ("sc_w", sc_conv_w[0].rearrange("k (r p) -> (k r) p", p=P)),
                              ("sc_b", sc_conv_b.rearrange("l (r p) -> (l r) p", p=P)),
                              ("state", state_lru[0, 0].rearrange("d (r p) -> (d r) p", p=P))):
                rows.append((vec_rows[COL[name]:COL[name] + src.shape[0], 0, :], src))
            for dst, src in rows:
                act.dma_start(dst, src).then_inc(s_vec, 16)
            act.dma_start(x[:, 0, :], x_prompt[0]).then_inc(s_x, 16)
            act.dma_start(x[:, 1:3, :], x_sample[0].rearrange("(t p) d -> p t d", p=P)).then_inc(s_x, 16)
            act.wait_ge(bdz, 1)
            for d in range(2):
                for g, wt in enumerate((lru_wa, lru_wx)):
                    for b in range(2):
                        dst = bd[64 * b:64 * b + 64, (2 * d + g) * LC:(2 * d + g + 1) * LC, 64 * b:64 * b + 64]
                        src = wt[0, d].rearrange("(c b) i j -> b i c j", b=2)[b]
                        act.dma_start(dst, src).then_inc(s_bd, 16)
            act.dma_start(router[:, :, :], w_router[0].rearrange("(k p) e -> p k e", p=P)).then_inc(s_router, 16)

            act.wait_ge(cols_ok, 1)
            act.activation(cond[:, :, 0], cols[:, COL["c_ctx"]:COL["c_ctx"] + 8], ACT.Silu).then_inc(cond_ok, 1)
            act.activation(cond[:, :, 1], cols[:, COL["c"]:COL["c"] + 8], ACT.Silu).then_inc(cond_ok, 1)

            def mod_out(*groups):
                for g in groups:
                    if g:
                        act.wait_ge(mod_stored, 16 * g)
                    for hf in range(2):
                        act.wait_ge(mod_used, 4 * g + 2 * hf + 2)
                        act.activation(mod_row[:, 512 * hf:512 * hf + 512], ps[0:2, 6 + hf, :],
                                       ACT.Copy).then_inc(mod_copied, 1)

            def squares(n):
                for t in range(TILES):
                    if n == 0:
                        act.wait_ge(s_x, 32)
                    else:
                        act.wait_ge(res_ok, (n - 1) * TILES + t + 1)
                    if n in (0, 4):
                        dropped = xn_tok[:, t, :]
                    else:
                        free = at(HEADS * 6 * GRID_W, 2, D) if n == 2 else mod_extra[:, :].rearrange("p (a d) -> p a d", a=2)
                        dropped = free[:, t % 2, :]
                        if t == 2:
                            act.wait_ge(ssq_ok, TILES * n + 1)
                    act.activation(dropped, x[:, t, :], ACT.Square,
                                   accum_out=stats[:, n, t:t + 1]).then_inc(ssq_ok, 1)

            def norm(n):
                if n:
                    squares(n)
                act.wait_ge(var_ok, n + 1)
                act.activation(stats[:, n, 0:3], stats[:, n, 0:3], ACT.Sqrt).then_inc(std_ok, 1)
                if n == 4:
                    return
                act.wait_ge(rms_ok, n + 1)
                act.activation(xn_tok[:, 1, :], x[:, 1, :], ACT.Copy, scale=stats[:, n, 1:2]).then_inc(xn_act, 1)
                if n == 0:
                    mod_out(3)
                act.wait_ge(gains_ok, n + 1)
                base = (n // 2) * 48 + (n % 2) * 24
                for ci in range(KC):
                    if ci % 2:
                        act.wait_ge(nt_done, n * KC + ci + 1)
                        for g, (lo, hi, plo) in enumerate(((0, T_PROMPT, 0), (S0, W, P))):
                            ins = act.activation(hn_t[:, ci, lo:hi], ps[:, ci, plo:plo + hi - lo], ACT.Identity,
                                                 bias=modv[:, base + ci, g:g + 1], scale=gains[:, ci, g:g + 1])
                        ins.then_inc(hn_act, 1)

            def gate_in(n):
                at_ = (n // 2) * MODS + (3 * (n % 2) + 2) * D
                if n:
                    act.wait_ge(res_ok, n * TILES)
                else:
                    act.wait_ge(mod_stored, 16 * (2 * MODS // GROUP))
                for g in range(2):
                    act.dma_start(gate_b[:, g, :], mod_rows[g, at_:at_ + D].partition_broadcast(P)).then_inc(gb_ok, 16)

            act.sem_inc(mod_copied, 2)
            squares(0)
            mod_out(0, 1, 2)
            norm(0)
            act.wait_ge(lam_e, 1)
            act.activation(lamz, lamz, ACT.Exp).then_inc(lam_e, 1)

            mods_before = {"c": (4, 5), "gate": (6, 7), "g": (10, 11)}
            for n, (kind, m, eng) in enumerate(items):
                if eng != "a":
                    continue
                if m == 0 and kind in mods_before:
                    mod_out(*mods_before[kind])
                act.wait_ge(pj, n + 1)
                src = ps[:, n % PB, 0:W]
                if kind == "c":
                    act.wait_ge(gap_ok, 3)
                    ins = act.activation(cvpad[:, m, 2:2 + W], src, ACT.Copy)
                elif kind == "gate":
                    d, g, ch = m // 8, m // 4 % 2, m % 4
                    dst = (gr, gi)[g][d]
                    col = COL[("ba", "bx")[g]] + d * LC + ch
                    ins = act.activation(dst[:, ch, :], src, ACT.Sigmoid, bias=cols[:, col:col + 1])
                elif kind == "b":
                    ins = act.activation(y_t[:, LC + m, :], src, ACT.Copy)
                else:
                    ins = act.activation(y_t[:, m, :], src, ACT.Gelu_apprx_tanh)
                ins.then_inc(ev_a, 1)
                if kind == "gate" and m == 15:
                    act.wait_ge(lam_ok, 1)
                    for d in range(2):
                        if d:
                            act.wait_ge(mix_ok, 1)
                        act.wait_ge(ev_a, [v for (s, v), it in zip(ev_n, items) if it[:2] == ("gate", 15)][0])
                        for ch in range(LC):
                            act.activation(dec[:, ch, :], gr[d][:, ch, :], ACT.Exp,
                                           scale=lamk[:, d * LC + ch:d * LC + ch + 1])
                        for ch in range(LC):
                            ins = act.activation(gr[d][:, ch, :], gr[d][:, ch, :], ACT.Tanh,
                                                 scale=lamk[:, d * LC + ch:d * LC + ch + 1])
                        ins.then_inc(tanh_ok, 1)
                        act.wait_ge(m_ok, d + 1)
                        act.activation(gr[d], gr[d], ACT.Sqrt).then_inc(root_ok, 1)
                        mod_out(8 + d)

            gate_in(0)
            act.wait_ge(zero_ok, 1)
            busy = [y_rows[(e * TILES + 1) * P:(e + 1) * TILES * P, :] for e in range(EXPERTS)]
            for dst in (*busy, y_rows[EXPERTS * TILES * P:, :]):
                dst = dst.rearrange("(p r) (q f) -> p (r q) f", p=P, f=256)
                act.dma_start(dst, zeros[:, :].unsqueeze(1).to_broadcast([P, dst.shape[1], 256])).then_inc(y_zero, 16)
            act.wait_ge(st_r, 1)
            act.dma_start(new_state[0, 0].rearrange("d (r p) -> (d r) p", p=P), st_rows[0:8, :]).then_inc(st_out, 16)

            def split_high(j, s):
                for n in range(PIECES):
                    raw, high = split_piece(j, s, 0, n)
                    act.activation(high, raw, ACT.Copy).then_inc(hi_ok, 1)

            def split_high_ffn(j):
                n = F_FFN + j
                act.wait_ge(ring_full[slot_of(n)], filled(n))
                split_high(j, slot_of(n))

            def tokens_high(n):
                act.wait_ge(nt_done, (n + 1) * KC)
                act.wait_ge(hn_dve, (n + 1) * 4)
                act.wait_ge(hn_act, (n + 1) * 4)
                for t in range(TILES):
                    tok = columns_of(n, t)
                    act.activation(hn_hi[:, :, tok], hn_t[:, :, tok], ACT.Copy).then_inc(hx_hi, 1)

            act.wait_ge(y_ok, 1)
            act.wait_ge(st_t, 1)
            split_high_ffn(0)
            norm(1)
            tokens_high(1)
            split_high_ffn(1)

            gate_in(1)

            def silu(k, j, count, buf):
                act.wait_ge(gu_ready[k], count + 1)
                act.activation(buf[0][:, 0:WIDTH[j]], ps[:, 0, 0:WIDTH[j]], ACT.Silu).then_inc(silu_ok[k], 1)

            for j in range(STEPS):
                for k in range(TILES):
                    silu(k, j, j, ffn_buf)
                    act.wait_ge(h_turned[k], j + 1)
                    act.activation(h_split[:, 0, 0:WIDTH[j] // P, :],
                                   ps[:, 1, 0:WIDTH[j]].rearrange("p (f t) -> p f t", t=P), ACT.Copy).then_inc(ht_hi, 1)
                    if k == 0:
                        act.wait_ge(down_full[slot_of(F_FFN + j)], 16 * (j // SLOTS + 1))
                        if j:
                            act.wait_ge(down_used, j)
                        for f in range(WIDTH[j] // P):
                            act.activation(down_high(j)[:, f, :], down_raw(slot_of(F_FFN + j), j)[:, f, :],
                                           ACT.Copy).then_inc(down_hi, 1)
                if j + 2 < STEPS:
                    split_high_ffn(j + 2)

            norm(2)
            tokens_high(2)
            gate_in(2)

            def high(raw, dst):
                act.activation(dst, raw, ACT.Copy).then_inc(qkv_hi, 1)

            for n in range(-4, 16):
                if n >= 0 and n % 2:
                    act.wait_ge(qk_ps, n + 1)
                    m = n % 8
                    if n < 8:
                        act.activation(kk_t[:, m, 0:W], ps[:, n % 6, 0:W], ACT.Copy).then_inc(qk_ok, 1)
                    else:
                        act.activation(q_t[:, m, 0:P], ps[:, n % 6, 0:P], ACT.Copy, scale=HD ** -0.5)
                        act.activation(by_tile(q_t[:, m, S0:W]), reverse(ps[:, n % 6, S0:W]), ACT.Copy,
                                       scale=HD ** -0.5).then_inc(qk_ok, 1)
                if n + 4 < 16:
                    if n >= 0:
                        act.wait_ge(qk_ps, n + 1)
                    if (n + 4) % 4 == 0:
                        f = F_QKV + (n + 4) // 4
                        act.wait_ge(ring_full[slot_of(f)], filled(f))
                    high(qk_raw(n + 4), qk_split(n + 4, 0))
            for n in range(4):
                if n % 2 == 0:
                    f = F_QKV + 4 + n // 2
                    act.wait_ge(ring_full[slot_of(f)], filled(f))
                if n >= 2:
                    act.wait_ge(v_ps, 3 * (n - 1))
                high(v_raw(n), v_split(n, 0))
            for n in range(6):
                if n % 2:
                    f, t = n // 3, n % 3
                    act.wait_ge(v_ps, 6 * f + 3 + t + 1)
                    act.activation(v_tok[:, t, f * 512:(f + 1) * 512], ps[:, n, :], ACT.Copy).then_inc(v_ok, 1)
            act.wait_ge(v_ok, 3)
            act.wait_ge(v_dve_ok, 3)
            act.dma_start(new_v[0, 0].rearrange("h s d -> s h d"),
                          v_tok[:, 0, :].rearrange("p (h d) -> p h d", h=HEADS)).then_inc(st_kv, 16)
            act.wait_ge(kt_ok, 1)
            act.dma_start(new_k[0, 0].rearrange("h s d -> s h d"),
                          k_out.rearrange("p (h d) -> p h d", h=HEADS)).then_inc(st_kv, 16)

            act.wait_ge(ctx_t, 1)
            act.activation(kc_t[:, 4:8, :], ps[:, 7, :].rearrange("p (a b) -> p a b", a=4), ACT.Copy).then_inc(ctx_ok, 1)
            def prob_turned(u):
                n = 384 if units[u][0] else P
                act.wait_ge(pt_ps, u + 1)
                if u >= 2:
                    act.wait_ge(pv, u - 1)
                act.activation(pt_buf[:, u % 2, 0:n], ps[:, 2 + u % 2, 0:n], ACT.Copy).then_inc(pt_ok, 1)

            for u, (t, h) in enumerate(units):
                n = 384 if t else P
                act.wait_ge(max_ok, u + 1)
                if u >= 3:
                    act.wait_ge(pt_ps, u - 2)
                act.activation(p_buf[:, u % 3, 0:n], s_buf[:, u % 2, 0:n], ACT.Exp, bias=nmx[:, u % 2, :],
                               accum_out=sums[:, t, h:h + 1]).then_inc(p_ok, 1)
                if u >= 2:
                    prob_turned(u - 2)
            prob_turned(len(units) - 2)
            prob_turned(len(units) - 1)

            norm(3)
            act.wait_ge(ring_full[slot_of(F_MOE)], BASE_FULL[slot_of(F_MOE)] + 32)
            split_high(0, slot_of(F_MOE))
            for n in range(6):
                if n % 2:
                    act.wait_ge(hk_ps, n + 1)
                    t, hf = n // 2, n % 2
                    act.activation(xn_tok[:, t, hf * 512:(hf + 1) * 512], ps[:, n, :], ACT.Copy).then_inc(hk_ok, 1)
                    act.wait_ge(hk_ok, t + 1)
                    act.wait_ge(hk_dve, t + 1)
                    act.dma_start(hn_rows[t * P:(t + 1) * P, :], xn_tok[:, t, :]).then_inc(hk_st, 16)
            act.wait_ge(st_kv, 32)
            act.dma_start(fin_b, final_g.partition_broadcast(P)).then_inc(s_fin, 16)
            act.wait_ge(top_ok, 1)
            act.activation(dv, dv, ACT.Exp).then_inc(exp_v, 1)
            gate_in(3)

            act.wait_ge(route_ok, 1)
            act.wait_ge(ring_full[slot_of(F_MOE + 1)], BASE_FULL[slot_of(F_MOE + 1)] + 32)
            split_high(1, slot_of(F_MOE + 1))
            rounds = act.value_load(over[0:1, 20:21], min_val=EXPERTS, max_val=2 * EXPERTS)

            def turned_in(k, count):
                act.wait_ge(xg_turned[k], count)
                for hf in range(2):
                    ins = act.activation(xg_hi[k][:, 4 * hf:4 * hf + 4, :],
                                         ps[:, 6 + hf, :].rearrange("p (a b) -> p a b", a=4), ACT.Copy)
                ins.then_inc(xgt_a[k], 1)

            turned_in(0, 1)
            act.wait_ge(y_zero, 16 * (EXPERTS + 1))
            for k in range(2):
                act.sem_inc(y_a[k], 1)
                act.sem_inc(y_st[k], 16)
            with act.Fori(0, rounds) as i:
                e = act.snap(i % EXPERTS, min_val=0, max_val=EXPERTS - 1)
                row = act.snap(e * (P * TILES) + (i // EXPERTS) * (2 * P), min_val=0,
                               max_val=EXPERTS * P * TILES - P)
                more = act.value_load(over[0:1, bass.ds(i, 1)])

                left = act.snap(rounds - i, min_val=1, max_val=2 * EXPERTS)

                def split_ahead(j, of_round):
                    s = slot_of(F_MOE + j)
                    act.wait_ge(ring_full[s], of_round * (32 * TURNS) + (BASE_FULL[s] + 32 * (j // SLOTS + 1)))
                    split_high(j, s)

                def moe_round(ks):
                    if 1 in ks:
                        turned_in(1, i + 1)
                    for j in range(STEPS):
                        for k in ks:
                            silu(k, j, i * STEPS + (STEPS + j), moe_buf)
                        if j + 2 < STEPS:
                            split_ahead(j + 2, i)
                        else:
                            if j == STEPS - 1:
                                turned_in(0, i + 2)
                            with act.If(left > 1):
                                split_ahead(j + 2 - STEPS, i + 1)
                    for k in ks:
                        act.wait_ge(y_st[k], i * 16 + 16)
                        act.wait_ge(done[k], i + 1)
                        act.activation(y_out[k][:, 512:1024], ps[:, 3 + 2 * k, :], ACT.Copy).then_inc(y_a[k], 1)
                    for k in ks:
                        act.wait_ge(y_a[k], i + 2)
                        act.wait_ge(y_d[k], i + 2)
                        act.dma_start(y_rows[bass.ds(row + P * k, P), :], y_out[k]).then_inc(y_st[k], 16)

                with act.If(more > 0):
                    moe_round((0, 1))
                with act.Else():
                    moe_round((0,))
                    act.sem_inc(xgt_a[1], 1)
                    act.sem_inc(silu_ok[1], STEPS)
                    act.sem_inc(y_a[1], 1)
                    act.sem_inc(y_st[1], 16)
                act.nop()
            act.wait_ge(y_st[0], rounds * 16 + 16)
            act.wait_ge(y_st[1], rounds * 16 + 16)
            act.sem_inc(rounds_over, 1)
            act.wait_ge(weights_ok, 1)
            for t in range(TILES):
                act.wait_ge(collected[t], 16 * 2)
                act.activation(got[0][:, t, :], got[0][:, t, :], ACT.Copy, scale=w12[:, 0, t:t + 1]).then_inc(first_ok, 1)
            norm(4)
            for t in range(TILES):
                act.wait_ge(y_fin, t + 1)
                dst = y_prompt[0] if t == 0 else y_sample[0, (t - 1) * P:t * P, :]
                act.dma_start(dst, xn_tok[:, t, :]).then_inc(st_y, 16)
            act.wait_ge(st_y, 16 * TILES)
            act.wait_ge(st_kv, 32)
            act.wait_ge(st_out, 16)

        @block.vector
        def _(dve):
            n_chain = [0]

            def ordered(ins):
                n_chain[0] += 1
                ins.then_inc(chain_d, 1)
                dve.wait_ge(chain_d, n_chain[0])

            def col(name, n):
                return cols[:, COL[name] + n:COL[name] + n + 1]

            def mod_columns(a, b, bank):
                dve.wait_ge(vec_t, 2 if a == 0 else 3)
                dve.tensor_copy(modv[:, a:b, :],
                                ps[:, bank, 0:2 * P].rearrange("p (g m) -> p m g", g=2)[:, 0:b - a, :]).then_inc(mod_ok, 1)

            def set_gains(n):
                base = (n // 2) * 48 + (n % 2) * 24 + 8
                name = ("norm1", "norm2")[n % 2]
                g0 = COL[name] + 8 * (n // 2)
                if n:
                    dve.wait_ge(hn_act, 4 * n)
                dve.scalar_tensor_tensor(out=gains[:, :, :], in0=modv[:, base:base + 8, :], scalar=1.0,
                                         in1=cols[:, g0:g0 + 8].unsqueeze(2).to_broadcast([P, 8, 2]),
                                         op0=ALU.add, op1=ALU.mult).then_inc(gains_ok, 1)

            def norm(n):
                if n < 4:
                    set_gains(n)
                dve.wait_ge(ssq_ok, TILES * (n + 1))
                st = stats[:, n, 0:3]
                dve.tensor_scalar(st, st, 1.0 / D, EPS, ALU.mult, ALU.add).then_inc(var_ok, 1)
                dve.wait_ge(std_ok, n + 1)
                dve.reciprocal(st, st).then_inc(rms_ok, 1)
                dve.wait_ge(rms_ok, n + 1)
                if n == 4:
                    return
                for t in (0, 2):
                    dve.tensor_scalar(xn_tok[:, t, :], x[:, t, :], stats[:, n, t:t + 1], None, ALU.mult).then_inc(xn_ok, 1)
                base = (n // 2) * 48 + (n % 2) * 24
                dve.wait_ge(gains_ok, n + 1)
                for ci in range(0, KC, 2):
                    dve.wait_ge(nt_done, n * KC + ci + 1)
                    for g, (lo, hi, plo) in enumerate(((0, T_PROMPT, 0), (S0, W, P))):
                        ins = dve.tensor_scalar(hn_t[:, ci, lo:hi], ps[:, ci, plo:plo + hi - lo],
                                                gains[:, ci, g:g + 1], modv[:, base + ci, g:g + 1], ALU.mult, ALU.add)
                    ins.then_inc(hn_dve, 1)

            def residual(n, bank, tiles=range(TILES)):
                dve.wait_ge(gb_ok, 32 * (n + 1))
                for t in tiles:
                    dve.wait_ge(out_ps, n * TILES + t + 1)
                    for hf in range(2):
                        lo, hi = hf * 512, hf * 512 + 512
                        b = ps[:, bank(t, hf), :]
                        dve.tensor_tensor(b, b, gate_b[:, min(t, 1), lo:hi], ALU.mult).then_inc(chain_d, 1)
                        n_chain[0] += 1
                    dve.wait_ge(chain_d, n_chain[0])
                    for hf in range(2):
                        lo, hi = hf * 512, hf * 512 + 512
                        ins = dve.tensor_tensor(x[:, t, lo:hi], x[:, t, lo:hi], ps[:, bank(t, hf), :], ALU.add)
                        if hf == 0:
                            n_chain[0] += 1
                            ins.then_inc(chain_d, 1)
                        else:
                            ins.then_inc(res_ok, 1)

            dve.wait_ge(vec_t, 1)
            dve.tensor_copy(cols[:, 0:N_COLS], ps[:, 0, 0:N_COLS]).then_inc(cols_ok, 1)
            dve.wait_ge(cols_ok, 1)

            lam = cols[:, COL["lam"]:COL["lam"] + 2 * LC]
            ordered(dve.scalar_tensor_tensor(out=lamz, in0=lam, scalar=-1.0, in1=lam, op0=ALU.mult, op1=ALU.min))
            dve.tensor_scalar(lamp, lam, -1.0, 0.0, ALU.mult, ALU.max).then_inc(lam_e, 1)
            mod_columns(0, SHIFT_SCALE, 0)
            dve.wait_ge(mod_ok, 1)
            dve.wait_ge(s_x, 32)
            norm(0)
            dve.wait_ge(lam_e, 2)
            ordered(dve.tensor_scalar(lamk, lamz, 2.0, None, ALU.add))
            ordered(dve.reciprocal(lamk, lamk))
            ordered(dve.tensor_tensor(lamz, lamz, lamk, ALU.mult))
            zz, acc = small[:, 0:8], small[:, 8:16]
            ordered(dve.tensor_tensor(zz, lamz, lamz, ALU.mult))
            ordered(dve.tensor_scalar(acc, zz, 1.0 / 17, 1.0 / 15, ALU.mult, ALU.add))
            for n in (13, 11, 9, 7, 5, 3, 1):
                ordered(dve.tensor_tensor(acc, acc, zz, ALU.mult))
                ordered(dve.tensor_scalar(acc, acc, 1.0 / n, None, ALU.add))
            ordered(dve.tensor_tensor(acc, acc, lamz, ALU.mult))
            ordered(dve.scalar_tensor_tensor(out=acc, in0=acc, scalar=2.0, in1=lamp, op0=ALU.mult, op1=ALU.add))
            dve.tensor_scalar(lamk, acc, -LRU_C, None, ALU.mult).then_inc(lam_ok, 1)

            dve.wait_ge(gap_ok, 3)
            for m in range(LC):
                n = first_item["x"] + m
                dve.wait_ge(pj, n + 1)
                dve.tensor_copy(xpad[:, m, 2:2 + W], ps[:, n % PB, 0:W]).then_inc(ev_d, 1)
                dve.wait_ge(ev_d, ev_n[n][1])
                ordered(dve.tensor_scalar(xc[:, m, :], xpad[:, m, 0:W], col("conv_w", m), col("conv_b", m),
                                          ALU.mult, ALU.add))
                for k in range(1, 4):
                    ins = dve.scalar_tensor_tensor(out=xc[:, m, :], in0=xpad[:, m, k:k + W],
                                                   scalar=col("conv_w", 4 * k + m), in1=xc[:, m, :],
                                                   op0=ALU.mult, op1=ALU.add)
                    if k < 3:
                        ordered(ins)
                ins.then_inc(xc_ok, 1)
            dve.wait_ge(xc_ok, LC)
            for d in range(2):
                dve.wait_ge(tanh_ok, d + 1)
                ordered(dve.tensor_scalar(tmp, gr[d], -1.0, None, ALU.add))
                ordered(dve.reciprocal(tmp, tmp))
                dve.scalar_tensor_tensor(out=gr[d], in0=gr[d], scalar=2.0, in1=tmp,
                                         op0=ALU.mult, op1=ALU.mult).then_inc(m_ok, 1)
                ordered(dve.tensor_tensor(gi[d], gi[d], xc, ALU.mult))
                dve.wait_ge(root_ok, d + 1)
                ordered(dve.tensor_tensor(gi[d], gi[d], gr[d], ALU.mult))
                at_gap = S0 - 1 if d == 0 else T_PROMPT
                ordered(dve.memset(dec[:, :, at_gap:at_gap + 1], 0.0))
                if d == 0:
                    st0 = COL["state"]
                    ordered(dve.tensor_copy(gi[d][:, :, at_gap:at_gap + 1], cols[:, st0:st0 + LC].unsqueeze(2)))
                else:
                    ordered(dve.memset(gi[d][:, :, at_gap:at_gap + 1], 0.0))
                for m in range(LC):
                    if d == 0:
                        ins = dve.tensor_tensor_scan(gr[d][:, m, :], dec[:, m, :], gi[d][:, m, :], 0.0, ALU.mult, ALU.add)
                    else:
                        ins = dve.tensor_tensor_scan(gr[d][:, m, ::-1], dec[:, m, ::-1], gi[d][:, m, ::-1],
                                                     col("state", LC + m), ALU.mult, ALU.add)
                    ordered(ins)
                dve.sem_inc(mix_ok, 1)
            dve.tensor_copy(st8[:, 0:LC], gr[0][:, :, T_PROMPT - 1]).then_inc(st_ok, 1)
            dve.tensor_copy(st8[:, LC:2 * LC], gr[1][:, :, 0]).then_inc(st_ok, 1)
            ordered(dve.tensor_tensor(tmp, gr[0], gr[1], ALU.add))
            for m in range(LC):
                n = first_item["v"] + m
                dve.wait_ge(pj, n + 1)
                dve.wait_ge(ev_a, ev_n[first_item["c"] + m][1])
                dve.tensor_tensor(cvpad[:, m, 2:2 + W], cvpad[:, m, 2:2 + W], ps[:, n % PB, 0:W],
                                  ALU.mult).then_inc(ev_d, 1)
                dve.wait_ge(ev_d, ev_n[n][1])
                ordered(dve.tensor_scalar(sc_conv[:, m, :], cvpad[:, m, 1:1 + W], col("sc_w", m), col("sc_b", m),
                                          ALU.mult, ALU.add))
                for k in range(1, 3):
                    ordered(dve.scalar_tensor_tensor(out=sc_conv[:, m, :], in0=cvpad[:, m, 1 + k:1 + k + W],
                                                     scalar=col("sc_w", 4 * k + m), in1=sc_conv[:, m, :],
                                                     op0=ALU.mult, op1=ALU.add))
            dve.wait_ge(ev_a, ev_n[first_item["b"] + 3][1])
            ordered(dve.tensor_tensor(y_t[:, LC:KC, :], y_t[:, LC:KC, :], sc_conv, ALU.mult))
            dve.wait_ge(ev_a, ev_n[first_item["g"] + 3][1])
            dve.tensor_tensor(y_t[:, 0:LC, :], y_t[:, 0:LC, :], tmp, ALU.mult).then_inc(y_ok, 1)
            dve.wait_ge(st_t, 1)
            dve.tensor_copy(st_rows[0:8, :], ps[0:8, 7, 0:P]).then_inc(st_r, 1)

            def split_low(j, s, count, pieces):
                for n in pieces:
                    raw, high = split_piece(j, s, 0, n)
                    _, low = split_piece(j, s, 1, n)
                    dve.wait_ge(hi_ok, count + (n + 1))
                    dve.tensor_tensor(low, raw, high.bitcast(F32), ALU.subtract).then_inc(lo_ok, 1)

            def split_low_ffn(j, pieces):
                split_low(j, slot_of(F_FFN + j), PIECES * j, pieces)

            def tokens_low(n):
                dve.wait_ge(nt_done, (n + 1) * KC)
                for t in range(TILES):
                    tok = columns_of(n, t)
                    dve.wait_ge(hx_hi, (n - 1) * TILES + t + 1)
                    dve.tensor_tensor(hn_lo[:, :, tok], hn_t[:, :, tok], hn_hi[:, :, tok].bitcast(F32),
                                      ALU.subtract).then_inc(hx_lo, 1)

            split_low_ffn(0, range(PIECES))
            mod_columns(SHIFT_SCALE, 96, 6)
            residual(0, lambda t, hf: 3 * hf + t)
            dve.wait_ge(mod_ok, 2)

            norm(1)
            tokens_low(1)
            split_low_ffn(1, range(PIECES))

            def hidden(k, j, count, buf):
                w = WIDTH[j]
                dve.wait_ge(silu_ok[k], count + 1)
                dve.tensor_tensor(buf[1][:, 0:w], buf[0][:, 0:w], ps[:, 0, w:2 * w], ALU.mult).then_inc(h_ok[k], 1)

            def hidden_turned(k, j, count, buf):
                w = WIDTH[j]
                dve.wait_ge(h_turned[k], count + 1)
                dve.tensor_copy(buf[2][:, 0:w // P, :], ps[:, 1, 0:w].rearrange("p (f t) -> p f t", t=P))\
                    .then_inc(ht_ok[k], 1)

            for j in range(STEPS):
                for k in range(TILES):
                    ahead = k == TILES - 1 and j + 2 < STEPS
                    hidden(k, j, j, ffn_buf)
                    if ahead:
                        split_low_ffn(j + 2, range(0, PIECES // 2))
                    f_n = WIDTH[j] // P
                    dve.wait_ge(ht_hi, TILES * j + k + 1)
                    dve.tensor_tensor(h_split[:, 1, 0:f_n, :], ps[:, 1, 0:WIDTH[j]].rearrange("p (f t) -> p f t", t=P),
                                      h_split[:, 0, 0:f_n, :].bitcast(F32), ALU.subtract).then_inc(ht_ok[k], 1)
                    if k == 0:
                        s = slot_of(F_FFN + j)
                        for f in range(f_n):
                            dve.wait_ge(down_hi, START[j] // P + f + 1)
                            dve.tensor_tensor(down_low(s, j)[:, f, :], down_raw(s, j)[:, f, :],
                                              down_high(j)[:, f, :].bitcast(F32), ALU.subtract).then_inc(down_lo, 1)
                    if ahead:
                        split_low_ffn(j + 2, range(PIECES // 2, PIECES))
                    if j == STEPS - 1 and k:
                        residual(1, lambda t, hf: 2 + 2 * t + hf, (k - 1,))
            residual(1, lambda t, hf: 2 + 2 * t + hf, (TILES - 1,))

            norm(2)
            tokens_low(2)

            def low(raw, hi, dst, count):
                dve.wait_ge(qkv_hi, count)
                dve.tensor_tensor(dst, raw, hi.bitcast(F32), ALU.subtract).then_inc(qkv_lo, 1)

            for n in range(-4, 16):
                if n >= 0 and n % 2 == 0:
                    dve.wait_ge(qk_ps, n + 1)
                    m = n % 8
                    if n < 8:
                        dve.tensor_copy(kk_t[:, m, 0:W], ps[:, n % 6, 0:W]).then_inc(qk_dve, 1)
                    else:
                        dve.tensor_scalar(q_t[:, m, 0:P], ps[:, n % 6, 0:P], HD ** -0.5, None, ALU.mult)
                        dve.tensor_scalar(by_tile(q_t[:, m, S0:W]), reverse(ps[:, n % 6, S0:W]), HD ** -0.5, None,
                                          ALU.mult).then_inc(qk_dve, 1)
                if n + 4 < 16:
                    low(qk_raw(n + 4), qk_split(n + 4, 0), qk_split(n + 4, 1), n + 5)
            for n in range(4):
                low(v_raw(n), v_split(n, 0), v_split(n, 1), 16 + n + 1)
            for n in range(0, 6, 2):
                f, t = n // 3, n % 3
                dve.wait_ge(v_ps, 6 * f + 3 + t + 1)
                dve.tensor_copy(v_tok[:, t, f * 512:(f + 1) * 512], ps[:, n, :]).then_inc(v_dve_ok, 1)
            dve.wait_ge(kt_ps, 1)
            dve.tensor_copy(k_out, ps[:, 6:8, :].rearrange("p a b -> p (a b)")).then_inc(kt_ok, 1)
            dve.wait_ge(ctx_t, 1)
            dve.tensor_copy(kc_t[:, 0:4, :], ps[:, 6, :].rearrange("p (a b) -> p a b", a=4)).then_inc(ctx_d, 1)

            def divide(u):
                t, h = units[u]
                n = 384 if t else P
                dve.wait_ge(p_ok, u + 1)
                ordered(dve.reciprocal(sums[:, t, h:h + 1], sums[:, t, h:h + 1]))
                dve.tensor_scalar(p_buf[:, u % 3, 0:n], p_buf[:, u % 3, 0:n], sums[:, t, h:h + 1], None,
                                  ALU.mult).then_inc(pn_ok, 1)

            def output_in(ti, tt):
                dve.wait_ge(pv, HEADS * (ti + 1))
                src = ps[:, 4 + 2 * (ti % 2):6 + 2 * (ti % 2), :].rearrange("p a (c q) -> p (a c) q", q=P)
                dve.tensor_copy(hn_t[:, :, TOK[tt]:TOK[tt] + P], src[:, :, ::-1] if tt else src).then_inc(o_ok, 1)

            dve.wait_ge(bias_ok, 1)
            for u, (t, h) in enumerate(units):
                n = 384 if t else P
                dve.wait_ge(sc_ps, u + 1)
                if u >= 2:
                    dve.wait_ge(p_ok, u - 1)
                if t:
                    j0 = 6 * h + 2 - 2 * (t - 1)
                    dve.tensor_tensor(s_buf[:, u % 2, 0:256].rearrange("p (a b) -> p a b", a=4),
                                      ps[:, u % 2, 0:256].rearrange("p (a b) -> p a b", a=4),
                                      bias[:, j0:j0 + 4, :], ALU.add).then_inc(s_ok, 1)
                    dve.tensor_copy(s_buf[:, u % 2, 256:384], ps[:, u % 2, 256:384]).then_inc(s_ok, 1)
                else:
                    dve.sem_inc(s_ok, 1)
                    dve.tensor_copy(s_buf[:, u % 2, 0:P], ps[:, u % 2, 0:P]).then_inc(s_ok, 1)
                dve.wait_ge(s_ok, 2 * u + 2)
                ordered(dve.tensor_reduce(mx[:, u % 2, :], s_buf[:, u % 2, 0:n], AX_X, ALU.max))
                dve.tensor_scalar(nmx[:, u % 2, :], mx[:, u % 2, :], -1.0, None, ALU.mult).then_inc(max_ok, 1)
                if u:
                    divide(u - 1)
                for ti, tt in enumerate((1, 2)):
                    if u == HEADS * (ti + 1) + 4:
                        output_in(ti, tt)
            divide(len(units) - 1)
            output_in(2, 0)
            dve.wait_ge(st_kv, 32)
            residual(2, lambda t, hf: 3 * hf + t)

            norm(3)
            split_low(0, slot_of(F_MOE), PIECES * STEPS, range(PIECES))
            for n in range(0, 6, 2):
                dve.wait_ge(hk_ps, n + 1)
                t, hf = n // 2, n % 2
                dve.tensor_copy(xn_tok[:, t, hf * 512:(hf + 1) * 512], ps[:, n, :]).then_inc(hk_dve, 1)

            dve.wait_ge(lg_ps, 1)
            dve.wait_ge(st_kv, 32)
            ordered(dve.tensor_copy(lg, ps[:, 6, 0:24].rearrange("p (t e) -> p t e", t=TILES)))
            for t in range(TILES):
                ordered(dve.max(m8[:, t, :], lg[:, t, :]))
                ordered(dve.max_index(i8[:, t, :], m8[:, t, :], lg[:, t, :]))
            dve.tensor_tensor(dv, m8[:, :, 1], m8[:, :, 0], ALU.subtract).then_inc(top_ok, 1)
            experts = k_sb[:, C_EXP:C_EXP + 8].unsqueeze(1).to_broadcast([P, TILES, EXPERTS])
            for k, oh in enumerate((oh1, oh2)):
                ordered(dve.tensor_copy(e12[:, k, :], i8[:, :, k]))
                ordered(dve.tensor_tensor(oh, experts, e12[:, k, :].unsqueeze(2).to_broadcast([P, TILES, EXPERTS]),
                                          ALU.is_equal))
            dve.tensor_tensor(mask, oh1, oh2, ALU.add).then_inc(mask_ok, 1)
            dve.wait_ge(rk_ps, 1)
            ordered(dve.tensor_copy(rank, ps[:, 7, 0:24].rearrange("p (t e) -> p t e", t=TILES)))
            dve.tensor_copy(token_ids[:, :, :], k_sb[:, C_TOKEN:C_TOKEN + TILES].unsqueeze(2)
                            .to_broadcast([P, TILES, 2]))
            dve.tensor_copy(cnt_f, ps[:, 7, 24:32]).then_inc(rk_ok, 1)
            ordered(dve.scalar_tensor_tensor(out=rankm, in0=rank, scalar=1.0, in1=mask, op0=ALU.add, op1=ALU.mult))
            ordered(dve.tensor_scalar(rankm, rankm, -1.0, None, ALU.add))
            for e in range(EXPERTS):
                if e >= 2:
                    dve.wait_ge(hot_used, e - 1)
                for t in range(TILES):
                    dve.tensor_scalar(slot_hot[:, e % 2, t, :], k_sb[:, C_IOTA:C_IOTA + 384], rankm[:, t, e:e + 1],
                                      None, ALU.is_equal).then_inc(hot_ok, 1)
                if e == 2:
                    rows_e = k_sb[:, C_ROW:C_ROW + 8].unsqueeze(1).to_broadcast([P, TILES, EXPERTS])
                    ordered(dve.tensor_tensor(rk_e, rank, rows_e, ALU.add))
                if e in (3, 4):
                    k, oh = e - 3, (oh1, oh2)[e - 3]
                    ordered(dve.tensor_tensor(pick, oh, rk_e, ALU.mult))
                    ordered(dve.tensor_reduce(pos_f[:, k, :], pick, AX_X, ALU.add))
                if e == 5:
                    dve.wait_ge(rk_ok, 1)
                    ordered(dve.tensor_reduce(small[:, 16:17], cnt_f, AX_X, ALU.max))
                    ordered(dve.tensor_scalar(small[:, 17:18], small[:, 16:17], 256.5, 8.0, ALU.is_gt, ALU.mult))
                    ordered(dve.tensor_scalar(small[:, 18:19], small[:, 17:18], 8.0, None, ALU.add))
                    ordered(dve.memset(over[:, :], 0))
                if e == 6:
                    ordered(dve.tensor_scalar(over[0:1, 0:8], cnt_f[0:1, :], -128.0, None, ALU.add))
                    ordered(dve.tensor_copy(over[0:1, 20:21], small[0:1, 18:19]))
                    ordered(dve.memset(idx_a[:, :], 0))
                    ordered(dve.memset(idx_b[:, :], 0))
            dve.wait_ge(hot_used, EXPERTS)
            ordered(dve.tensor_copy(idx_f, ps[:, 7, 64:112:2]))
            by_chunk = idx_f.rearrange("p (e c) -> p e c", c=TILES)
            ordered(dve.tensor_copy(idx_a[:, 0:8], by_chunk[:, :, 0]))
            ordered(dve.tensor_copy(idx_a[:, 8:16], by_chunk[:, :, 2]))
            ordered(dve.tensor_copy(idx_b[:, 0:8], by_chunk[:, :, 1]))
            dve.sem_inc(route_ok, 1)
            dve.tensor_copy(pos_i[:, :], pos_f.rearrange("p k t -> p (k t)")).then_inc(pos_ok, 1)
            dve.wait_ge(exp_v, 1)
            ordered(dve.tensor_scalar(w12[:, 0, :], dv, 1.0, None, ALU.add))
            ordered(dve.reciprocal(w12[:, 0, :], w12[:, 0, :]))
            dve.tensor_tensor(w12[:, 1, :], w12[:, 0, :], dv, ALU.mult).then_inc(weights_ok, 1)
            split_low(1, slot_of(F_MOE + 1), PIECES * (STEPS + 1), range(PIECES))

            rounds = dve.value_load(over[0:1, 20:21], min_val=EXPERTS, max_val=2 * EXPERTS)

            def turned_in(k, count):
                dve.wait_ge(xgt_a[k], count)
                for hf in range(2):
                    c_ = slice(4 * hf, 4 * hf + 4)
                    ins = dve.tensor_tensor(xg_lo[k][:, c_, :], ps[:, 6 + hf, :].rearrange("p (a b) -> p a b", a=4),
                                            xg_hi[k][:, c_, :].bitcast(F32), ALU.subtract)
                ins.then_inc(xgt_d[k], 1)

            turned_in(0, 1)
            for k in range(2):
                dve.sem_inc(y_d[k], 1)
            with dve.Fori(0, rounds) as i:
                more = dve.value_load(over[0:1, bass.ds(i, 1)])

                left = dve.snap(rounds - i, min_val=1, max_val=2 * EXPERTS)

                def split_ahead(j, of_round, pieces):
                    split_low(j, slot_of(F_MOE + j), of_round * (PIECES * STEPS) + PIECES * (STEPS + j), pieces)

                def moe_round(ks):
                    if 1 in ks:
                        turned_in(1, i + 1)
                    for j in range(STEPS):
                        for k in ks:
                            ahead = k == ks[-1] and j + 2 < STEPS
                            hidden(k, j, i * STEPS + (STEPS + j), moe_buf)
                            if ahead:
                                split_ahead(j + 2, i, range(0, PIECES // 2))
                            hidden_turned(k, j, i * STEPS + (STEPS + j), moe_buf)
                            if ahead:
                                split_ahead(j + 2, i, range(PIECES // 2, PIECES))
                        if j == STEPS - 1:
                            turned_in(0, i + 2)
                        if j + 2 >= STEPS:
                            with dve.If(left > 1):
                                split_ahead(j + 2 - STEPS, i + 1, range(PIECES))
                    for k in ks:
                        dve.wait_ge(y_st[k], i * 16 + 16)
                        dve.wait_ge(done[k], i + 1)
                        dve.tensor_copy(y_out[k][:, 0:512], ps[:, 2 + 2 * k, :]).then_inc(y_d[k], 1)

                with dve.If(more > 0):
                    moe_round((0, 1))
                with dve.Else():
                    moe_round((0,))
                    dve.sem_inc(xgt_d[1], 1)
                    dve.sem_inc(h_ok[1], STEPS)
                    dve.sem_inc(ht_ok[1], STEPS)
                    dve.sem_inc(y_d[1], 1)
                dve.nop()

            dve.wait_ge(gb_ok, 32 * 4)
            dve.wait_ge(weights_ok, 1)
            for t in range(TILES):
                a, b = got[0][:, t, :], got[1][:, t, :]
                dve.wait_ge(first_ok, t + 1)
                ordered(dve.scalar_tensor_tensor(out=a, in0=b, scalar=w12[:, 1, t:t + 1], in1=a,
                                                 op0=ALU.mult, op1=ALU.add))
                ordered(dve.tensor_tensor(a, a, gate_b[:, min(t, 1), :], ALU.mult))
                dve.tensor_tensor(x[:, t, :], x[:, t, :], a, ALU.add).then_inc(res_ok, 1)
            dve.wait_ge(res_ok, 4 * TILES)
            norm(4)
            dve.wait_ge(s_fin, 16)
            for t in range(TILES):
                dve.scalar_tensor_tensor(out=xn_tok[:, t, :], in0=x[:, t, :], scalar=stats[:, 4, t:t + 1], in1=fin_b,
                                         op0=ALU.mult, op1=ALU.mult).then_inc(y_fin, 1)

        @block.tensor
        def _(pe):
            def turn(dst, src):
                return pe.transpose(dst, src, ident[0:src.shape[0], 0:src.shape[0]])

            def norm(n):
                for t in range(TILES):
                    if t == 1:
                        pe.wait_ge(xn_act, n + 1)
                    else:
                        pe.wait_ge(xn_ok, 2 * n + 1 + t // 2)
                    for ci in range(KC):
                        ins = turn(ps[:, ci, t * P:(t + 1) * P], xn_tok[:, t, ci * P:(ci + 1) * P])
                        if t == TILES - 1:
                            ins.then_inc(nt_done, 1)

            def hn_ready(n):
                pe.wait_ge(hn_dve, 4 * (n + 1))
                pe.wait_ge(hn_act, 4 * (n + 1))

            def mod_groups(lo, hi):
                with pe.Fori(lo, hi) as g:
                    for s in range(4):
                        if s % 2 == 0:
                            pe.wait_ge(mod_copied, g * 2 + (s // 2 + 1))
                        pe.wait_ge(mod_full[s], g * 16 + 16)
                        wt = mod_slot(s).rearrange("p (k f) -> p k f", k=KC)
                        for k in range(KC):
                            ins = pe.matmul(ps[0:2, 6 + s // 2, (s % 2) * 256:(s % 2 + 1) * 256], cond[:, k, :],
                                            wt[:, k, :], start=(k == 0), stop=(k == KC - 1))
                        ins.then_inc(mod_used, 1)

            def turn_mod_rows(n_rows, count, bank):
                pe.wait_ge(mod_in, count)
                for g in range(2):
                    ins = turn(ps[:, bank, g * P:g * P + n_rows], vec_rows[0:n_rows, g, :])
                ins.then_inc(vec_t, 1)

            def full(n):
                pe.wait_ge(ring_full[slot_of(n)], filled(n))

            pe.wait_ge(s_const, 16)
            pe.wait_ge(s_vec, 16 * 12)
            turn(ps[:, 0, 0:N_COLS], vec_rows[0:N_COLS, 0, :]).then_inc(vec_t, 1)
            pe.wait_ge(cond_ok, 2)
            mod_groups(0, 3)
            turn_mod_rows(SHIFT_SCALE, 32, 0)
            mod_groups(3, 4)
            pe.wait_ge(mod_copied, 2 + 2 * 4)
            pe.wait_ge(mod_ok, 1)
            norm(0)
            hn_ready(0)
            pe.wait_ge(gap_ok, 3)

            fill_n = {"x": 0, "c": 1, "v": 2, "b": 3, "g": 4}
            for n, (kind, m, eng) in enumerate(items):
                if n >= PB:
                    pe.wait_ge(*ev_n[n - PB])
                if kind == "gate":
                    if n == first_item["gate"]:
                        pe.wait_ge(s_bd, 16 * 8)
                    pe.wait_ge(xc_ok, m % 4 + 1)
                    pe.matmul(ps[:, n % PB, 0:W], bd[:, m, :], xc[:, m % 4, :], start=True, stop=True).then_inc(pj, 1)
                    continue
                f = fill_n[kind]
                if m == 0:
                    full(F_IN + f)
                for k in range(KC):
                    ins = pe.matmul(ps[:, n % PB, 0:W], slab(F_IN + f)[:, k, m * P:(m + 1) * P], hn_t[:, k, :],
                                    start=(k == 0), stop=(k == KC - 1))
                ins.then_inc(pj, 1)
                if m == 3:
                    if MOD_SPLIT[kind]:
                        mod_groups(*MOD_SPLIT[kind])

            def product(n_sub, base_fill, lhs, bank):
                for f in range(2):
                    n = base_fill + f
                    full(n)
                    for t in range(TILES):
                        for k in range(KC):
                            ins = pe.matmul(ps[:, bank(t, f), :], lhs[:, k, TOK[t]:TOK[t] + P], slab(n)[:, k, :],
                                            start=(k == 0), stop=(k == KC - 1))
                        if f == 1:
                            ins.then_inc(out_ps, 1)
                    if f == 0:
                        ins.then_inc(ring_free[slot_of(n)], 1)
                        if n == F_OUT:
                            turn_mod_rows(96 - SHIFT_SCALE, 64, 6)

            pe.wait_ge(ev_a, ev_n[-1][1])
            pe.wait_ge(st_ok, 2)
            pe.wait_ge(mod_copied, 2 + 2 * (2 * MODS // GROUP))
            turn(ps[0:8, 7, 0:P], st8).then_inc(st_t, 1)
            pe.wait_ge(y_ok, 1)
            product(0, F_OUT, y_t, lambda t, f: 3 * f + t)

            def gate_up(j, hi, lo, k):
                w = WIDTH[j]
                for c_ in range(KC):
                    for n, (xt, part) in enumerate(((hi, 0), (hi, 1), (lo, 0))):
                        ins = pe.matmul(ps[:, 0, 0:2 * w], xt(c_), split[:, j % 2, part, c_, 0:2 * w],
                                        start=(c_ == 0 and n == 0), stop=(c_ == KC - 1 and n == 2))
                ins.then_inc(gu_ready[k], 1)

            def turn_hidden(k, j, count, buf):
                pe.wait_ge(h_ok[k], count + 1)
                for f in range(WIDTH[j] // P):
                    ins = turn(ps[:, 1, f * P:(f + 1) * P], buf[1][:, f * P:(f + 1) * P])
                ins.then_inc(h_turned[k], 1)

            def down(s, j, k, count, buf):
                pe.wait_ge(ht_ok[k], count + 1)
                last = WIDTH[j] // P - 1
                for f in range(last + 1):
                    for hf in range(2):
                        ins = pe.matmul(ps[:, 2 + 2 * k + hf, :], buf[2][:, f, :],
                                        down_raw(s, j)[:, f, hf * 512:(hf + 1) * 512],
                                        start=(j == 0 and f == 0), stop=(j == STEPS - 1 and f == last))
                return ins

            def down_split(s, j, k):
                last = WIDTH[j] // P - 1
                for f in range(last + 1):
                    for i, (part, wt) in enumerate(((0, down_high(j)), (0, down_low(s, j)), (1, down_high(j)))):
                        for hf in range(2):
                            ins = pe.matmul(ps[:, 2 + 2 * k + hf, :], h_split[:, part, f, :],
                                            wt[:, f, hf * 512:(hf + 1) * 512], start=(j == 0 and f == 0 and i == 0),
                                            stop=(j == STEPS - 1 and f == last and i == 2))
                return ins

            norm(1)
            hn_ready(1)
            todo = [(j, k) for j in range(STEPS) for k in range(TILES)]
            for u in range(len(todo) + 1):
                if u:
                    pj_, pk = todo[u - 1]
                    turn_hidden(pk, pj_, pj_, ffn_buf)
                if u < len(todo):
                    j, k = todo[u]
                    if k == 0:
                        pe.wait_ge(lo_ok, PIECES * (j + 1))
                    if j == 0:
                        pe.wait_ge(hx_lo, k + 1)
                    tok = slice(TOK[k], TOK[k] + P)
                    gate_up(j, lambda c_: hn_hi[:, c_, tok], lambda c_: hn_lo[:, c_, tok], k)
                if u:
                    pe.wait_ge(ht_ok[pk], pj_ + 1)
                    if pk == 0:
                        pe.wait_ge(down_lo, (START[pj_] + WIDTH[pj_]) // P)
                    ins = down_split(slot_of(F_FFN + pj_), pj_, pk)
                    if pj_ == STEPS - 1:
                        ins.then_inc(out_ps, 1)
                    elif pk == TILES - 1:
                        ins.then_inc(down_used, 1)

            norm(2)
            pe.wait_ge(hx_lo, 2 * TILES)
            for n in range(16):
                pe.wait_ge(qkv_lo, n + 1)
                if n >= 6:
                    pe.wait_ge((qk_dve, qk_ok)[n % 2], (n - 6) // 2 + 1)
                for k in range(KC):
                    for i, (part, tokens) in enumerate(((0, hn_hi), (0, hn_lo), (1, hn_hi))):
                        ins = pe.matmul(ps[:, n % 6, 0:W], qk_split(n, part)[:, k, :], tokens[:, k, :],
                                        start=(k == 0 and i == 0), stop=(k == KC - 1 and i == 2))
                ins.then_inc(qk_ps, 1)
            pe.wait_ge(qk_dve, 8)
            pe.wait_ge(qk_ok, 8)
            for n in range(4):
                pe.wait_ge(qkv_lo, 16 + n + 1)
                for t in range(TILES):
                    out = ps[:, 3 * (n // 2) + t, n % 2 * SF:(n % 2 + 1) * SF]
                    tok = slice(TOK[t], TOK[t] + P)
                    for k in range(KC):
                        for i, (tokens, part) in enumerate(((hn_hi, 0), (hn_hi, 1), (hn_lo, 0))):
                            ins = pe.matmul(out, tokens[:, k, tok], v_split(n, part)[:, k, :],
                                            start=(k == 0 and i == 0), stop=(k == KC - 1 and i == 2))
                    ins.then_inc(v_ps, 1)
            for k in range(KC):
                ins = turn(ps[:, 6 + k // 4, (k % 4) * P:(k % 4 + 1) * P], kk_t[:, k, 0:P])
            ins.then_inc(kt_ps, 1)
            pe.wait_ge(kt_ok, 1)
            pe.wait_ge(s_cache, 16)
            for k in range(KC):
                ins = turn(ps[:, 6 + k // 4, (k % 4) * P:(k % 4 + 1) * P], kc_tok[:, k * P:(k + 1) * P])
            ins.then_inc(ctx_t, 1)
            pe.wait_ge(ctx_d, 1)
            pe.wait_ge(ctx_ok, 1)
            pe.wait_ge(v_dve_ok, 3)
            pe.wait_ge(v_ok, 3)
            pe.wait_ge(s_vc, 16)

            n_units = len(units)
            for u in range(n_units + 3):
                if u < n_units:
                    t, h = units[u]
                    r, ci = 64 * (h % 2), h // 2
                    if u >= 2:
                        pe.wait_ge(s_ok, 2 * (u - 1))
                    q = q_t[r:r + 64, ci, TOK[t]:TOK[t] + P]
                    if t:
                        ins = pe.matmul(ps[:, u % 2, 0:384], q, kk_t[r:r + 64, ci, S0:W + P], start=True, stop=True)
                    else:
                        ins = pe.matmul(ps[:, u % 2, 0:P], q, kk_t[r:r + 64, ci, 0:P], start=True, stop=True)
                    ins.then_inc(sc_ps, 1)
                if 2 <= u <= n_units + 1:
                    w_ = u - 2
                    tp = units[w_][0]
                    pe.wait_ge(pn_ok, w_ + 1)
                    if w_ >= 2:
                        pe.wait_ge(pt_ok, w_ - 1)
                    for b in range(3 if tp else 1):
                        ins = turn(ps[:, 2 + w_ % 2, b * P:(b + 1) * P], p_buf[:, w_ % 3, b * P:(b + 1) * P])
                    ins.then_inc(pt_ps, 1)
                if u >= 3:
                    w_ = u - 3
                    tp, hp = units[w_]
                    ti = w_ // HEADS
                    if ti == 2 and hp == 0:
                        pe.wait_ge(o_ok, 1)
                    pe.wait_ge(pt_ok, w_ + 1)
                    vs = [v_tok[:, 1, :], v_tok[:, 2, :], vc] if tp else [v_tok[:, 0, :]]
                    b0, c0, r0 = 4 + 2 * (ti % 2) + hp // 8, hp // 2 % 4 * P, HD * (hp % 2)
                    for b, vv in enumerate(vs):
                        ins = pe.matmul(ps[r0:r0 + HD, b0, c0:c0 + P], vv[:, hp * HD:(hp + 1) * HD],
                                        pt_buf[:, w_ % 2, b * P:(b + 1) * P], start=(b == 0), stop=(b == len(vs) - 1))
                    ins.then_inc(pv, 1)
            pe.wait_ge(o_ok, 3)
            product(2, F_O, hn_t, lambda t, f: 3 * f + t)

            norm(3)
            hn_ready(3)
            pe.wait_ge(s_router, 16)
            for t in range(TILES):
                for k in range(KC):
                    ins = pe.matmul(ps[:, 6, t * 8:(t + 1) * 8], hn_t[:, k, TOK[t]:TOK[t] + P], router[:, k, :],
                                    start=(k == 0), stop=(k == KC - 1))
            ins.then_inc(lg_ps, 1)
            for n in range(6):
                t, hf = n // 2, n % 2
                for k in range(4):
                    ins = turn(ps[:, n, k * P:(k + 1) * P], hn_t[:, 4 * hf + k, TOK[t]:TOK[t] + P])
                ins.then_inc(hk_ps, 1)
            pe.wait_ge(mask_ok, 1)
            for t in range(TILES):
                for b in range(t + 1):
                    pe.matmul(ps[:, 7, t * 8:(t + 1) * 8], before if b == t else ones, mask[:, b, :],
                              start=(b == 0), stop=(b == t))
            for b in range(TILES):
                ins = pe.matmul(ps[:, 7, 24:32], ones, mask[:, b, :], start=(b == 0), stop=(b == TILES - 1))
            ins.then_inc(rk_ps, 1)
            pe.wait_ge(rk_ok, 1)
            for e in range(EXPERTS):
                pe.wait_ge(hot_ok, TILES * (e + 1))
                for ch in range(TILES):
                    for t in range(ch, TILES):
                        o = 64 + 2 * (TILES * e + ch)
                        ins = pe.matmul(ps[:, 7, o:o + 2], slot_hot[:, e % 2, t, ch * P:(ch + 1) * P],
                                        token_ids[:, t, :],
                                        start=(t == ch), stop=(t == TILES - 1))
                ins.then_inc(hot_used, 1)
            pe.wait_ge(hk_dve, 3)
            pe.wait_ge(hk_ok, 3)
            pe.wait_ge(route_ok, 1)

            def turn_gathered(k, count):
                pe.wait_ge(gathered[k], count)
                for c_ in range(KC):
                    ins = turn(ps[:, 6 + c_ // 4, (c_ % 4) * P:(c_ % 4 + 1) * P], xg[k][:, c_ * P:(c_ + 1) * P])
                ins.then_inc(xg_turned[k], 1)

            turn_gathered(0, 16)
            rounds = pe.value_load(over[0:1, 20:21], min_val=EXPERTS, max_val=2 * EXPERTS)
            with pe.Fori(0, rounds) as i:
                more = pe.value_load(over[0:1, bass.ds(i, 1)])

                def moe_round(ks):
                    pe.wait_ge(xgt_d[0], i + 1)
                    if 1 in ks:
                        turn_gathered(1, i * 16 + 16)
                    todo = [(j, k) for j in range(STEPS) for k in ks]
                    for u in range(len(todo) + 1):
                        if u:
                            pj_, pk = todo[u - 1]
                            turn_hidden(pk, pj_, i * STEPS + (STEPS + pj_), moe_buf)
                        if u < len(todo):
                            j, k = todo[u]
                            if k == 0:
                                pe.wait_ge(lo_ok, i * (PIECES * STEPS) + PIECES * (STEPS + j + 1))
                            elif j == 0:
                                pe.wait_ge(xgt_d[1], i + 1)
                            gate_up(j, lambda c_: xg_hi[k][:, c_, :], lambda c_: xg_lo[k][:, c_, :], k)
                        if u:
                            s = slot_of(F_FFN + pj_)
                            if pk == 0:
                                pe.wait_ge(down_full[s], i * (16 * TURNS) + 16 * (TURNS + pj_ // SLOTS + 1))
                            if pj_ == 0:
                                pe.wait_ge(y_d[pk], i + 1)
                                pe.wait_ge(y_a[pk], i + 1)
                            ins = down(s, pj_, pk, i * STEPS + (STEPS + pj_), moe_buf)
                            if pj_ == STEPS - 1:
                                ins.then_inc(done[pk], 1)
                            elif pk == ks[-1]:
                                ins.then_inc(down_used, 1)
                            if pj_ == 5 and pk == ks[-1]:
                                turn_gathered(0, i * 16 + 32)

                with pe.If(more > 0):
                    moe_round((0, 1))
                with pe.Else():
                    pe.sem_inc(xg_turned[1], 1)
                    moe_round((0,))
                    pe.sem_inc(gu_ready[1], STEPS)
                    pe.sem_inc(h_turned[1], STEPS)
                    pe.sem_inc(done[1], 1)
                pe.nop()


_INS = ['x_prompt', 'x_sample', 'state_lru', 'cache_k', 'cache_v', 'c', 'c_ctx', 'norm1_g', 'norm2_g', 'w_mod', 'b_mod',
        'w_in', 'lru_conv_w', 'lru_conv_b', 'lru_wa', 'lru_ba', 'lru_wx', 'lru_bx', 'lru_lam', 'sc_conv_w', 'sc_conv_b',
        'w_out', 'ffn_w_gate', 'ffn_w_up', 'ffn_w_down', 'w_qkv', 'w_o', 'rpb', 'w_router', 'moe_w_gate', 'moe_w_up',
        'moe_w_down', 'final_g']
_OUTS = [(1, 128, 1024), (1, 256, 1024), (1, 1, 2, 512), (1, 1, 16, 128, 64), (1, 1, 16, 128, 64)]


def kernel(**inputs):
    import concourse.bacc as _bacc
    from concourse.bass_utils import run_bass_kernel_spmd as _run

    nc = _bacc.Bacc("TRN2", target_bir_lowering=False, num_devices=1)
    arrays = {"shape_constants_dram": shape_constants()}
    args = [nc.dram_tensor("shape_constants_dram", (P, N_CONST), F32, kind="ExternalInput").ap()]
    for name in _INS:
        a = np.ascontiguousarray(inputs[name])
        arrays[f"in_{name}_dram"] = a
        args.append(nc.dram_tensor(f"in_{name}_dram", a.shape, mybir.dt.from_np(a.dtype), kind="ExternalInput").ap())
    for i, shape in enumerate(_OUTS):
        args.append(nc.dram_tensor(f"out_{i}_dram", shape, F32, kind="ExternalOutput").ap())
    hybrid_step(nc, *args)
    r = _run(nc, [arrays], core_ids=[0])
    return tuple(r.results[0][f"out_{i}_dram"] for i in range(len(_OUTS)))
```
